# Optimizing a Trainium2 kernel written in Bass

```python
import math
import numpy as np
import jax
import jax.numpy as jnp
from jax import lax

D_MODEL = 1024
BATCH = 1
SEQ = 256
DEPTH = 2

GRID_W = 64
CTX_LEN = 256
EPS = 1e-6
N_MOD = 6

GLA_HEADS = 4
GLA_DK = 64
GLA_DV = 128
GLA_GATE_RANK = 16
GLA_GATE_TEMP = 16.0
GLA_CHUNK = 64
GLA_QK = GLA_HEADS * GLA_DK
GLA_V = GLA_HEADS * GLA_DV

ATT_Q_HEADS = 8
ATT_KV_HEADS = 2
ATT_HD = 64
ATT_WINDOW = 128
ATT_BLOCK = 128
ROPE_BASE = 10000.0
ATT_Q = ATT_Q_HEADS * ATT_HD
ATT_KV = ATT_KV_HEADS * ATT_HD

SSD_HEADS = 16
SSD_HD = 64
SSD_GROUPS = 2
SSD_STATE = 128
SSD_CONV = 5
SSD_CHUNK = 128
SSD_INNER = SSD_HEADS * SSD_HD
SSD_BC = SSD_GROUPS * SSD_STATE
SSD_XBC = SSD_INNER + 2 * SSD_BC
SSD_HPG = SSD_HEADS // SSD_GROUPS

N_BRANCH = 3

N_EXPERTS = 16
N_EXPERT_GROUPS = 4
EXPERTS_PER_GROUP = N_EXPERTS // N_EXPERT_GROUPS
TOP_K = 2
EXPERT_FF = 1024
MOE_BLOCK = 128

IN_NAMES = ('gla_q', 'gla_k', 'gla_v', 'gla_r', 'gla_gf', 'gla_gb', 'att_q', 'att_k', 'att_v', 'ssd_z', 'ssd_xbc', 'ssd_dtf', 'ssd_dtb', 'merge')
IN_SPLITS = (GLA_QK, GLA_QK, GLA_V, GLA_V, GLA_GATE_RANK, GLA_GATE_RANK, ATT_Q, ATT_KV, ATT_KV, SSD_INNER, SSD_XBC, SSD_HEADS, SSD_HEADS, N_BRANCH * D_MODEL)
N_IN = sum(IN_SPLITS)

kernel_name = 'hybrid_gla_swa_ssd_moe_prefix_dit'

F32 = jnp.float32

def rms_norm(x, g):
    xf = x.astype(F32)
    y = xf * lax.rsqrt(jnp.mean(xf * xf, axis=-1, keepdims=True) + EPS)
    return (y * g.astype(F32)).astype(x.dtype)

def modulate(x, g, shift, scale):
    return (rms_norm(x, g) * (1.0 + scale) + shift).astype(x.dtype)

def split_proj(p):
    offsets = np.cumsum(IN_SPLITS)[:-1].tolist()
    return dict(zip(IN_NAMES, jnp.split(p, offsets, axis=-1)))

def axial_rope_tables(n):
    rows = n // GRID_W
    row = jnp.repeat(jnp.arange(rows), GRID_W).astype(F32)
    col = jnp.tile(jnp.arange(GRID_W), rows).astype(F32)
    axis_dim = ATT_HD // 2
    inv_freq = ROPE_BASE ** (-jnp.arange(0, axis_dim, 2, dtype=F32) / axis_dim)
    ang_r = row[:, None] * inv_freq
    ang_c = col[:, None] * inv_freq
    return (jnp.cos(ang_r), jnp.sin(ang_r), jnp.cos(ang_c), jnp.sin(ang_c))

def _rotate_half(x, cos, sin):
    x1, x2 = jnp.split(x, 2, axis=-1)
    return jnp.concatenate([x1 * cos - x2 * sin, x1 * sin + x2 * cos], axis=-1)

def apply_axial_rope(x, cos_r, sin_r, cos_c, sin_c):
    xr, xc = jnp.split(x.astype(F32), 2, axis=-1)
    yr = _rotate_half(xr, cos_r[:, None, :], sin_r[:, None, :])
    yc = _rotate_half(xc, cos_c[:, None, :], sin_c[:, None, :])
    return jnp.concatenate([yr, yc], axis=-1).astype(x.dtype)

def gla_chunk_scan(q, k, v, g, s0):
    bsz, n, nh, _ = q.shape
    dv = v.shape[-1]
    nc = n // GLA_CHUNK

    def chunks(a):
        return a.astype(F32).reshape(bsz, nc, GLA_CHUNK, nh, a.shape[-1]).transpose(1, 0, 3, 2, 4)

    causal = jnp.tril(jnp.ones((GLA_CHUNK, GLA_CHUNK), dtype=bool))[:, :, None]

    def step(state, inp):
        qc, kc, vc, gc = inp
        b = jnp.cumsum(gc, axis=2)
        inter = jnp.einsum('bhtd,bhde->bhte', qc * jnp.exp(b), state)
        diff = b[:, :, :, None, :] - b[:, :, None, :, :]
        decay = jnp.exp(jnp.where(causal, diff, -jnp.inf))
        scores = jnp.einsum('bhtd,bhsd,bhtsd->bhts', qc, kc, decay)
        intra = jnp.einsum('bhts,bhse->bhte', scores, vc)
        b_last = b[:, :, -1:, :]
        new_state = jnp.exp(b_last[:, :, 0, :])[..., None] * state + jnp.einsum('bhsd,bhse->bhde', kc * jnp.exp(b_last - b), vc)
        return new_state, inter + intra

    s_fin, out = lax.scan(step, s0, (chunks(q), chunks(k), chunks(v), chunks(g)))
    out = out.transpose(1, 0, 3, 2, 4).reshape(bsz, n, nh, dv)
    return out, s_fin

def gla_bidirectional(q, k, v, g_fwd, g_bwd, s0_fwd, s0_bwd):
    flip = lambda a: a[:, ::-1]
    o_f, s_f = gla_chunk_scan(q, k, v, g_fwd, s0_fwd)
    o_b, s_b = gla_chunk_scan(flip(q), flip(k), flip(v), flip(g_bwd), s0_bwd)
    return o_f + flip(o_b), s_f, s_b

def _gla_prep(p, lp):
    bsz, n = p['gla_q'].shape[:2]
    hs = (bsz, n, GLA_HEADS)
    q = p['gla_q'].reshape(*hs, GLA_DK) * (GLA_DK ** -0.5)
    k = p['gla_k'].reshape(*hs, GLA_DK)
    v = p['gla_v'].reshape(*hs, GLA_DV)

    def gate(lowrank, d):
        logits = (lowrank @ lp['gla_w2'][d] + lp['gla_b2'][d]).astype(F32)
        return (jax.nn.log_sigmoid(logits) / GLA_GATE_TEMP).reshape(*hs, GLA_DK)

    return q, k, v, gate(p['gla_gf'], 0), gate(p['gla_gb'], 1)

def _gla_out(o, r, lp):
    bsz, n = o.shape[:2]
    o = rms_norm(o, lp['gla_norm_g']).reshape(bsz, n, GLA_V)
    return (o * jax.nn.silu(r.astype(F32))).astype(r.dtype)

def gla_branch(pc, pl, lp, need_ctx):
    qc, kc, vc, gfc, gbc = _gla_prep(pc, lp)
    s0 = jnp.zeros((qc.shape[0], GLA_HEADS, GLA_DK, GLA_DV), F32)
    oc, s_f, s_b = gla_bidirectional(qc, kc, vc, gfc, gbc, s0, s0)
    ql, kl, vl, gfl, gbl = _gla_prep(pl, lp)
    ol, _, _ = gla_bidirectional(ql, kl, vl, gfl, gbl, s_f, s_b)
    y_ctx = _gla_out(oc, pc['gla_r'], lp) if need_ctx else None
    return y_ctx, _gla_out(ol, pl['gla_r'], lp)

def sink_attention(q, k, v, sink, mask):
    bsz, lq = q.shape[:2]
    rep = ATT_Q_HEADS // ATT_KV_HEADS
    qg = q.reshape(bsz, lq, ATT_KV_HEADS, rep, ATT_HD)
    s = jnp.einsum('blgrd,bmgd->bgrlm', qg, k, preferred_element_type=F32) * (ATT_HD ** -0.5)
    if mask is not None:
        s = jnp.where(mask, s, -jnp.inf)
    sk = sink.astype(F32).reshape(1, ATT_KV_HEADS, rep, 1, 1)
    m = jnp.maximum(jnp.max(s, axis=-1, keepdims=True), sk)
    p = jnp.exp(s - m)
    w = p / (jnp.sum(p, axis=-1, keepdims=True) + jnp.exp(sk - m))
    o = jnp.einsum('bgrlm,bmgd->blgrd', w.astype(v.dtype), v)
    return o.reshape(bsz, lq, ATT_Q)

def windowed_latent_attention(q, k, v, k_ctx, v_ctx, sink):
    bsz, n = q.shape[:2]
    nb = n // ATT_BLOCK
    span = ATT_BLOCK + 2 * ATT_WINDOW
    pad = ((0, 0), (ATT_WINDOW, ATT_WINDOW), (0, 0), (0, 0))
    kp = jnp.pad(k, pad)
    vp = jnp.pad(v, pad)
    qb = jnp.moveaxis(q.reshape(bsz, nb, ATT_BLOCK, ATT_Q_HEADS, ATT_HD), 1, 0)
    a = jnp.arange(ATT_BLOCK)[:, None]
    j = jnp.arange(span)[None, :]
    band = (j >= a) & (j <= a + 2 * ATT_WINDOW)
    ctx_mask = jnp.ones((ATT_BLOCK, k_ctx.shape[1]), dtype=bool)

    def one_block(args):
        qi, i = args
        start = i * ATT_BLOCK
        kw = lax.dynamic_slice_in_dim(kp, start, span, axis=1)
        vw = lax.dynamic_slice_in_dim(vp, start, span, axis=1)
        pos = start - ATT_WINDOW + jnp.arange(span)
        valid = (pos >= 0) & (pos < n)
        mask = jnp.concatenate([ctx_mask, band & valid[None, :]], axis=1)
        keys = jnp.concatenate([k_ctx, kw], axis=1)
        vals = jnp.concatenate([v_ctx, vw], axis=1)
        return sink_attention(qi, keys, vals, sink, mask)

    out = lax.map(one_block, (qb, jnp.arange(nb)))
    return jnp.moveaxis(out, 0, 1).reshape(bsz, n, ATT_Q)

def attn_branch(pc, pl, lp, rope, need_ctx):
    def prep(p):
        bsz, n = p['att_q'].shape[:2]
        q = rms_norm(p['att_q'].reshape(bsz, n, ATT_Q_HEADS, ATT_HD), lp['q_norm_g'])
        k = rms_norm(p['att_k'].reshape(bsz, n, ATT_KV_HEADS, ATT_HD), lp['k_norm_g'])
        v = p['att_v'].reshape(bsz, n, ATT_KV_HEADS, ATT_HD)
        return q, k, v

    qc, kc, vc = prep(pc)
    ql, kl, vl = prep(pl)
    ql = apply_axial_rope(ql, *rope)
    kl = apply_axial_rope(kl, *rope)
    y_lat = windowed_latent_attention(ql, kl, vl, kc, vc, lp['att_sink'])
    y_ctx = sink_attention(qc, kc, vc, lp['att_sink'], None) if need_ctx else None
    return y_ctx, y_lat

def dwconv_centred(x, w, b):
    pad = SSD_CONV // 2
    y = lax.conv_general_dilated(x, w[:, None, :].astype(x.dtype), window_strides=(1,), padding=[(pad, pad)], dimension_numbers=('NWC', 'WIO', 'NWC'), feature_group_count=x.shape[-1])
    return y + b.astype(x.dtype)

def ssd_chunk_scan(xs, dt, a, bm, cm, h0):
    bsz, n = xs.shape[:2]
    nc = n // SSD_CHUNK

    def chunks(t):
        return jnp.moveaxis(t.astype(F32).reshape(bsz, nc, SSD_CHUNK, *t.shape[2:]), 1, 0)

    causal = jnp.tril(jnp.ones((SSD_CHUNK, SSD_CHUNK), dtype=bool))[None, :, :, None]

    def step(h, inp):
        xc, dtc, ac, bc, cc = inp
        cum = jnp.cumsum(ac, axis=1)
        seg = cum[:, :, None, :] - cum[:, None, :, :]
        decay = jnp.exp(jnp.where(causal, seg, -jnp.inf))
        cb = jnp.repeat(jnp.einsum('btgn,bsgn->btsg', cc, bc), SSD_HPG, axis=-1)
        y_intra = jnp.einsum('btsh,bsh,bshp->bthp', cb * decay, dtc, xc)
        bc_h = jnp.repeat(bc, SSD_HPG, axis=2)
        cc_h = jnp.repeat(cc, SSD_HPG, axis=2)
        y_inter = jnp.einsum('bthn,bhpn->bthp', cc_h, h) * jnp.exp(cum)[..., None]
        w = jnp.exp(cum[:, -1:, :] - cum) * dtc
        h_new = jnp.exp(cum[:, -1, :])[:, :, None, None] * h + jnp.einsum('bsh,bshn,bshp->bhpn', w, bc_h, xc)
        return h_new, y_intra + y_inter

    h_fin, y = lax.scan(step, h0, (chunks(xs), chunks(dt), chunks(a), chunks(bm), chunks(cm)))
    return jnp.moveaxis(y, 0, 1).reshape(xs.shape), h_fin

def _ssd_core(p, lp, h0_f, h0_b):
    bsz, n = p['ssd_xbc'].shape[:2]
    xbc = jax.nn.silu(dwconv_centred(p['ssd_xbc'], lp['ssd_conv_w'], lp['ssd_conv_b']))
    xs, bm, cm = jnp.split(xbc, [SSD_INNER, SSD_INNER + SSD_BC], axis=-1)
    xs = xs.reshape(bsz, n, SSD_HEADS, SSD_HD)
    bm = bm.reshape(bsz, n, SSD_GROUPS, SSD_STATE)
    cm = cm.reshape(bsz, n, SSD_GROUPS, SSD_STATE)

    def dir_params(raw, d):
        dt = jax.nn.softplus(raw.astype(F32) + lp['ssd_dt_bias'][d].astype(F32))
        return dt, dt * -jnp.exp(lp['ssd_a_log'][d].astype(F32))

    dt_f, a_f = dir_params(p['ssd_dtf'], 0)
    dt_b, a_b = dir_params(p['ssd_dtb'], 1)
    flip = lambda t: t[:, ::-1]
    y_f, h_f = ssd_chunk_scan(xs, dt_f, a_f, bm, cm, h0_f)
    y_b, h_b = ssd_chunk_scan(flip(xs), flip(dt_b), flip(a_b), flip(bm), flip(cm), h0_b)
    y = y_f + flip(y_b) + lp['ssd_d'].astype(F32)[:, None] * xs.astype(F32)
    return y, h_f, h_b

def _ssd_out(y, z, lp):
    bsz, n = z.shape[:2]
    gsz = SSD_INNER // SSD_GROUPS
    yz = y.reshape(bsz, n, SSD_GROUPS, gsz) * jax.nn.silu(z.astype(F32)).reshape(bsz, n, SSD_GROUPS, gsz)
    return rms_norm(yz, lp['ssd_norm_g'].reshape(SSD_GROUPS, gsz)).reshape(bsz, n, SSD_INNER).astype(z.dtype)

def ssd_branch(pc, pl, lp, need_ctx):
    bsz = pc['ssd_xbc'].shape[0]
    h0 = jnp.zeros((bsz, SSD_HEADS, SSD_HD, SSD_STATE), F32)
    yc, h_f, h_b = _ssd_core(pc, lp, h0, h0)
    yl, _, _ = _ssd_core(pl, lp, h_f, h_b)
    y_ctx = _ssd_out(yc, pc['ssd_z'], lp) if need_ctx else None
    return y_ctx, _ssd_out(yl, pl['ssd_z'], lp)

def merge_branches(p, y_gla, y_att, y_ssd, lp):
    bsz, n = y_gla.shape[:2]
    gates = jax.nn.sigmoid((p['merge'] + lp['gate_b'].reshape(-1)).astype(F32)).reshape(bsz, n, N_BRANCH, D_MODEL)
    merged = (gates[:, :, 0] * (y_gla @ lp['w_br_a'])
              + gates[:, :, 1] * (y_att @ lp['w_br_b'])
              + gates[:, :, 2] * (y_ssd @ lp['w_br_c']))
    return merged.astype(y_gla.dtype) @ lp['w_out']

def moe_ffn(h, router_w, router_b, w1, w3, w2):
    bsz, n, d = h.shape
    tok_x = h.reshape(-1, d)
    n_tok = tok_x.shape[0]
    scores = jax.nn.sigmoid(jnp.dot(tok_x, router_w, preferred_element_type=F32))
    biased = (scores + router_b.astype(F32)).reshape(n_tok, N_EXPERT_GROUPS, EXPERTS_PER_GROUP)
    group_score = jnp.sum(lax.top_k(biased, TOP_K)[0], axis=-1)
    group = jnp.argmax(group_score, axis=-1)
    in_group = jnp.take_along_axis(biased, group[:, None, None], axis=1)[:, 0]
    local = lax.top_k(in_group, TOP_K)[1]
    expert = group[:, None] * EXPERTS_PER_GROUP + local
    gate = jnp.take_along_axis(scores, expert, axis=1)
    gate = gate / jnp.sum(gate, axis=-1, keepdims=True)
    flat_e = expert.reshape(-1)
    n_assign = flat_e.shape[0]
    order = jnp.argsort(flat_e)
    sorted_e = flat_e[order]
    src_tok = order // TOP_K
    counts = jnp.bincount(flat_e, length=N_EXPERTS)
    padded = (counts + MOE_BLOCK - 1) // MOE_BLOCK * MOE_BLOCK
    pad_end = jnp.cumsum(padded)
    pad_start = pad_end - padded
    start = jnp.cumsum(counts) - counts
    dest = pad_start[sorted_e] + jnp.arange(n_assign) - start[sorted_e]
    n_blocks = -(-n_assign // MOE_BLOCK) + N_EXPERTS
    buf = jnp.zeros((n_blocks * MOE_BLOCK, d), h.dtype).at[dest].set(tok_x[src_tok])
    block_e = jnp.minimum(jnp.searchsorted(pad_end, jnp.arange(n_blocks) * MOE_BLOCK, side='right'), N_EXPERTS - 1)

    def expert_block(args):
        xb, e = args
        hid = jax.nn.silu(xb @ w1[e]) * (xb @ w3[e])
        return hid @ w2[e]

    out = lax.map(expert_block, (buf.reshape(n_blocks, MOE_BLOCK, d), block_e)).reshape(-1, d)
    y = out[dest].astype(F32) * gate.reshape(-1)[order][:, None]
    return jax.ops.segment_sum(y, src_tok, num_segments=n_tok).astype(h.dtype).reshape(bsz, n, d)

def trunk_layer(x, ctx, c, c_ctx, lp, router_w, router_b, rope, need_ctx):
    mod_lat = jnp.split((jax.nn.silu(c) @ lp['w_mod'] + lp['b_mod'])[:, None, :], N_MOD, axis=-1)
    mod_ctx = jnp.split((jax.nn.silu(c_ctx) @ lp['w_mod'] + lp['b_mod'])[None, None, :], N_MOD, axis=-1)
    shift1, scale1, gate1, shift2, scale2, gate2 = mod_lat
    cshift1, cscale1, cgate1, cshift2, cscale2, cgate2 = mod_ctx

    h_lat = modulate(x, lp['norm1_g'], shift1, scale1)
    h_ctx = modulate(ctx, lp['norm1_g'], cshift1, cscale1)
    p_lat = split_proj(h_lat @ lp['w_in'])
    p_ctx = split_proj(h_ctx @ lp['w_in'])

    gla_ctx, gla_lat = gla_branch(p_ctx, p_lat, lp, need_ctx)
    att_ctx, att_lat = attn_branch(p_ctx, p_lat, lp, rope, need_ctx)
    ssd_ctx, ssd_lat = ssd_branch(p_ctx, p_lat, lp, need_ctx)

    x = x + (gate1 * merge_branches(p_lat, gla_lat, att_lat, ssd_lat, lp)).astype(x.dtype)
    if not need_ctx:
        ffn = moe_ffn(modulate(x, lp['norm2_g'], shift2, scale2), router_w, router_b, lp['w1'], lp['w3'], lp['w2'])
        return x + (gate2 * ffn).astype(x.dtype), ctx

    ctx = ctx + (cgate1 * merge_branches(p_ctx, gla_ctx, att_ctx, ssd_ctx, lp)).astype(ctx.dtype)
    h2 = jnp.concatenate([modulate(ctx, lp['norm2_g'], cshift2, cscale2), modulate(x, lp['norm2_g'], shift2, scale2)], axis=1)
    ffn = moe_ffn(h2, router_w, router_b, lp['w1'], lp['w3'], lp['w2'])
    n_ctx = ctx.shape[1]
    ctx = ctx + (cgate2 * ffn[:, :n_ctx]).astype(ctx.dtype)
    x = x + (gate2 * ffn[:, n_ctx:]).astype(x.dtype)
    return x, ctx

def setup_inputs(seed: int = 0) -> dict:
    key = jax.random.key(seed)
    ks = jax.random.split(key, 31)
    D = D_MODEL
    L = DEPTH

    def nrm(k, shape, s):
        return jax.random.normal(k, shape, jnp.float32) * s

    dt = jnp.exp(jax.random.uniform(ks[16], (L, 2, SSD_HEADS), minval=math.log(1e-3), maxval=math.log(1e-1)))
    return {
        'x': nrm(ks[0], (BATCH, SEQ, D), 1.0),
        'c': nrm(ks[1], (BATCH, D), 1.0),
        'ctx': nrm(ks[2], (BATCH, CTX_LEN, D), 1.0),
        'c_ctx': nrm(ks[3], (D,), 1.0),
        'w_mod': nrm(ks[4], (L, D, N_MOD * D), 0.02),
        'b_mod': nrm(ks[5], (L, N_MOD * D), 0.02),
        'norm1_g': 1.0 + nrm(ks[6], (L, D), 0.05),
        'w_in': nrm(ks[7], (L, D, N_IN), D ** -0.5),
        'gla_w2': nrm(ks[8], (L, 2, GLA_GATE_RANK, GLA_QK), GLA_GATE_RANK ** -0.5),
        'gla_b2': nrm(ks[9], (L, 2, GLA_QK), 0.1),
        'gla_norm_g': 1.0 + nrm(ks[10], (L, GLA_DV), 0.05),
        'q_norm_g': 1.0 + nrm(ks[11], (L, ATT_HD), 0.05),
        'k_norm_g': 1.0 + nrm(ks[12], (L, ATT_HD), 0.05),
        'att_sink': nrm(ks[13], (L, ATT_Q_HEADS), 0.5),
        'ssd_conv_w': nrm(ks[14], (L, SSD_CONV, SSD_XBC), SSD_CONV ** -0.5),
        'ssd_conv_b': nrm(ks[15], (L, SSD_XBC), 0.02),
        'ssd_dt_bias': dt + jnp.log(-jnp.expm1(-dt)),
        'ssd_a_log': jnp.log(jax.random.uniform(ks[17], (L, 2, SSD_HEADS), minval=1.0, maxval=16.0)),
        'ssd_d': 1.0 + nrm(ks[18], (L, SSD_HEADS), 0.05),
        'ssd_norm_g': 1.0 + nrm(ks[19], (L, SSD_INNER), 0.05),
        'gate_b': nrm(ks[20], (L, N_BRANCH, D), 0.1),
        'w_br_a': nrm(ks[21], (L, GLA_V, D), GLA_V ** -0.5),
        'w_br_b': nrm(ks[22], (L, ATT_Q, D), ATT_Q ** -0.5),
        'w_br_c': nrm(ks[23], (L, SSD_INNER, D), SSD_INNER ** -0.5),
        'w_out': nrm(ks[24], (L, D, D), D ** -0.5),
        'norm2_g': 1.0 + nrm(ks[25], (L, D), 0.05),
        'router_w': nrm(ks[26], (D, N_EXPERTS), D ** -0.5),
        'router_b': nrm(ks[27], (N_EXPERTS,), 0.01),
        'w1': nrm(ks[28], (L, N_EXPERTS, D, EXPERT_FF), D ** -0.5),
        'w3': nrm(ks[29], (L, N_EXPERTS, D, EXPERT_FF), D ** -0.5),
        'w2': nrm(ks[30], (L, N_EXPERTS, EXPERT_FF, D), EXPERT_FF ** -0.5),
    }

def reference(x, c, ctx, c_ctx, w_mod, b_mod, norm1_g, w_in, gla_w2, gla_b2, gla_norm_g, q_norm_g, k_norm_g, att_sink, ssd_conv_w, ssd_conv_b, ssd_dt_bias, ssd_a_log, ssd_d, ssd_norm_g, gate_b, w_br_a, w_br_b, w_br_c, w_out, norm2_g, router_w, router_b, w1, w3, w2):
    rope = axial_rope_tables(x.shape[1])
    for l in range(DEPTH):
        lp = {
            'w_mod': w_mod[l], 'b_mod': b_mod[l], 'norm1_g': norm1_g[l], 'w_in': w_in[l],
            'gla_w2': gla_w2[l], 'gla_b2': gla_b2[l], 'gla_norm_g': gla_norm_g[l],
            'q_norm_g': q_norm_g[l], 'k_norm_g': k_norm_g[l], 'att_sink': att_sink[l],
            'ssd_conv_w': ssd_conv_w[l], 'ssd_conv_b': ssd_conv_b[l], 'ssd_dt_bias': ssd_dt_bias[l],
            'ssd_a_log': ssd_a_log[l], 'ssd_d': ssd_d[l], 'ssd_norm_g': ssd_norm_g[l],
            'gate_b': gate_b[l], 'w_br_a': w_br_a[l], 'w_br_b': w_br_b[l], 'w_br_c': w_br_c[l],
            'w_out': w_out[l], 'norm2_g': norm2_g[l], 'w1': w1[l], 'w3': w3[l], 'w2': w2[l],
        }
        x, ctx = trunk_layer(x, ctx, c, c_ctx, lp, router_w, router_b, rope, l < DEPTH - 1)
    return x


_drawn_inputs = setup_inputs


def setup_inputs(seed=0):
    import zlib

    import numpy as np

    out = dict(_drawn_inputs(seed))
    spreads = {}
    factors = {'q_norm_g': 8.0, 'k_norm_g': 7.664, 'att_sink': 8.0, 'ssd_d': 2.812}
    for name, (base, spread) in spreads.items():
        noise = np.random.default_rng([zlib.crc32(name.encode()), seed]).standard_normal(out[name].shape)
        drawn = base * np.exp(spread * noise) if base else spread * noise
        out[name] = jnp.asarray(drawn.astype(out[name].dtype))
    for name, factor in factors.items():
        out[name] = (out[name] * factor).astype(out[name].dtype)
    return out
```

```python
import numpy as np
import concourse.bass as bass
from concourse import mybir
from contextlib import ExitStack

F32 = mybir.dt.float32
I32 = mybir.dt.int32
U32 = mybir.dt.uint32
ALU = mybir.AluOpType
ACT = mybir.ActivationFunctionType
AX = mybir.AxisListType

P = 128
D = 1024
KO = D // P
CTX, LAT = 256, 256
TOK = CTX + LAT
TT = TOK // P
NL = 2
NMOD = 6
EPS = 1e-6
NE, NG, EPG = 16, 4, 4
FF = 1024
CLAMP = 40.0
BIG = 1e30
XTRA = 7
SLOTS = (NE + XTRA) * P

C_GQ, C_GK, C_GV, C_GR, C_GF, C_GB = 0, 256, 512, 1024, 1536, 1552
C_AQ, C_AK, C_Z, C_XBC, C_DT, C_MG = 1568, 2080, 2336, 3360, 4896, 4928
N_IN = 8000
QH, HD = 8, 64
SH, SP = 16, 64

CONST = {}


def const_pack():
    s, t = np.arange(P)[:, None], np.arange(P)[None, :]
    parts = {
        "ident": s == t, "upper": s <= t, "lower": s >= t, "strict": s < t, "ones": np.ones((P, P)),
    }
    window = np.zeros((P, 2, 256), np.float32)
    for b in range(2):
        far = np.abs(np.arange(256)[None, :] - (b * P + np.arange(P)[:, None])) > 128
        window[:, b] = np.where(far, -BIG, 0.0)
    parts["window"] = window.reshape(P, -1)
    pos = np.arange(LAT)
    inv = (10000.0 ** (-np.arange(0, 32, 2, dtype=np.float32) / 32)).astype(np.float32)
    row = (pos // 64).astype(np.float32)[:, None] * inv
    col = (pos % 64).astype(np.float32)[:, None] * inv
    cos = np.concatenate([np.cos(row), np.cos(row), np.cos(col), np.cos(col)], 1)
    sin = np.concatenate([-np.sin(row), np.sin(row), -np.sin(col), np.sin(col)], 1)
    parts["cos"] = cos.reshape(2, P, 64).transpose(1, 0, 2).reshape(P, -1)
    parts["sin"] = sin.reshape(2, P, 64).transpose(1, 0, 2).reshape(P, -1)
    parts["token"] = np.arange(P)[:, None] + P * np.arange(TT)[None, :]
    parts["first_slot"] = np.tile(np.arange(NE) * P, (P, 1))
    parts["block"] = np.tile(np.arange(8), (P, 1))
    parts["rank4"] = np.tile(4 - np.arange(4), (P, 1))
    at = 0
    cols = []
    for k, v in parts.items():
        v = np.asarray(v, np.float32)
        CONST[k] = (at, v.shape[1])
        at += v.shape[1]
        cols.append(v)
    return np.concatenate(cols, 1)


NCONST = const_pack().shape[1]

ROWS = {}
_at = 0
for _k, _n in (("q_norm", 64), ("k_norm", 64), ("gla_norm", 128), ("ssd_norm", 1024), ("dt_bias", 32),
               ("a_log", 32), ("ssd_d", 16), ("sink", 8), ("gla_b2", 512), ("router_b", 16)):
    ROWS[_k] = (_at, _n)
    _at += _n
NROWS = _at
COLS = {"norm1": (0, 8), "norm2": (8, 8), "conv_w": (16, 60), "conv_b": (76, 12), "gate_b": (88, 24)}
NCOLS = 112
RING = 4
SLOT_W = 512
NSTREAM = 2


def plan_layer(l):
    act, dve = "act", "dve"
    tiles = list(range(TT)) if l < NL - 1 else [2, 3]
    out = [(("mod", c), [("mod", c, dve)]) for c in range(12)]
    for b in range(3):
        groups = [("xbc", b * 4 + i, act) for i in range(4)]
        out.append((("xbc", b), groups))
    out.append((("dt", 0), [("dt", t, dve) for t in range(TT)]))
    out.append((("qk", 0), [("qk", i, act) for i in range(4)]))
    out.append((("gates", 0), [("gates", i, act) for i in range(2)]))
    out.append((("v", 0), [("v", t, act) for t in range(TT)]))
    out.append((("attq", 0), [("attq", t, act) for t in tiles]))
    out.append((("attkv", 0), [("attkv", t, act) for t in range(TT)]))
    for b in range(2):
        out.append((("z", b), [("z", (b, t), act) for t in tiles]))
    out.append((("r", 0), [("r", t, act) for t in tiles]))
    for j in range(3):
        for half in range(2):
            pairs = []
            for i in range(4):
                pairs += [("gate", (j, half * 4 + i), act), ("prod", (j, half * 4 + i), dve)]
            out.append((("pair", j, half), pairs))
    for half in range(2):
        out.append((("out", half), [("out", (half, t), dve) for t in tiles]))
    return tiles, out


def plan():
    loads, groups, find = [], [], {}
    ordinal = {"act": 0, "dve": 0}
    for l in range(NL):
        for block, served in plan_layer(l)[1]:
            kinds = [block]
            if block[0] == "pair":
                _, j, half = block
                kinds = [("mg", j, half), ("wbr", j, half)]
            first = len(loads)
            for k in kinds:
                loads.append({"layer": l, "block": k, "slot": len(loads) % RING})
            for kind, index, engine in served:
                n = len(groups)
                ordinal[engine] += 1
                need = first + (1 if kind == "prod" else 0)
                groups.append({"layer": l, "kind": kind, "index": index, "engine": engine,
                               "ordinal": ordinal[engine], "bank": n % NSTREAM, "load": need, "number": n})
                find[(l, kind, index)] = n
                loads[need]["last"] = n
    return loads, groups, find




EXPERT_SEMS = ("up_full", "down_full", "gathered", "xt_full", "xt_ready", "stored", "hid_ready",
               "ht_full", "ht_ready", "ob_done", "silu_ready")
STEPS = {
    "pool_step": "branches_final",
    "pe_step": "modT_full cum_full lg_full logit_full rank_full",
    "act_step": "sp2 ecs_ready gsp bme_ready gsq ar_ready branch_rs sink_exp logit_exp all_stored",
    "dve_step": "neg_ready sp1 da_ready cum_ready wd_pre w_ready gabs g_ready btm_ready sp_ready "
                "ass_ready gss_ready sink_pre merged x_new assigned route_ready layer_done",
}
NORMS = {"ss": TT, "rs": 1, "xn": TT, "tr": TT, "hT": TT}
SHARED = {n: (sem, i) for sem, names in STEPS.items() for i, n in enumerate(names.split())}
SHARED.update({f"{n}{which}": (n, first * (which - 1)) for n, first in NORMS.items() for which in (1, 2)})
FIRST_LAYER = {"x_in": 0, "zeroed": 0, "y_zero": 0, "eps_set": 0, "tok_id": 0, "xd_saved": 0, "out_saved": 0,
               "small_in": 16 * 5, "mod_saved": 16, "tok_zero": 16, "x_saved": 16, "row_saved": 16, "tok_got": 16,
               "x_again": 16 * (TT + 2), "tok_put": 16 * 2 * TT, "y_got": 16 * (2 * TT + 3),
               "merge_acc": 2 * KO, "conv_acc": 12, "conv_done": 12, "ct_full": 10, "ct_done": 10,
               "pool_x": 3 * TT, "wx_ready": 6, "upd_full": 6, "s_ready": 6, "inter_full": 6, "inter_done": 6, "yt_full": 4 * TT}
FIRST_LAYER.update({sem: len(names.split()) for sem, names in STEPS.items()})
FIRST_LAYER.update({n: 2 * first for n, first in NORMS.items()})
for _names, _n in (
        ("cb_full cbm_ready y_evac b_full b_done kdt_full "
         "kdt_ready kv_full kv_done eb_ready qkd_ready sc_full gy_full gy_done qk_full qk_turned att_prep o_raw o_done", TT),
        ("p_ready yz_ready yt_act yt_dve rows_full row_ready", 2 * TT),
        ("bc_full diff_done dm_ready e_ready m_ready ymm_done s_full nmax_ready p_exp pt_full pt_ready o_full", 8 * TT)):
    FIRST_LAYER.update(dict.fromkeys(_names.split(), _n))


def build(nc, I, out):
    loads, groups, find = plan()
    with ExitStack() as ctx:
        def sb(name, shape, dt=F32):
            return ctx.enter_context(nc.sbuf_tensor(name, shape, dt))

        def sem(name):
            return ctx.enter_context(nc.semaphore(name))

        def sems(name):
            return [sem(f"{name}_{l}") for l in range(NL)]

        consts = sb("consts", [P, NCONST])
        rows = sb("rows", [P, NROWS])
        cols = sb("cols", [P, NCOLS])
        router_w = sb("router_w", [P, KO, NE])
        gate_w2 = sb("gate_w2", [16, 512])
        eps_t = sb("eps_t", [P, 1])
        cond = sb("cond", [P, KO, 2])
        cond_e = sb("cond_e", [P, KO, 2])
        modc = sb("modc", [P, 4, KO, 2])
        scale_a = sb("scale_a", [P, 2, KO, 2])
        neg_sink = sb("neg_sink", [P, 8])
        neg_a = sb("neg_a", [P, 32])
        sumsq = sb("sumsq", [P, 16])
        rstd = sb("rstd", [P, 16])
        hT = sb("hT", [P, KO, TOK])
        xb = sb("xb", [P, TT, D])
        ring = sb("ring", [P, RING, KO, SLOT_W])
        small = sb("small", [P, 1408])
        slot_idx = sb("slot_idx", [P, 2 * TT], U32)
        tok_idx = sb("tok_idx", [P, NE + XTRA + 1], U32)
        tok_id = sb("tok_id", [P, TT], U32)
        zero_idx = sb("zero_idx", [P, NE + XTRA + 1], U32)
        extra = sb("extra", [P, 16], I32)
        arena = sb("arena", [P, 22528])
        ps = ctx.enter_context(nc.psum_tensor("ps", [P, 8, 512], F32))

        x_dram = nc.dram_tensor("x_scratch", (TOK, D), F32).ap()
        mod_dram = nc.dram_tensor("mod_scratch", (NL, 2, NMOD * D), F32).ap()
        h_dram = nc.dram_tensor("h_scratch", (TOK, D), F32).ap()
        tok_dram = nc.dram_tensor("tok_scratch", ((NE + XTRA + 1) * P, 1), U32).ap()
        y_dram = nc.dram_tensor("y_scratch", (SLOTS, D), F32).ap()

        def K(name):
            at, n = CONST[name]
            return consts[:, at:at + n]

        def Rw(name):
            at, n = ROWS[name]
            return rows[:, at:at + n]

        def Cl(name):
            at, n = COLS[name]
            return cols[:, at:at + n]

        def region(at, *shape):
            n = int(np.prod(shape))
            v = arena[:, at:at + n]
            names = "abcd"[:len(shape)]
            if len(shape) == 1:
                return v
            spec = "p (" + " ".join(names) + ") -> p " + " ".join(names)
            return v.rearrange(spec, **dict(zip(names, shape)))

        def view(ap, *shape):
            names = "abcd"[:len(shape)]
            spec = "p (" + " ".join(names) + ") -> p " + " ".join(names)
            return ap.rearrange(spec, **dict(zip(names, shape)))

        ident, upper, lower, ones = K("ident"), K("upper"), K("lower"), K("ones")
        tri = [upper, lower]
        qkT = region(0, 4, TOK)
        gv = region(2048, TT, 512)
        gT = region(4096, 2, TOK)
        att = region(5120, TT, 768)
        ys = region(8192, TT, 1024)
        yg = region(12288, TT, 512)
        modr = region(8192, NMOD * D)
        bcT = region(14336, 4, TOK)
        b_tm = region(16384, TT, 256)
        TMP = 17408
        xn = region(TMP, TT, D)
        junk = region(TMP + 4096, D)
        raw = region(TMP, 3, TOK)
        xsT = region(TMP + 1536, 2, TOK)
        xs = xb
        xw = [[region(TMP + i * 2048 + d * 1024, 1024) for d in range(2)] for i in range(2)]
        state = region(TMP + 2048, 2, 1024)
        cbm = region(TMP + 4096, 2, 2, P)
        dd = [region(12288, 512), region(12800, 512), region(TMP + 4608, 512)]
        mm = [region(13312 + i * 512, 512) for i in range(2)]
        o = [0]

        def sm(*shape):
            n = int(np.prod(shape))
            v = small[:, o[0]:o[0] + n]
            o[0] += n
            return v if len(shape) == 1 else view(v, *shape)

        dt_raw = sm(TT, 32)
        dt = sm(TT, 32)
        da = sm(TT, 32)
        cums = sm(TT, 64)
        ecs = sm(TT, 64)
        wd = sm(TT, 32)
        zs = [region(4096 + i * 512, 512) for i in range(2)]
        gg = view(xb[:, 0:2, :].rearrange("p a b -> p (a b)"), TT, 512)
        kv = view(xb[:, 2:4, :].rearrange("p a b -> p (a b)"), TT, 2, 2, P)
        qd = region(14336, TT * 2, 2, P)
        kd = region(16384, TT * 2, 2, P)
        sp = region(18432, TT * 2, 2, P)
        eb = region(20480, 2, 2, 2, P)
        pm = [region(21504, 4, P), region(22016, 4, P)]
        kdT = region(21504, 4, P)
        gs = region(20480, 4, P)
        bmt = sm(TT, 2, 2, 2)
        bme = sm(TT, 2, 2, 2)
        btm = sm(TT, 2, 2)
        gss = sm(TT, 4)
        qT = region(14336, 4, TOK)
        kT2 = region(16384, 2, TOK)
        pb = [region(17408 + i * 512, 512) for i in range(2)]
        pT = [region(18432 + i * 512, 4, P) for i in range(2)]
        rt, ru = region(19456, 640), region(20096, 640)
        kdup = region(20736, TT, 2, 2, 64)
        ass = sm(TT, 10)
        nmax = sm(TT * 8)
        rsum = sm(TT * 8)
        yT = region(14336, 16, TOK)
        merged = region(0, KO, TOK)
        gate_e = [region(4096 + i * 512, 512) for i in range(2)]
        gate_bc = region(8192, 2, D)
        o[0] = 0
        sc = sm(TT, NE)
        bi = sm(TT, NE)
        oh = [sm(TT, NE), sm(TT, NE)]
        t16 = sm(TT, NE)
        m1, m2, gsc, gsel = sm(TT, 4), sm(TT, 4), sm(TT, 4), sm(TT, 4)
        gmax = sm(TT)
        gates = sm(2, TT)
        rank = sm(TT, NE)
        over = sm(TT, NE)
        slotf = sm(2, TT)
        cnt, xtr, incl, scan_t = sm(NE), sm(NE), sm(NE), sm(NE)
        off = sm(NE)
        blk = sm(8, NE)
        blkf = sm(8)
        ex_slot = [region(i * 4096, KO, 512) for i in range(5)] + [view(xb[:].rearrange("p a b -> p (a b)"), KO, 512)]
        hflat = hT[:].rearrange("p a b -> p (a b)")
        h_rows = region(TMP, TT, D)
        xg = hflat[:, 0:1024]
        xT = view(hflat[:, 1024:2048], KO, P)
        hid = hflat[:, 2048:3072]
        hidT = view(hflat[:, 3072:4096], KO, P)
        ob = region(20480, 1024)
        silu_h = [region(21504 + i * 512, 512) for i in range(2)]
        yr = region(0, TT, 2, D)


        landed = [sem(f"landed{i}") for i in range(RING)]
        stream_full = sem("stream_full")
        free = {"act": sem("free_act"), "dve": sem("free_dve")}
        const_in = sem("const_in")
        cond_exp, cond_ready = sem("cond_exp"), sem("cond_ready")
        chain = {"dve": sem("chain_dve"), "act": sem("chain_act"), "pool": sem("chain_pool")}
        made = {}

        def own(name):
            return name in EXPERT_SEMS or name.startswith("expert_in")

        def s(name, l):
            name, _ = SHARED.get(name, (name, 0))
            key = f"{name}_{l}" if own(name) else name
            if key not in made:
                made[key] = sem(key)
            return made[key]

        def first(i):
            return isinstance(i, int) and i == 0

        def count(name, l, value):
            sem_name, before = SHARED.get(name, (name, 0))
            earlier = 0 if own(name) or l == 0 else FIRST_LAYER[sem_name]
            return value + before + earlier

        class Chain:

            def __init__(self, eng, name):
                self.eng, self.sem, self.n = eng, chain[name], 0

            def __call__(self, ins):
                self.n += 1
                ins.then_inc(self.sem, 1)
                self.eng.wait_ge(self.sem, self.n)

        alink = None

        def tiles_of(l):
            return plan_layer(l)[0]

        def span_of(l):
            return (0, TOK) if l < NL - 1 else (CTX, TOK)

        def filled(l, kind, index):
            return groups[find[l, kind, index]]["number"] + 1

        def bank_of(l, kind, index):
            return groups[find[l, kind, index]]["bank"]

        def freer(l, kind, index):
            return free[groups[find[l, kind, index]]["engine"]]

        def freed(l, kind, index):
            return groups[find[l, kind, index]]["ordinal"]

        def z_groups(l, step):
            tiles = tiles_of(l)
            every = [(b * len(tiles) + i, (b, t)) for b in range(2) for i, t in enumerate(tiles)]
            return every[step * len(every) // TT:(step + 1) * len(every) // TT]

        def n_inters(l):
            return sum(b in tiles_of(l) for d in range(2) for b in ORDER[d][1:])

        SPREAD = (3, 4, 7)

        def fills(l, step):
            groups_ = [("v", t) for t in range(TT)] + [("attq", t) for t in tiles_of(l)] + [("attkv", t) for t in range(TT)]
            n = 8 * len(tiles_of(l))
            return groups_[step * len(groups_) // n:(step + 1) * len(groups_) // n]

        ORDER = [[0, 1, 2, 3], [1, 0, 3, 2]]

        def block_source(l, block):
            kind = block[0]
            w_in = I["w_in"][l].rearrange("(k p) n -> p k n", p=P)

            def cols_of(w, a, n):
                return w[:, :, a:a + n], n
            if kind == "mod":
                return cols_of(I["w_mod"][l].rearrange("(k p) n -> p k n", p=P), block[1] * 512, 512)
            if kind == "out":
                return cols_of(I["w_out"][l].rearrange("(k p) n -> p k n", p=P), block[1] * 512, 512)
            if kind == "wbr":
                name = ("w_br_a", "w_br_b", "w_br_c")[block[1]]
                return cols_of(I[name][l].rearrange("(k p) n -> p k n", p=P), block[2] * 512, 512)
            at, n = {"xbc": (C_XBC + 512 * block[1], 512), "dt": (C_DT, 32), "qk": (C_GQ, 512),
                     "gates": (C_GF, 32), "v": (C_GV, 512), "attq": (C_AQ, 512), "attkv": (C_AK, 256),
                     "z": (C_Z + 512 * block[1], 512), "r": (C_GR, 512),
                     "mg": (C_MG + D * block[1] + 512 * (block[2] if len(block) > 2 else 0), 512),
                     }[kind]
            return cols_of(w_in, at, n)

        def sp_stream(sp, l):
            for n, load in enumerate(loads):
                if load["layer"] != l:
                    continue
                if n >= RING:
                    sp.wait_ge(stream_full, loads[n - RING]["last"] + 1)
                src, w = block_source(l, load["block"])
                dst = ring[:, load["slot"], 0:src.shape[1], 0:w]
                sp.dma_start(dst, src).then_inc(landed[load["slot"]], 16)

        EXPERT = [("w1", 0), ("w3", 0), ("w1", 1), ("w3", 1), ("w2", 0), ("w2", 1)]

        def sp_experts(sp, l):
            def load(slot, e):
                name, half = EXPERT[slot]
                src = I[name][l][bass.ds(e, 1), :, half * 512:(half + 1) * 512]
                sp.dma_start(ex_slot[slot], src.rearrange("e (k p) n -> p (e k) n", p=P))\
                  .then_inc(s(f"expert_in{slot}", l), 16)

            UP, DOWN = range(4), range(4, 6)

            def consumed(slot, i):
                if slot in UP:
                    sp.wait_ge(s("up_full", l), count("up_full", l, i * 2 + (1 if slot < 2 else 2)))
                else:
                    sp.wait_ge(s("down_full", l), count("down_full", l, i * 2 + (slot - 3)))
            sp.wait_ge(s("x_new", l), count("x_new", l, 1))
            for slot in UP:
                load(slot, 0)
            sp.wait_ge(s("x_saved", l), count("x_saved", l, 16))
            sp.wait_ge(s("xn2", l), count("xn2", l, len(tiles_of(l))))
            load(5, 0)
            sp.wait_ge(s("row_saved", l), count("row_saved", l, 16))
            load(4, 0)
            for slot in UP:
                consumed(slot, 0)
                load(slot, 1)
            with sp.Fori(2, NE) as i:
                for slot in UP:
                    consumed(slot, i - 1)
                    load(slot, i)
                for slot in DOWN:
                    consumed(slot, i - 2)
                    load(slot, i - 1)
            for slot in DOWN:
                consumed(slot, NE - 2)
                load(slot, NE - 1)
            sp.wait_ge(s("route_ready", l), count("route_ready", l, 1))
            n_extra = sp.value_load(extra[0:1, 8:9], min_val=0, max_val=XTRA)
            for j in range(extra_blocks(l)):
                with sp.If(n_extra > j):
                    e = sp.value_load(extra[0:1, j:j + 1], min_val=0, max_val=NE - 1)
                    for slot in (*UP, *DOWN):
                        consumed(slot, NE + j - 1)
                        load(slot, e)

        def extra_blocks(l):
            return (len(tiles_of(l)) * P * 2 - 1) // P

        def pool_layer(pool, link, l):
            tiles = tiles_of(l)
            small_in = s("small_in", l)
            if l == 0:
                pool.dma_start(consts[:], I["consts"]).then_inc(const_in, 16)
                pool.dma_start(cond[:], I["cond"]).then_inc(const_in, 16)
                for t in range(TT):
                    src = I["ctx"][0] if t < 2 else I["x"][0]
                    pool.dma_start(xb[:, t, :], src[(t % 2) * P:(t % 2 + 1) * P, :]).then_inc(s("x_in", 0), 16)
                pool.memset(zero_idx[:], 0).then_inc(s("zeroed", 0), 1)
                pool.memset(eps_t[:], EPS).then_inc(s("eps_set", 0), 1)
            else:
                pool.wait_ge(s("layer_done", l - 1), count("layer_done", l - 1, 1))
                for t in range(TT):
                    pool.dma_start(x_dram[t * P:(t + 1) * P, :], xb[:, t, :]).then_inc(s("xd_saved", l), 16)
            pool.dma_start(rows[:], I["rows"][l:l + 1, :].to_broadcast([P, NROWS])).then_inc(small_in, 16)
            pool.dma_start(cols[:], I["cols"][l]).then_inc(small_in, 16)
            pool.dma_start(router_w[:], I["router_w"].rearrange("(k p) e -> p k e", p=P)).then_inc(small_in, 16)
            pool.dma_start(view(gate_w2[:], 2, 256), I["gla_w2"][l].rearrange("d r n -> r d n")).then_inc(small_in, 16)
            pool.dma_start(modr[0:2, :], I["b_mod"][l:l + 1, :].to_broadcast([2, NMOD * D])).then_inc(small_in, 16)
            pool.wait_ge(freer(l, "mod", 11), freed(l, "mod", 11))
            pool.dma_start(mod_dram[l], modr[0:2, :]).then_inc(s("mod_saved", l), 16)
            pool.wait_ge(s("mod_saved", l), count("mod_saved", l, 16))
            if l == 0:
                pool.wait_ge(s("ss1", 0), count("ss1", 0, TT))
                pool.memset(junk, 0.0).then_inc(s("zeroed", 0), 1)
                pool.wait_ge(s("zeroed", 0), count("zeroed", 0, 2))
                for b in range(NE * P, SLOTS, P):
                    pool.dma_start(y_dram[b:b + P, :], junk).then_inc(s("y_zero", 0), 16)
            pool.dma_start(tok_dram.rearrange("(p b) o -> p (b o)", p=P), zero_idx[:]).then_inc(s("tok_zero", l), 16)
            pool.wait_ge(s("ct_done", l), count("ct_done", l, 10))
            pool.wait_ge(s("w_ready", l), count("w_ready", l, 1))
            for q, t in enumerate(tiles):
                x3 = view(xs[:, t, :], SH, SP)
                for d in range(2):
                    if q >= 2:
                        pool.wait_ge(s("ymm_done", l), count("ymm_done", l, 8 * (q - 1)))
                    pool.tensor_tensor(view(xw[q % 2][d], SH, SP), x3,
                                       dt[:, t, d * 16:d * 16 + 16].unsqueeze(2).to_broadcast([P, SH, SP]),
                                       ALU.mult).then_inc(s("pool_x", l), 1)
                pool.tensor_tensor(view(ys[:, t, :], SH, SP), x3,
                                   Rw("ssd_d").unsqueeze(2).to_broadcast([P, SH, SP]),
                                   ALU.mult).then_inc(s("pool_x", l), 1)
            pool.wait_ge(s("ymm_done", l), count("ymm_done", l, 8 * len(tiles)))
            for k in range(3):
                for d in range(2):
                    b = ORDER[d][k]
                    if k:
                        pool.wait_ge(s("upd_full", l), count("upd_full", l, 2 * (k - 1) + d + 1))
                    pool.tensor_tensor(view(xw[0][d], SH, SP), view(xs[:, b, :], SH, SP),
                                       wd[:, b, d * 16:d * 16 + 16].unsqueeze(2).to_broadcast([P, SH, SP]),
                                       ALU.mult).then_inc(s("wx_ready", l), 1)
            pool.wait_ge(s("branch_rs", l), count("branch_rs", l, 1))
            t0 = tiles[0]
            pool.wait_ge(freer(l, "r", tiles[-1]), freed(l, "r", tiles[-1]))
            for t in tiles:
                y4 = view(yg[:, t, :], 4, P)
                link(pool.tensor_tensor(y4, y4, bc(gss[:, t, :], P), ALU.mult))
                link(pool.tensor_tensor(y4, y4, bc_mid(Rw("gla_norm"), 4), ALU.mult))
                pool.tensor_tensor(yg[:, t, :], yg[:, t, :], kv[:, t].rearrange("p a b c -> p (a b c)"), ALU.mult)
                y2 = view(ys[:, t, :], 2, 512)
                link(pool.tensor_tensor(y2, y2, bc(rstd[:, 2 * t:2 * t + 2], 512), ALU.mult))
                ins = pool.tensor_tensor(ys[:, t, :], ys[:, t, :], Rw("ssd_norm"), ALU.mult)
            ins.then_inc(s("branches_final", l), 1)
            pool.wait_ge(s("yt_act", l), count("yt_act", l, 2 * len(tiles)))
            pool.wait_ge(s("yt_dve", l), count("yt_dve", l, 2 * len(tiles)))
            if l:
                pool.wait_ge(s("xd_saved", l), count("xd_saved", l, 16 * TT))
            for t in tiles:
                if l == 0:
                    src = (I["ctx"][0] if t < 2 else I["x"][0])[(t % 2) * P:(t % 2 + 1) * P, :]
                else:
                    src = x_dram[t * P:(t + 1) * P, :]
                pool.dma_start(xb[:, t, :], src).then_inc(s("x_again", l), 16)
            for c in range(2):
                pool.dma_start(gate_bc[:, c, :], mod_dram[l, c:c + 1, 2 * D:3 * D].to_broadcast([P, D]))\
                    .then_inc(s("x_again", l), 16)
            pool.wait_ge(s("x_new", l), count("x_new", l, 1))
            pool.dma_start(x_dram[t0 * P:, :].rearrange("(t p) d -> p t d", p=P), xb[:, t0:, :])\
                .then_inc(s("x_saved", l), 16)
            pool.wait_ge(s("row_ready", l), count("row_ready", l, 2 * len(tiles)))
            pool.dma_start(h_dram[t0 * P:, :].rearrange("(t p) d -> p t d", p=P), h_rows[:, t0:, :])\
                .then_inc(s("row_saved", l), 16)
            if l == 0:
                pool.tensor_copy(tok_id[:], K("token")).then_inc(s("tok_id", 0), 1)
                pool.wait_ge(s("tok_id", 0), count("tok_id", 0, 1))
            pool.wait_ge(s("tok_zero", l), count("tok_zero", l, 16))
            pool.wait_ge(s("route_ready", l), count("route_ready", l, 1))
            n = 0
            for c in range(2):
                for t in tiles:
                    pool.indirect_dma_start(tok_dram, bass.IndirectOffsetOnAxis(ap=slot_idx[:, c * TT + t:c * TT + t + 1], axis=0),
                                            tok_id[:, t:t + 1], None).then_inc(s("tok_put", l), 16)
                    n += 1
            pool.wait_ge(s("tok_put", l), count("tok_put", l, 16 * n))
            pool.wait_ge(s("row_saved", l), count("row_saved", l, 16))
            pool.dma_start(tok_idx[:], tok_dram.rearrange("(b p) o -> p (b o)", p=P), allow_slow_non_contiguous=True).then_inc(s("tok_got", l), 16)
            pool.wait_ge(s("tok_got", l), count("tok_got", l, 16))
            pool.wait_ge(s("rows_full", l), count("rows_full", l, 2 * len(tiles)))

            def gather(idx):
                pool.indirect_dma_start(xg, None, h_dram, bass.IndirectOffsetOnAxis(ap=idx, axis=0))\
                    .then_inc(s("gathered", l), 16)
            gather(tok_idx[:, 0:1])
            for i in range(NE):
                pool.wait_ge(s("xt_full", l), count("xt_full", l, i + 1))
                gather(tok_idx[:, i + 1:i + 2])
            n_extra = pool.value_load(extra[0:1, 8:9], min_val=0, max_val=XTRA)
            for j in range(extra_blocks(l)):
                with pool.If(n_extra > j):
                    pool.wait_ge(s("xt_full", l), count("xt_full", l, NE + j + 1))
                    gather(tok_idx[:, NE + j + 1:NE + j + 2])
                    pool.wait_ge(s("stored", l), count("stored", l, 16 * (NE + j)))
            pool.wait_ge(s("all_stored", l), count("all_stored", l, 1))
            for t in tiles:
                for c in range(2):
                    pool.indirect_dma_start(yr[:, t, c, :], None, y_dram,
                                            bass.IndirectOffsetOnAxis(ap=slot_idx[:, c * TT + t:c * TT + t + 1], axis=0))\
                        .then_inc(s("y_got", l), 16)
            pool.dma_start(xb[:, t0:, :], x_dram[t0 * P:, :].rearrange("(t p) d -> p t d", p=P)).then_inc(s("y_got", l), 16)
            for c in range(2):
                pool.dma_start(gate_bc[:, c, :], mod_dram[l, c:c + 1, 5 * D:6 * D].to_broadcast([P, D]))\
                    .then_inc(s("y_got", l), 16)

        def pe_group(pe, l, kind, index):
            n = find[l, kind, index]
            g = groups[n]
            load = g["load"]
            pe.wait_ge(landed[loads[load]["slot"]], 16 * (load // RING + 1))
            if n >= NSTREAM:
                before = groups[n - NSTREAM]
                pe.wait_ge(free[before["engine"]], before["ordinal"])
            w = ring[:, loads[load]["slot"]]
            a, b = span_of(l)
            ks = KO
            if kind == "mod":
                dst, left, right = ps[0:2, g["bank"], :], lambda k: cond[:, k, :], lambda k: w[:, k, :]
            elif kind in ("xbc", "qk"):
                i = index % 4
                dst = ps[:, g["bank"], :]
                left, right = lambda k: w[:, k, i * P:(i + 1) * P], lambda k: hT[:, k, :]
            elif kind == "gates":
                dst = ps[0:16, g["bank"], :]
                left, right = lambda k: w[:, k, index * 16:(index + 1) * 16], lambda k: hT[:, k, :]
            elif kind in ("dt", "v", "attq", "attkv", "z", "r"):
                t = index[1] if kind == "z" else index
                n_cols = {"dt": 32, "attkv": 256}.get(kind, 512)
                dst = ps[:, g["bank"], 0:n_cols]
                left, right = lambda k: hT[:, k, t * P:(t + 1) * P], lambda k: w[:, k, 0:n_cols]
            elif kind == "gate":
                i = index[1] % 4
                dst = ps[:, g["bank"], 0:b - a]
                left, right = lambda k: w[:, k, i * P:(i + 1) * P], lambda k: hT[:, k, a:b]
            elif kind == "prod":
                j, i = index[0], index[1] % 4
                row = (0, 4, 8)[j]
                ks = (4, 4, 8)[j]
                dst = ps[:, g["bank"], 0:b - a]
                left, right = lambda k: w[:, k, i * P:(i + 1) * P], lambda k: yT[:, row + k, a:b]
            else:
                t = index[1]
                dst = ps[:, g["bank"], :]
                left, right = lambda k: merged[:, k, t * P:(t + 1) * P], lambda k: w[:, k, :]
            for k in range(ks):
                ins = pe.matmul(dst, left(k), right(k), start=(k == 0), stop=(k == ks - 1))
            ins.then_inc(stream_full, 1)

        def pe_norm(pe, l, which, tiles):
            for n, t in enumerate(tiles):
                pe.wait_ge(s(f"xn{which}", l), count(f"xn{which}", l, n + 1))
                if n >= 2:
                    pe.wait_ge(s(f"hT{which}", l), count(f"hT{which}", l, n - 1))
                for k in range(KO):
                    ins = pe.transpose(ps[:, 2 + 2 * (n % 2) + k // 4, (k % 4) * P:(k % 4 + 1) * P],
                                       xn[:, t, k * P:(k + 1) * P], ident)
                ins.then_inc(s(f"tr{which}", l), 1)
            pe.wait_ge(s(f"hT{which}", l), count(f"hT{which}", l, len(tiles)))

        def pe_ssd(pe, l):
            tiles = tiles_of(l)
            pe.wait_ge(s("da_ready", l), count("da_ready", l, 1))
            pe.wait_ge(s("ct_done", l), count("ct_done", l, 9))
            for t in range(TT):
                pe.matmul(ps[:, 4, t * 64:t * 64 + 16], upper, da[:, t, 0:16], start=True, stop=True)
                pe.matmul(ps[:, 4, t * 64 + 16:t * 64 + 32], lower, da[:, t, 16:32], start=True, stop=True)
                ins = pe.matmul(ps[:, 4, t * 64 + 32:t * 64 + 64], ones, da[:, t, :], start=True, stop=True)
            ins.then_inc(s("cum_full", l), 1)

        def pe_scan(pe, l):
            tiles = tiles_of(l)
            pe.wait_ge(s("ct_done", l), count("ct_done", l, 10))

            def spread(q, t, k):
                kq = q * 8 + k
                if kq >= 3:
                    pe.wait_ge(s("diff_done", l), count("diff_done", l, kq - 2))
                d, quad = k // 4, k % 4
                for i in range(4):
                    h = d * 16 + quad * 4 + i
                    ins = pe.matmul(ps[:, SPREAD[kq % 3], i * P:(i + 1) * P],
                                    da[:, t, h:h + 1].to_broadcast([P, P]), tri[d], start=True, stop=True)
                ins.then_inc(s("bc_full", l), 1)

            def within(q, t, k):
                kq = q * 8 + k
                d, quad = k // 4, k % 4
                pe.wait_ge(s("m_ready", l), count("m_ready", l, kq + 1))
                if k == 0:
                    pe.wait_ge(s("pool_x", l), count("pool_x", l, 3 * q + 3))
                    if q:
                        pe.wait_ge(s("y_evac", l), count("y_evac", l, q))
                for i in range(4):
                    h = quad * 4 + i
                    ins = pe.matmul(ps[:, 5 + h // 8, (h % 8) * SP:(h % 8 + 1) * SP],
                                    mm[kq % 2][:, i * P:(i + 1) * P], xw[q % 2][d][:, h * SP:(h + 1) * SP],
                                    start=(d == 0 and h % 8 == 0), stop=(d == 1), skip_group_check=True)
                ins.then_inc(s("ymm_done", l), 1)
            pe.wait_ge(s("cum_ready", l), count("cum_ready", l, 1))
            steps = []
            for q, t in enumerate(tiles):
                if q:
                    pe.wait_ge(s("cbm_ready", l), count("cbm_ready", l, q))
                for g in range(2):
                    ins = pe.matmul(ps[:, 2, g * P:(g + 1) * P], bcT[:, g, t * P:(t + 1) * P],
                                    bcT[:, 2 + g, t * P:(t + 1) * P], start=True, stop=True)
                ins.then_inc(s("cb_full", l), 1)
                for k in range(8):
                    spread(q, t, k)
                    for kind, index in fills(l, q * 8 + k):
                        pe_group(pe, l, kind, index)
                    steps.append((q, t, k))
                    if len(steps) > 2:
                        within(*steps[-3])
            within(*steps[-2])
            within(*steps[-1])
            pe.wait_ge(s("y_evac", l), count("y_evac", l, len(tiles)))
            pe.wait_ge(s("cbm_ready", l), count("cbm_ready", l, len(tiles)))
            n_inter = 0
            for k in range(4):
                for d in range(2):
                    b = ORDER[d][k]
                    u = 2 * k + d
                    if k and b in tiles:
                        pe.wait_ge(s("s_ready", l), count("s_ready", l, u - 1))
                        if n_inter:
                            pe.wait_ge(s("inter_done", l), count("inter_done", l, n_inter))
                        for g in range(2):
                            ins = pe.matmul(ps[:, 2 + g, :], bcT[:, 2 + g, b * P:(b + 1) * P],
                                            state[:, d, g * 512:(g + 1) * 512], start=True, stop=True)
                        ins.then_inc(s("inter_full", l), 1)
                        n_inter += 1
                    if k < 3:
                        if u:
                            pe.wait_ge(s("s_ready", l), count("s_ready", l, u))
                        pe.wait_ge(s("wx_ready", l), count("wx_ready", l, u + 1))
                        for g in range(2):
                            ins = pe.matmul(ps[:, 5 + g, :], b_tm[:, b, g * P:(g + 1) * P],
                                            xw[0][d][:, g * 512:(g + 1) * 512], start=True, stop=True)
                        ins.then_inc(s("upd_full", l), 1)

        def pe_gla(pe, l):
            tiles = tiles_of(l)
            pe.wait_ge(s("inter_done", l), count("inter_done", l, n_inters(l)))
            pe.wait_ge(s("s_ready", l), count("s_ready", l, 6))
            for t in range(TT):
                for d in range(2):
                    ins = pe.matmul(ps[:, 2 + t, d * 256:(d + 1) * 256], gT[0:16, d, t * P:(t + 1) * P],
                                    gate_w2[:, d * 256:(d + 1) * 256], start=True, stop=True)
            ins.then_inc(s("lg_full", l), 1)
            pe.wait_ge(s("g_ready", l), count("g_ready", l, 1))

            def running(t):
                if t >= 2:
                    pe.wait_ge(s("b_done", l), count("b_done", l, t - 1))
                for d in range(2):
                    for f in range(2):
                        j = d * 2 + f
                        ins = pe.matmul(ps[:, 6 + t % 2, j * P:(j + 1) * P],
                                        gg[:, t, d * 256 + f * P:d * 256 + (f + 1) * P], tri[d], start=True, stop=True)
                ins.then_inc(s("b_full", l), 1)
            running(0)
            for t in range(TT):
                if t < TT - 1:
                    running(t + 1)
                for _, index in z_groups(l, t):
                    pe_group(pe, l, "z", index)
                pe.wait_ge(s("qkd_ready", l), count("qkd_ready", l, t + 1))
                if t:
                    pe.wait_ge(s("kdt_ready", l), count("kdt_ready", l, t))
                for d in range(2):
                    for f in range(2):
                        ins = pe.transpose(ps[:, 2, (d * 2 + f) * P:(d * 2 + f + 1) * P], kd[:, t * 2 + d, f, :], ident)
                ins.then_inc(s("kdt_full", l), 1)
                pe.wait_ge(s("kdt_ready", l), count("kdt_ready", l, t + 1))
                if t:
                    pe.wait_ge(s("kv_done", l), count("kv_done", l, t))
                for d in range(2):
                    for f in range(2):
                        ins = pe.matmul(ps[:, 3 + d, f * 256:(f + 1) * 256], kdT[:, d * 2 + f, :],
                                        gv[:, t, f * 256:(f + 1) * 256], start=True, stop=True)
                ins.then_inc(s("kv_full", l), 1)
            pe.wait_ge(s("kv_done", l), count("kv_done", l, TT))
            for q, t in enumerate(tiles):
                if q >= 2:
                    pe.wait_ge(s("p_ready", l), count("p_ready", l, 2 * (q - 1)))
                for d in range(2):
                    for h in range(4):
                        lo, f = 64 * (h % 2), h // 2
                        ins = pe.matmul(ps[:, (2, 6)[q % 2] + h % 2, (d * 2 + f) * P:(d * 2 + f + 1) * P],
                                        kd[lo:lo + 64, t * 2 + d, f, :],
                                        qd[lo:lo + 64, t * 2 + d, f, :], start=True, stop=True)
                ins.then_inc(s("sc_full", l), 1)
                if q == 0:
                    pe.wait_ge(s("sp_ready", l), count("sp_ready", l, 1))
                pe_group(pe, l, "r", t)
                pe.wait_ge(s("p_ready", l), count("p_ready", l, 2 * q + 2))
                if q:
                    pe.wait_ge(s("gy_done", l), count("gy_done", l, q))
                for h in range(4):
                    lo, f = 64 * (h % 2), h // 2
                    dst = ps[:, 4 + h % 2, f * P:(f + 1) * P]
                    terms = [(pm[d][:, h, :], gv[:, t, h * P:(h + 1) * P]) for d in range(2)]
                    terms += [(qd[lo:lo + 64, t * 2 + d, f, :], sp[lo:lo + 64, t * 2 + d, f, :])
                              for d in range(2) if t != ORDER[d][0]]
                    for n, (a, b) in enumerate(terms):
                        ins = pe.matmul(dst, a, b, start=(n == 0), stop=(n == len(terms) - 1))
                ins.then_inc(s("gy_full", l), 1)

        def pe_att(pe, l):
            tiles = tiles_of(l)
            for t in range(TT):
                pe.wait_ge(s("att_prep", l), count("att_prep", l, t + 1))
                if t:
                    pe.wait_ge(s("qk_turned", l), count("qk_turned", l, t))
                if t in tiles:
                    for f in range(4):
                        pe.transpose(ps[:, 2, f * P:(f + 1) * P], att[:, t, f * P:(f + 1) * P], ident)
                for g in range(2):
                    ins = pe.transpose(ps[:, 3, g * P:(g + 1) * P],
                                       kdup[:, t, g, :, :].rearrange("p a b -> p (a b)"), ident)
                ins.then_inc(s("qk_full", l), 1)
            pe.wait_ge(s("qk_turned", l), count("qk_turned", l, TT))
            pe.wait_ge(s("gy_done", l), count("gy_done", l, len(tiles)))

            def scores(q, t, h):
                n = q * 8 + h
                if n >= 2:
                    pe.wait_ge(s("p_exp", l), count("p_exp", l, n - 1))
                lo = 64 * (h % 2)
                w = CTX if t < 2 else TOK
                a = qT[lo:lo + 64, h // 2, t * P:(t + 1) * P]
                ins = pe.matmul(ps[:, 4 + n % 2, 0:w], a, kT2[lo:lo + 64, h // 4, 0:w], start=True, stop=(t < 2),
                                skip_group_check=True)
                if t >= 2:
                    ins = pe.matmul(ps[:, 4 + n % 2, CTX:TOK], ident, view(K("window"), 2, 256)[:, t - 2, :],
                                    start=False, stop=True, skip_group_check=True)
                ins.then_inc(s("s_full", l), 1)

            def turn(q, t, h):
                n = q * 8 + h
                pe.wait_ge(s("p_exp", l), count("p_exp", l, n + 1))
                if n >= 2:
                    pe.wait_ge(s("pt_ready", l), count("pt_ready", l, n - 1))
                for j in range(2 if t < 2 else 4):
                    ins = pe.transpose(ps[:, 6 + n % 2, j * P:(j + 1) * P], pb[n % 2][:, j * P:(j + 1) * P], ident)
                ins.then_inc(s("pt_full", l), 1)

            def values(q, t, h):
                n = q * 8 + h
                pe.wait_ge(s("pt_ready", l), count("pt_ready", l, n + 1))
                if h == 0 and q >= 2:
                    pe.wait_ge(s("o_raw", l), count("o_raw", l, q - 1))
                nk = 2 if t < 2 else 4
                for j in range(nk):
                    g = h // 4
                    ins = pe.matmul(ps[:, 2 + q % 2, h * 64:(h + 1) * 64], pT[n % 2][:, j, :],
                                    att[:, j, 640 + g * 64:640 + (g + 1) * 64], start=(j == 0), stop=(j == nk - 1))
                ins.then_inc(s("o_full", l), 1)
            seq = [(q, t, h) for q, t in enumerate(tiles) for h in range(8)]
            for i in range(len(seq) + 2):
                if i < len(seq):
                    scores(*seq[i])
                if 1 <= i <= len(seq):
                    turn(*seq[i - 1])
                if i >= 2:
                    values(*seq[i - 2])

        def y_source(t, c):
            if c < 2:
                return ys[:, t, c * 512:(c + 1) * 512], 8 + 4 * c
            if c == 2:
                return yg[:, t, :], 0
            return att[:, t, 0:512], 4

        def pe_turn_y(pe, l):
            tiles = tiles_of(l)
            pe.wait_ge(s("branches_final", l), count("branches_final", l, 1))
            pe.wait_ge(s("o_done", l), count("o_done", l, len(tiles)))
            for n in range(4 * len(tiles)):
                src, _ = y_source(tiles[n // 4], n % 4)
                if n >= 4:
                    pe.wait_ge(s("yt_dve" if n % 2 else "yt_act", l), count("yt_dve" if n % 2 else "yt_act", l, (n - 4) // 2 + 1))
                for i in range(4):
                    ins = pe.transpose(ps[:, 2 + n % 4, i * P:(i + 1) * P], src[:, i * P:(i + 1) * P], ident)
                ins.then_inc(s("yt_full", l), 1)
            pe.wait_ge(s("yt_act", l), count("yt_act", l, 2 * len(tiles)))
            pe.wait_ge(s("yt_dve", l), count("yt_dve", l, 2 * len(tiles)))

        def pe_route(pe, l):
            tiles = tiles_of(l)
            for t in tiles:
                for k in range(KO):
                    ins = pe.matmul(ps[:, 6, t * NE:(t + 1) * NE], hT[:, k, t * P:(t + 1) * P], router_w[:, k, :],
                                    start=(k == 0), stop=(k == KO - 1))
            ins.then_inc(s("logit_full", l), 1)
            for n in range(2 * len(tiles)):
                t, half = tiles[n // 2], n % 2
                if n >= 2:
                    pe.wait_ge(s("row_ready", l), count("row_ready", l, n - 1))
                for i in range(4):
                    ins = pe.transpose(ps[:, 2 + n % 2, i * P:(i + 1) * P],
                                       hT[:, half * 4 + i, t * P:(t + 1) * P], ident)
                ins.then_inc(s("rows_full", l), 1)
            pe.wait_ge(s("assigned", l), count("assigned", l, 1))
            for n, t in enumerate(tiles):
                for m in range(n):
                    pe.matmul(ps[:, 6, t * NE:(t + 1) * NE], ones, t16[:, tiles[m], :], start=(m == 0), stop=False)
                pe.matmul(ps[:, 6, t * NE:(t + 1) * NE], K("strict"), t16[:, t, :], start=(n == 0), stop=True)
            for n, t in enumerate(tiles):
                ins = pe.matmul(ps[:, 6, 64:64 + NE], ones, t16[:, t, :], start=(n == 0), stop=(n == len(tiles) - 1))
            ins.then_inc(s("rank_full", l), 1)

        def pe_experts(pe, l):
            def turn_x(i):
                pe.wait_ge(s("gathered", l), count("gathered", l, (i + 1) * 16))
                for k in range(KO):
                    ins = pe.transpose(ps[:, k // 4, (k % 4) * P:(k % 4 + 1) * P], xg[:, k * P:(k + 1) * P], ident)
                ins.then_inc(s("xt_full", l), 1)

            def up(i, half):
                if half == 0:
                    pe.wait_ge(s("xt_ready", l), count("xt_ready", l, i + 1))
                if not first(i):
                    pe.wait_ge(s("hid_ready", l), count("hid_ready", l, i * 2 - 1 + half))
                for m in range(2):
                    slot = half * 2 + m
                    pe.wait_ge(s(f"expert_in{slot}", l), count(f"expert_in{slot}", l, (i + 1) * 16))
                    for k in range(KO):
                        ins = pe.matmul(ps[:, 2 + slot, :], xT[:, k, :], ex_slot[slot][:, k, :],
                                        start=(k == 0), stop=(k == KO - 1))
                ins.then_inc(s("up_full", l), 1)

            def turn_hid(i):
                pe.wait_ge(s("xt_ready", l), count("xt_ready", l, i + 2))
                for half in range(2):
                    pe.wait_ge(s("hid_ready", l), count("hid_ready", l, i * 2 + half + 1))
                    for j in range(4):
                        ins = pe.transpose(ps[:, half, j * P:(j + 1) * P],
                                           hid[:, half * 512 + j * P:half * 512 + (j + 1) * P], ident)
                    ins.then_inc(s("ht_full", l), 1)

            def down(i):
                pe.wait_ge(s("ht_ready", l), count("ht_ready", l, i * 2 + 2))
                for half in range(2):
                    pe.wait_ge(s(f"expert_in{4 + half}", l), count(f"expert_in{4 + half}", l, (i + 1) * 16))
                    for k in range(KO):
                        ins = pe.matmul(ps[:, 6 + half, :], hidT[:, k, :], ex_slot[4 + half][:, k, :],
                                        start=(k == 0), stop=(k == KO - 1))
                    ins.then_inc(s("down_full", l), 1)

            def block(i):
                up(i, 0)
                up(i, 1)
                if not first(i):
                    pe.wait_ge(s("ht_ready", l), count("ht_ready", l, i * 2))
                turn_x(i + 1)
                if not first(i):
                    down(i - 1)
                turn_hid(i)
            pe.wait_ge(s("row_ready", l), count("row_ready", l, 2 * len(tiles_of(l))))
            pe.wait_ge(s("route_ready", l), count("route_ready", l, 1))
            turn_x(0)
            block(0)
            with pe.Fori(1, NE) as i:
                block(i)
            n_extra = pe.value_load(extra[0:1, 8:9], min_val=0, max_val=XTRA)
            for j in range(extra_blocks(l)):
                with pe.If(n_extra > j):
                    block(NE + j)
            down(n_extra + (NE - 1))

        def pe_layer(pe, l):
            tiles = tiles_of(l)
            if l == 0:
                pe.wait_ge(const_in, 32)
                pe.wait_ge(cond_ready, 1)
            for c in range(12):
                pe_group(pe, l, "mod", c)
            pe.wait_ge(freer(l, "mod", 11), freed(l, "mod", 11))
            for v, m in enumerate((0, 1, 3, 4)):
                for k in range(KO):
                    ins = pe.transpose(ps[:, 6, (v * KO + k) * 2:(v * KO + k) * 2 + 2],
                                       modr[0:2, m * D + k * P:m * D + (k + 1) * P], ident[0:2, 0:2])
            ins.then_inc(s("modT_full", l), 1)
            pe_norm(pe, l, 1, range(TT))

            def turn_conv(i):
                pe.wait_ge(s("conv_done", l), count("conv_done", l, i + 1))
                if i >= 2:
                    pe.wait_ge(s("ct_done", l), count("ct_done", l, i - 1))
                src = xsT[:, i % 2, :] if i < 8 else bcT[:, i - 8, :]
                for t in range(TT):
                    ins = pe.transpose(ps[:, 2 + i % 2, t * P:(t + 1) * P], src[:, t * P:(t + 1) * P], ident)
                ins.then_inc(s("ct_full", l), 1)
            for i in range(12):
                pe_group(pe, l, "xbc", i)
                if i >= 2:
                    turn_conv(i - 2)
            for t in range(TT):
                pe_group(pe, l, "dt", t)
            for i in range(4):
                pe_group(pe, l, "qk", i)
            pe_ssd(pe, l)
            for i in range(2):
                pe_group(pe, l, "gates", i)
            pe_scan(pe, l)
            pe.wait_ge(freer(l, "attkv", TT - 1), freed(l, "attkv", TT - 1))
            pe_gla(pe, l)
            pe_att(pe, l)
            pe_turn_y(pe, l)
            for j in range(3):
                for i in range(KO):
                    pe_group(pe, l, "gate", (j, i))
                    pe_group(pe, l, "prod", (j, i))
            pe.wait_ge(freer(l, "prod", (2, KO - 1)), freed(l, "prod", (2, KO - 1)))
            pe.wait_ge(s("merged", l), count("merged", l, 1))
            for half in range(2):
                for t in tiles:
                    pe_group(pe, l, "out", (half, t))
            pe_norm(pe, l, 2, tiles)
            pe_route(pe, l)
            pe_experts(pe, l)

        def act_norm(act, l, which, tiles):
            for n, t in enumerate(tiles):
                if n:
                    act.wait_ge(s(f"ss{which}", l), count(f"ss{which}", l, n))
                act.activation(junk, xb[:, t, :], ACT.Square, accum_out=sumsq[:, t:t + 1]).then_inc(s(f"ss{which}", l), 1)
            act.wait_ge(s(f"ss{which}", l), count(f"ss{which}", l, len(tiles)))
            rms(act, sumsq[:, tiles[0]:TT], rstd[:, tiles[0]:TT], D).then_inc(s(f"rs{which}", l), 1)

        def rms(act, src, dst, n):
            alink(act.activation(dst, src, ACT.Ln, scale=1.0 / n, bias=eps_t[:, 0:1]))
            return act.activation(dst, dst, ACT.Exp, scale=-0.5)

        def softplus_of_minus_abs(act, ap, src):
            alink(act.activation(ap, src, ACT.Abs))
            alink(act.activation(ap, ap, ACT.Exp, scale=-1.0))
            return act.activation(ap, ap, ACT.Ln, bias=1.0)

        def act_group(act, l, kind, index, dst, scale=1.0):
            act.wait_ge(stream_full, filled(l, kind, index))
            bank = bank_of(l, kind, index)
            n_part = 16 if kind == "gates" else P
            w = {"attkv": 256}.get(kind, 512)
            act.activation(dst, ps[0:n_part, bank, 0:w], ACT.Copy, scale=scale).then_inc(free["act"], 1)

        def act_layer(act, l):
            tiles = tiles_of(l)
            n_t = len(tiles)
            t0 = tiles[0]
            if l == 0:
                act.wait_ge(const_in, 32)
                act.activation(cond_e[:], cond[:], ACT.Exp, scale=-1.0).then_inc(cond_exp, 1)
                act.wait_ge(s("x_in", 0), count("x_in", 0, 16 * TT))
                act.wait_ge(s("eps_set", 0), count("eps_set", 0, 1))
            else:
                act.wait_ge(s("layer_done", l - 1), count("layer_done", l - 1, 1))
            act_norm(act, l, 1, range(TT))
            act.wait_ge(s("small_in", l), count("small_in", l, 80))
            alink(act.activation(neg_a[:], Rw("a_log"), ACT.Exp))
            if l:
                act.wait_ge(s("xd_saved", l), count("xd_saved", l, 16 * TT))
            act.wait_ge(s("hT1", l), count("hT1", l, TT))
            for i in range(12):
                if i >= 3:
                    act.wait_ge(s("conv_acc", l), count("conv_acc", l, i - 2))
                act_group(act, l, "xbc", i, raw[:, i % 3, :])
                if i >= 1:
                    act_conv_silu(act, l, i - 1)
                if i >= 2:
                    act_conv_rows(act, l, i - 2)
            act_conv_silu(act, l, 11)
            act.wait_ge(s("sp1", l), count("sp1", l, 1))
            softplus_of_minus_abs(act, dt[:], dt_raw[:]).then_inc(s("sp2", l), 1)
            for i in range(4):
                act_group(act, l, "qk", i, qkT[:, i, :], scale=0.125 if i < 2 else 1.0)
            act.wait_ge(s("cum_ready", l), count("cum_ready", l, 1))
            alink(act.activation(ecs[:], cums[:], ACT.Exp))
            act.wait_ge(s("wd_pre", l), count("wd_pre", l, 1))
            act.activation(wd[:], wd[:], ACT.Exp).then_inc(s("ecs_ready", l), 1)
            for i in range(2):
                act_group(act, l, "gates", i, gT[0:16, i, :])
            for kq in range(8 * n_t):
                act.wait_ge(s("dm_ready", l), count("dm_ready", l, kq + 1))
                act.activation(dd[kq % 3], dd[kq % 3], ACT.Exp).then_inc(s("e_ready", l), 1)
                for kind, t in fills(l, kq):
                    place = {"v": gv, "attq": att[:, :, 0:512], "attkv": att[:, :, 512:768]}[kind]
                    act_group(act, l, kind, t, place[:, t, :])
            act.wait_ge(s("gabs", l), count("gabs", l, 1))
            softplus_of_minus_abs(act, kv.rearrange("p t a b c -> p (t a b c)"), gg.rearrange("p a b -> p (a b)")).then_inc(s("gsp", l), 1)
            act.wait_ge(s("upd_full", l), count("upd_full", l, 6))
            for t in range(TT):
                act.wait_ge(s("b_done", l), count("b_done", l, t + 1))
                act.activation(eb[:, 0], eb[:, 0], ACT.Exp)
                act.activation(eb[:, 1], eb[:, 1], ACT.Exp, scale=-1.0).then_inc(s("eb_ready", l), 1)
                for n, index in z_groups(l, t):
                    act.wait_ge(stream_full, filled(l, "z", index))
                    if n >= 2:
                        act.wait_ge(s("yz_ready", l), count("yz_ready", l, n - 1))
                    act.activation(zs[n % 2], ps[:, bank_of(l, "z", index), :], ACT.Silu).then_inc(free["act"], 1)
                act.wait_ge(s("kdt_full", l), count("kdt_full", l, t + 1))
                if t:
                    act.wait_ge(s("kv_full", l), count("kv_full", l, t))
                act.activation(kdT.rearrange("p a b -> p (a b)"), ps[:, 2, :], ACT.Copy).then_inc(s("kdt_ready", l), 1)
            act.wait_ge(s("btm_ready", l), count("btm_ready", l, 1))
            act.activation(btm[:], btm[:], ACT.Exp)
            act.activation(bme[:], bmt[:], ACT.Exp).then_inc(s("bme_ready", l), 1)
            act.wait_ge(s("sp_ready", l), count("sp_ready", l, 1))
            for q, t in enumerate(tiles):
                act.wait_ge(stream_full, filled(l, "r", t))
                act.activation(kv[:, t].rearrange("p a b c -> p (a b c)"), ps[:, bank_of(l, "r", t), :], ACT.Silu)\
                    .then_inc(free["act"], 1)
                act.wait_ge(s("gy_full", l), count("gy_full", l, q + 1))
                act.activation(yg[:, t, :].rearrange("p (f r e) -> p r f e", f=2, r=2),
                               ps[:, 4:6, 0:256].rearrange("p r (f e) -> p r f e", f=2), ACT.Copy).then_inc(s("gy_done", l), 1)
            act.wait_ge(s("gy_done", l), count("gy_done", l, n_t))
            act.activation(qd.rearrange("p a b c -> p (a b c)")[:, t0 * 512:], yg[:, t0:, :].rearrange("p a b -> p (a b)"), ACT.Square)\
                .then_inc(s("gsq", l), 1)
            act.wait_ge(s("yz_ready", l), count("yz_ready", l, 2 * n_t))
            for t in tiles:
                for g in range(2):
                    alink(act.activation(zs[0], ys[:, t, g * 512:(g + 1) * 512], ACT.Square,
                                         accum_out=sumsq[:, t * 2 + g:t * 2 + g + 1]))
            act.wait_ge(s("ass_ready", l), count("ass_ready", l, 1))
            rms(act, ass[:, :, 8:10], ass[:, :, 8:10], HD)
            rms(act, ass[:, t0:, 0:8], ass[:, t0:, 0:8], HD).then_inc(s("ar_ready", l), 1)
            act.wait_ge(s("gss_ready", l), count("gss_ready", l, 1))
            rms(act, gss[:, t0:, :], gss[:, t0:, :], P)
            rms(act, sumsq[:, 2 * t0:2 * TT], rstd[:, 2 * t0:2 * TT], 512).then_inc(s("branch_rs", l), 1)
            for t in range(TT):
                act.wait_ge(s("qk_full", l), count("qk_full", l, t + 1))
                if t in tiles:
                    act.activation(qT[:, :, t * P:(t + 1) * P], view(ps[:, 2, :], 4, P), ACT.Copy)
                act.activation(kT2[:, :, t * P:(t + 1) * P], view(ps[:, 3, 0:256], 2, P), ACT.Copy)\
                    .then_inc(s("qk_turned", l), 1)
            seq = [(q, t, h) for q, t in enumerate(tiles) for h in range(8)]

            def p_exp(n, t):
                w = CTX if t < 2 else TOK
                act.wait_ge(s("nmax_ready", l), count("nmax_ready", l, n + 1))
                if n >= 2:
                    act.wait_ge(s("pt_full", l), count("pt_full", l, n - 1))
                act.activation(pb[n % 2][:, 0:w], ps[:, 4 + n % 2, 0:w], ACT.Exp, scale=0.125,
                               bias=nmax[:, n:n + 1], accum_out=rsum[:, n:n + 1]).then_inc(s("p_exp", l), 1)

            def p_rows(n, t):
                w = CTX if t < 2 else TOK
                act.wait_ge(s("pt_full", l), count("pt_full", l, n + 1))
                if n >= 2:
                    act.wait_ge(s("o_full", l), count("o_full", l, n - 1))
                act.activation(pT[n % 2].rearrange("p a b -> p (a b)")[:, 0:w], ps[:, 6 + n % 2, 0:w], ACT.Copy)\
                    .then_inc(s("pt_ready", l), 1)
            for i in range(len(seq) + 1):
                if i < len(seq):
                    p_exp(i, seq[i][1])
                if i:
                    p_rows(i - 1, seq[i - 1][1])
            act.wait_ge(s("sink_pre", l), count("sink_pre", l, 1))
            act.activation(nmax[:, 0:8 * n_t], nmax[:, 0:8 * n_t], ACT.Exp).then_inc(s("sink_exp", l), 1)
            act.wait_ge(s("o_done", l), count("o_done", l, n_t))
            for n in range(0, 4 * n_t, 2):
                _, f = y_source(tiles[n // 4], n % 4)
                t = tiles[n // 4]
                act.wait_ge(s("yt_full", l), count("yt_full", l, n + 1))
                act.activation(yT[:, f:f + 4, t * P:(t + 1) * P], view(ps[:, 2 + n % 4, :], 4, P), ACT.Copy)\
                    .then_inc(s("yt_act", l), 1)
            a, b = span_of(l)
            w = b - a
            act.wait_ge(s("neg_ready", l), count("neg_ready", l, 1))
            for j in range(3):
                for i in range(KO):
                    n = j * KO + i
                    if n >= 2:
                        act.wait_ge(freer(l, "prod", ((n - 2) // KO, (n - 2) % KO)), freed(l, "prod", ((n - 2) // KO, (n - 2) % KO)))
                    if n - 2 >= KO:
                        act.wait_ge(s("merge_acc", l), count("merge_acc", l, n - 1 - KO))
                    act.wait_ge(stream_full, filled(l, "gate", (j, i)))
                    bank = bank_of(l, "gate", (j, i))
                    act.activation(gate_e[n % 2][:, 0:w], ps[:, bank, 0:w], ACT.Sigmoid,
                                   bias=Cl("gate_b")[:, n:n + 1]).then_inc(free["act"], 1)
            act.wait_ge(s("x_new", l), count("x_new", l, 1))
            act_norm(act, l, 2, tiles)
            act.wait_ge(s("logit_full", l), count("logit_full", l, 1))
            act.activation(sc[:, t0:, :], view(ps[:, 6, t0 * NE:TT * NE], n_t, NE), ACT.Exp, scale=-1.0)\
                .then_inc(s("logit_exp", l), 1)
            act.wait_ge(s("hT2", l), count("hT2", l, n_t))
            for n in range(2 * n_t):
                t, half = tiles[n // 2], n % 2
                act.wait_ge(s("rows_full", l), count("rows_full", l, n + 1))
                act.activation(h_rows[:, t, half * 512:(half + 1) * 512], ps[:, 2 + n % 2, :], ACT.Copy)\
                    .then_inc(s("row_ready", l), 1)
            act.wait_ge(s("row_saved", l), count("row_saved", l, 16))

            def results(i):
                for half in range(2):
                    act.wait_ge(s("down_full", l), count("down_full", l, i * 2 + half + 1))
                    act.activation(ob[:, half * 512:(half + 1) * 512], ps[:, 6 + half, :], ACT.Copy)\
                        .then_inc(s("ob_done", l), 1)
                act.wait_ge(s("ob_done", l), count("ob_done", l, i * 2 + 2))
                dst = y_dram[bass.ds(i * P, P), :] if not isinstance(i, int) else y_dram[i * P:(i + 1) * P, :]
                act.dma_start(dst, ob).then_inc(s("stored", l), 16)

            def expert(i):
                for half in range(2):
                    act.wait_ge(s("up_full", l), count("up_full", l, i * 2 + half + 1))
                    act.activation(silu_h[half], ps[:, 2 + 2 * half, :], ACT.Silu).then_inc(s("silu_ready", l), 1)
                if not first(i):
                    results(i - 1)
                for half in range(2):
                    act.wait_ge(s("ht_full", l), count("ht_full", l, i * 2 + half + 1))
                    act.activation(hidT[:, half * 4:half * 4 + 4, :].rearrange("p a b -> p (a b)"),
                                   ps[:, half, :], ACT.Copy).then_inc(s("ht_ready", l), 1)
                if not first(i):
                    act.wait_ge(s("stored", l), count("stored", l, i * 16))
            expert(0)
            with act.Fori(1, NE) as i:
                expert(i)
            act.wait_ge(s("route_ready", l), count("route_ready", l, 1))
            n_extra = act.value_load(extra[0:1, 8:9], min_val=0, max_val=XTRA)
            for j in range(extra_blocks(l)):
                with act.If(n_extra > j):
                    expert(NE + j)
            results(n_extra + (NE - 1))
            act.wait_ge(s("stored", l), count("stored", l, (n_extra + NE) * 16))
            act.activation(sumsq[:, 0:1], rstd[:, 0:1], ACT.Copy).then_inc(s("all_stored", l), 1)

        def act_conv_silu(act, l, i):
            act.wait_ge(s("conv_acc", l), count("conv_acc", l, i + 1))
            acc = xsT[:, i % 2, :] if i < 8 else bcT[:, i - 8, :]
            act.activation(acc, acc, ACT.Silu).then_inc(s("conv_done", l), 1)

        def act_conv_rows(act, l, i):
            act.wait_ge(s("ct_full", l), count("ct_full", l, i + 1))
            dst = xs[:, :, i * P:(i + 1) * P] if i < 8 else b_tm[:, :, (i - 8) * P:(i - 7) * P]
            act.activation(dst, view(ps[:, 2 + i % 2, :], TT, P), ACT.Copy).then_inc(s("ct_done", l), 1)

        def dve_norm(dve, l, which, tiles):
            dve.wait_ge(s(f"rs{which}", l), count(f"rs{which}", l, 1))
            for t in tiles:
                dve.tensor_scalar(xn[:, t, :], xb[:, t, :], rstd[:, t:t + 1], None, ALU.mult).then_inc(s(f"xn{which}", l), 1)
            for n, t in enumerate(tiles):
                c = 0 if t < 2 else 1
                dve.wait_ge(s(f"tr{which}", l), count(f"tr{which}", l, n + 1))
                for k in range(KO):
                    ins = dve.tensor_scalar(hT[:, k, t * P:(t + 1) * P],
                                            ps[:, 2 + 2 * (n % 2) + k // 4, (k % 4) * P:(k % 4 + 1) * P],
                                            scale_a[:, which - 1, k, c:c + 1], modc[:, 2 * (which - 1), k, c:c + 1],
                                            ALU.mult, ALU.add)
                ins.then_inc(s(f"hT{which}", l), 1)

        def bc(ap, n):
            return ap.unsqueeze(len(ap.shape)).to_broadcast([*ap.shape, n])

        def bc_mid(ap, n):
            return ap.unsqueeze(len(ap.shape) - 1).to_broadcast([*ap.shape[:-1], n, ap.shape[-1]])

        def dve_conv_acc(dve, link, l, i):
            dve.wait_ge(freer(l, "xbc", i), freed(l, "xbc", i))
            if 2 <= i < 8:
                dve.wait_ge(s("ct_full", l), count("ct_full", l, i - 1))
            acc = view(xsT[:, i % 2, :] if i < 8 else bcT[:, i - 8, :], 2, 256)
            src = view(raw[:, i % 3, :], 2, 256)
            w = view(Cl("conv_w"), 12, 5)
            link(dve.tensor_scalar(acc, src, w[:, i, 2:3], Cl("conv_b")[:, i:i + 1], ALU.mult, ALU.add))
            for tap in (0, 1, 3, 4):
                o_ = tap - 2
                a0, a1 = max(0, -o_), 256 - max(0, o_)
                ins = dve.scalar_tensor_tensor(out=acc[:, :, a0:a1], in0=src[:, :, a0 + o_:a1 + o_], scalar=w[:, i, tap:tap + 1],
                                               in1=acc[:, :, a0:a1], op0=ALU.mult, op1=ALU.add)
                if tap < 4:
                    link(ins)
            ins.then_inc(s("conv_acc", l), 1)

        def dve_ssd(dve, link, l):
            tiles = tiles_of(l)
            for t in range(TT):
                dve.wait_ge(stream_full, filled(l, "dt", t))
                bank = bank_of(l, "dt", t)
                dve.tensor_tensor(dt_raw[:, t, :], ps[:, bank, 0:32], Rw("dt_bias"), ALU.add).then_inc(free["dve"], 1)
            dve.wait_ge(freer(l, "dt", TT - 1), freed(l, "dt", TT - 1))
            dve.tensor_copy(rstd[:, 15:16], dt_raw[:, 0, 0:1]).then_inc(s("sp1", l), 1)
            dve.wait_ge(s("sp2", l), count("sp2", l, 1))
            link(dve.scalar_tensor_tensor(out=dt[:], in0=dt_raw[:], scalar=0.0, in1=dt[:], op0=ALU.max, op1=ALU.add))
            dve.scalar_tensor_tensor(out=da[:], in0=dt[:], scalar=-1.0, in1=bc_mid(neg_a[:], TT),
                                     op0=ALU.mult, op1=ALU.mult).then_inc(s("da_ready", l), 1)
            dve.wait_ge(s("cum_full", l), count("cum_full", l, 1))
            dve.tensor_copy(cums[:], view(ps[:, 4, 0:256], TT, 64)).then_inc(s("cum_ready", l), 1)
            dve.wait_ge(s("cum_ready", l), count("cum_ready", l, 1))
            dve.tensor_tensor(wd[:], cums[:, :, 32:64], cums[:, :, 0:32], ALU.subtract).then_inc(s("wd_pre", l), 1)
            dve.wait_ge(s("ecs_ready", l), count("ecs_ready", l, 1))
            dve.tensor_tensor(wd[:], wd[:], dt[:], ALU.mult).then_inc(s("w_ready", l), 1)

            def diff(q, t, k):
                kq = q * 8 + k
                h = (k // 4) * 16 + (k % 4) * 4
                d3 = view(dd[kq % 3], 4, P)
                if kq >= 3:
                    dve.wait_ge(s("m_ready", l), count("m_ready", l, kq - 2))
                dve.wait_ge(s("bc_full", l), count("bc_full", l, kq + 1))
                dve.tensor_tensor(d3, view(ps[:, SPREAD[kq % 3], :], 4, P), bc(cums[:, t, h:h + 4], P),
                                  ALU.subtract).then_inc(s("diff_done", l), 1)
                dve.wait_ge(s("diff_done", l), count("diff_done", l, kq + 1))
                dve.tensor_scalar(dd[kq % 3], dd[kq % 3], 0.0, None, ALU.min).then_inc(s("dm_ready", l), 1)

            def decay(q, t, k):
                kq = q * 8 + k
                dve.wait_ge(s("e_ready", l), count("e_ready", l, kq + 1))
                if kq >= 2:
                    dve.wait_ge(s("ymm_done", l), count("ymm_done", l, kq - 1))
                dve.tensor_tensor(view(mm[kq % 2], 4, P), view(dd[kq % 3], 4, P),
                                  bc_mid(cbm[:, k // 4, (k % 4) // 2, :], 4), ALU.mult).then_inc(s("m_ready", l), 1)
            def evacuate(q, t):
                dve.wait_ge(s("ymm_done", l), count("ymm_done", l, 8 * (q + 1)))
                dve.wait_ge(s("pool_x", l), count("pool_x", l, 3 * (q + 1)))
                for g in range(2):
                    part = ys[:, t, g * 512:(g + 1) * 512]
                    ins = dve.tensor_tensor(part, ps[:, 5 + g, :], part, ALU.add)
                ins.then_inc(s("y_evac", l), 1)
            dve.wait_ge(s("mod_saved", l), count("mod_saved", l, 16))
            if l == 0:
                dve.wait_ge(s("y_zero", 0), count("y_zero", 0, 16 * XTRA))
            for q, t in enumerate(tiles):
                dve.wait_ge(s("cb_full", l), count("cb_full", l, q + 1))
                cb = view(ps[:, 2, 0:256], 2, P)
                if q:
                    dve.wait_ge(s("m_ready", l), count("m_ready", l, 8 * q))
                dve.tensor_tensor(cbm[:, 0], cb, bc_mid(upper, 2), ALU.mult)
                dve.tensor_tensor(cbm[:, 1], cb, bc_mid(lower, 2), ALU.mult).then_inc(s("cbm_ready", l), 1)
                dve.wait_ge(s("cbm_ready", l), count("cbm_ready", l, q + 1))
                for k in range(8):
                    diff(q, t, k)
                    if k:
                        decay(q, t, k - 1)
                    elif q:
                        evacuate(q - 1, tiles[q - 1])
                decay(q, t, 7)
            evacuate(len(tiles) - 1, tiles[-1])
            dve.wait_ge(s("y_evac", l), count("y_evac", l, len(tiles)))
            n_inter = 0
            for k in range(4):
                for d in range(2):
                    b = ORDER[d][k]
                    if k and b in tiles:
                        n_inter += 1
                        dve.wait_ge(s("inter_full", l), count("inter_full", l, n_inter))
                        for g in range(2):
                            ins = dve.tensor_tensor(view(dd[g], 8, SP), view(ps[:, 2 + g, :], 8, SP),
                                                    bc(ecs[:, b, d * 16 + g * 8:d * 16 + g * 8 + 8], SP), ALU.mult)
                        ins.then_inc(s("inter_done", l), 1)
                        dve.wait_ge(s("inter_done", l), count("inter_done", l, n_inter))
                        for g in range(2):
                            part = ys[:, b, g * 512:(g + 1) * 512]
                            ins = dve.tensor_tensor(part, part, dd[g], ALU.add)
                        link(ins)
                    if k < 3:
                        dve.wait_ge(s("upd_full", l), count("upd_full", l, 2 * k + d + 1))
                        if k:
                            st = view(state[:, d, :], SH, SP)
                            link(dve.tensor_tensor(st, st, bc(ecs[:, b, 32 + d * 16:48 + d * 16], SP), ALU.mult))
                        for g in range(2):
                            part = state[:, d, g * 512:(g + 1) * 512]
                            if k:
                                ins = dve.tensor_tensor(part, ps[:, 5 + g, :], part, ALU.add)
                            else:
                                ins = dve.tensor_copy(part, ps[:, 5 + g, :])
                        ins.then_inc(s("s_ready", l), 1)
                        dve.wait_ge(s("s_ready", l), count("s_ready", l, 2 * k + d + 1))

        def dve_gla(dve, link, l):
            tiles = tiles_of(l)
            t0, n_t = tiles[0], len(tiles)
            dve.wait_ge(s("lg_full", l), count("lg_full", l, 1))
            for t in range(TT):
                ins = dve.tensor_tensor(gg[:, t, :], ps[:, 2 + t, :], Rw("gla_b2"), ALU.add)
            ins.then_inc(s("gabs", l), 1)
            flat = gg.rearrange("p a b -> p (a b)")
            kvf = kv.rearrange("p t a b c -> p (t a b c)")
            dve.wait_ge(s("gsp", l), count("gsp", l, 1))
            link(dve.scalar_tensor_tensor(out=flat, in0=flat, scalar=0.0, in1=kvf, op0=ALU.min, op1=ALU.subtract))
            dve.tensor_scalar(flat, flat, 1.0 / 16.0, None, ALU.mult).then_inc(s("g_ready", l), 1)
            for t in range(TT):
                dve.wait_ge(s("b_full", l), count("b_full", l, t + 1))
                b4 = ps[:, 6 + t % 2, :].rearrange("p (d f n) -> p d f n", d=2, f=2)
                for d in range(2):
                    mid, end = (P // 2 - 1, P - 1) if d == 0 else (P // 2, 0)
                    dve.tensor_copy(bmt[:, t, d, :, 0:1], b4[:, d, :, mid:mid + 1])
                    ins = dve.tensor_copy(bmt[:, t, d, :, 1:2], b4[:, d, :, end:end + 1])
                link(ins)
                if t:
                    dve.wait_ge(s("qkd_ready", l), count("qkd_ready", l, t))
                for d in range(2):
                    for f in range(2):
                        m = bmt[:, t, d, f, 0:1]
                        dve.tensor_scalar(eb[:, 0, d, f, :], b4[:, d, f, :], m, CLAMP, ALU.subtract, ALU.min)
                        ins = dve.tensor_scalar(eb[:, 1, d, f, :], b4[:, d, f, :], m, -CLAMP, ALU.subtract, ALU.max)
                ins.then_inc(s("b_done", l), 1)
                dve.wait_ge(s("eb_ready", l), count("eb_ready", l, t + 1))
                for d in range(2):
                    dve.tensor_tensor(qd[:, t * 2 + d], eb[:, 0, d], qkT[:, 0:2, t * P:(t + 1) * P], ALU.mult)
                    ins = dve.tensor_tensor(kd[:, t * 2 + d], eb[:, 1, d], qkT[:, 2:4, t * P:(t + 1) * P], ALU.mult)
                ins.then_inc(s("qkd_ready", l), 1)
                for n, index in z_groups(l, t):
                    dve.wait_ge(freer(l, "z", index), freed(l, "z", index))
                    b, tz = index
                    part = ys[:, tz, b * 512:(b + 1) * 512]
                    dve.tensor_tensor(part, part, zs[n % 2], ALU.mult).then_inc(s("yz_ready", l), 1)
                dve.wait_ge(s("kv_full", l), count("kv_full", l, t + 1))
                for d in range(2):
                    src = ps[:, 3 + d, :].rearrange("p (f e) -> p f e", f=2)
                    dve.tensor_copy(kv[0:64, t, d, :, :], src[0:64, :, 0:P])
                    ins = dve.tensor_copy(kv[64:128, t, d, :, :], src[64:128, :, P:2 * P])
                ins.then_inc(s("kv_done", l), 1)
            dve.tensor_tensor(btm[:], bmt[:, :, :, :, 1], bmt[:, :, :, :, 0], ALU.subtract).then_inc(s("btm_ready", l), 1)
            dve.wait_ge(s("bme_ready", l), count("bme_ready", l, 1))
            dve.wait_ge(s("kv_done", l), count("kv_done", l, TT))
            for d in range(2):
                S_ = gs[:, 2 * d:2 * d + 2, :]
                for k in range(4):
                    t = ORDER[d][k]
                    if k:
                        link(dve.tensor_tensor(sp[:, t * 2 + d], S_, bc(bme[:, t, d, :, 0], P), ALU.mult))
                    if k < 3:
                        link(dve.tensor_tensor(kv[:, t, d], kv[:, t, d], bc(btm[:, t, d, :], P), ALU.mult))
                        if k:
                            link(dve.tensor_tensor(S_, S_, bc(bme[:, t, d, :, 1], P), ALU.mult))
                            link(dve.tensor_tensor(S_, S_, kv[:, t, d], ALU.add))
                        else:
                            link(dve.tensor_copy(S_, kv[:, t, d]))
            dve.tensor_copy(gs[:, 0, 0:1], gs[:, 0, 0:1]).then_inc(s("sp_ready", l), 1)
            for q, t in enumerate(tiles):
                dve.wait_ge(s("sc_full", l), count("sc_full", l, q + 1))
                if q:
                    dve.wait_ge(s("gy_full", l), count("gy_full", l, q))
                for d in range(2):
                    bank = (2, 6)[q % 2]
                    for odd in range(2):
                        ins = dve.tensor_tensor(pm[d][:, odd::2, :],
                                                view(ps[:, bank + odd, d * 256:(d + 1) * 256], 2, P),
                                                bc_mid(tri[d], 2), ALU.mult)
                    ins.then_inc(s("p_ready", l), 1)

        def dve_att(dve, link, l):
            tiles = tiles_of(l)
            dve.wait_ge(s("gy_full", l), count("gy_full", l, len(tiles)))
            dve.wait_ge(freer(l, "attkv", TT - 1), freed(l, "attkv", TT - 1))

            def heads(t):
                lo = 0 if t in tiles else 8
                return lo, 10 - lo
            for t in range(TT):
                lo, n = heads(t)
                x3 = view(att[:, t, lo * 64:640], n, 64)
                r3 = view(rt[:, 0:n * 64], n, 64)
                link(dve.tensor_tensor(r3, x3, x3, ALU.mult))
                link(dve.tensor_reduce(ass[:, t, lo:10], r3, AX.X, ALU.add))
            dve.tensor_copy(rt[:, 0:1], rt[:, 0:1]).then_inc(s("ass_ready", l), 1)
            dve.wait_ge(s("gsq", l), count("gsq", l, 1))
            t0, n_t = tiles[0], len(tiles)
            dve.tensor_reduce(gss[:, t0:, :], view(qd.rearrange("p a b c -> p (a b c)")[:, t0 * 512:], n_t, 4, P), AX.X, ALU.add)\
                .then_inc(s("gss_ready", l), 1)
            dve.wait_ge(s("ar_ready", l), count("ar_ready", l, 1))
            for t in range(TT):
                lo, n = heads(t)
                x3 = view(att[:, t, lo * 64:640], n, 64)
                link(dve.tensor_tensor(x3, x3, bc(ass[:, t, lo:10], 64), ALU.mult))
                if lo == 0:
                    x8 = view(att[:, t, 0:512], 8, 64)
                    link(dve.tensor_tensor(x8, x8, bc_mid(Rw("q_norm"), 8), ALU.mult))
                k2 = view(att[:, t, 512:640], 2, 64)
                link(dve.tensor_tensor(k2, k2, bc_mid(Rw("k_norm"), 2), ALU.mult))
                if t >= 2:
                    cos = view(K("cos"), 2, 64)[:, t - 2, :]
                    sin = view(K("sin"), 2, 2, 2, 16)[:, t - 2]
                    r3 = view(rt[:, 0:n * 64], n, 64)
                    link(dve.tensor_tensor(r3, x3, bc_mid(cos, n), ALU.mult))
                    x5 = att[:, t, lo * 64:640].rearrange("p (h a c e) -> p h a c e", a=2, c=2, e=16)
                    u5 = ru[:, 0:n * 64].rearrange("p (h a c e) -> p h a c e", a=2, c=2, e=16)
                    for c in range(2):
                        sn = sin[:, :, c, :].unsqueeze(1).to_broadcast([P, n, 2, 16])
                        link(dve.tensor_tensor(u5[:, :, :, c, :], x5[:, :, :, 1 - c, :], sn, ALU.mult))
                    link(dve.tensor_tensor(x3, r3, view(ru[:, 0:n * 64], n, 64), ALU.add))
                dve.tensor_copy(kdup[:, t, :, 0, :], k2)
                dve.tensor_copy(kdup[:, t, :, 1, :], k2).then_inc(s("att_prep", l), 1)
            seq = [(q, t, h) for q, t in enumerate(tiles) for h in range(8)]

            def collect(q, t):
                dve.wait_ge(s("o_full", l), count("o_full", l, q * 8 + 8))
                dve.tensor_copy(att[:, t, 0:512], ps[:, 2 + q % 2, :]).then_inc(s("o_raw", l), 1)
            for n, (q, t, h) in enumerate(seq):
                w = CTX if t < 2 else TOK
                dve.wait_ge(s("s_full", l), count("s_full", l, n + 1))
                link(dve.tensor_reduce(nmax[:, n:n + 1], ps[:, 4 + n % 2, 0:w], AX.X, ALU.max))
                dve.tensor_scalar(nmax[:, n:n + 1], nmax[:, n:n + 1], -0.125, neg_sink[:, h:h + 1],
                                  ALU.mult, ALU.min).then_inc(s("nmax_ready", l), 1)
                if h == 4 and q:
                    collect(q - 1, tiles[q - 1])
            collect(len(tiles) - 1, tiles[-1])
            n_t = len(tiles)
            dve.wait_ge(s("p_exp", l), count("p_exp", l, 8 * n_t))
            v = view(nmax[:, 0:8 * n_t], n_t, 8)
            dve.tensor_tensor(v, v, bc_mid(Rw("sink"), n_t), ALU.add).then_inc(s("sink_pre", l), 1)
            dve.wait_ge(s("sink_exp", l), count("sink_exp", l, 1))
            rs = rsum[:, 0:8 * n_t]
            link(dve.tensor_tensor(rs, rs, nmax[:, 0:8 * n_t], ALU.add))
            link(dve.reciprocal(rs, rs))
            dve.wait_ge(s("o_raw", l), count("o_raw", l, n_t))
            for q, t in enumerate(tiles):
                o8 = view(att[:, t, 0:512], 8, 64)
                dve.tensor_tensor(o8, o8, bc(rs[:, q * 8:q * 8 + 8], 64), ALU.mult).then_inc(s("o_done", l), 1)

        def dve_merge(dve, link, l):
            tiles = tiles_of(l)
            for n in range(1, 4 * len(tiles), 2):
                _, f = y_source(tiles[n // 4], n % 4)
                t = tiles[n // 4]
                dve.wait_ge(s("yt_full", l), count("yt_full", l, n + 1))
                dve.tensor_copy(yT[:, f:f + 4, t * P:(t + 1) * P], view(ps[:, 2 + n % 4, :], 4, P))\
                    .then_inc(s("yt_dve", l), 1)
            a, b = span_of(l)
            w = b - a
            for j in range(3):
                for i in range(KO):
                    e = gate_e[(j * KO + i) % 2][:, 0:w]
                    dve.wait_ge(freer(l, "gate", (j, i)), freed(l, "gate", (j, i)))
                    dve.wait_ge(stream_full, filled(l, "prod", (j, i)))
                    bank = bank_of(l, "prod", (j, i))
                    dst = merged[:, i, a:b]
                    dve.tensor_tensor(dst if j == 0 else e, ps[:, bank, 0:w], e, ALU.mult).then_inc(free["dve"], 1)
                    dve.wait_ge(freer(l, "prod", (j, i)), freed(l, "prod", (j, i)))
                    if j:
                        dve.tensor_tensor(dst, dst, e, ALU.add).then_inc(s("merge_acc", l), 1)
                        dve.wait_ge(s("merge_acc", l), count("merge_acc", l, (j - 1) * KO + i + 1))
            dve.tensor_copy(gate_e[0][:, 0:1], merged[:, 0, a:a + 1]).then_inc(s("merged", l), 1)
            dve.wait_ge(s("merged", l), count("merged", l, 1))
            dve.wait_ge(s("x_again", l), count("x_again", l, 16 * (len(tiles) + 2)))
            n = 0
            for half in range(2):
                for t in tiles:
                    c = 0 if t < 2 else 1
                    e = gate_e[n % 2]
                    n += 1
                    dve.wait_ge(stream_full, filled(l, "out", (half, t)))
                    bank = bank_of(l, "out", (half, t))
                    cols_ = slice(half * 512, (half + 1) * 512)
                    dve.tensor_tensor(e, ps[:, bank, :], gate_bc[:, c, cols_], ALU.mult).then_inc(free["dve"], 1)
                    dve.wait_ge(freer(l, "out", (half, t)), freed(l, "out", (half, t)))
                    ins = dve.tensor_tensor(xb[:, t, cols_], xb[:, t, cols_], e, ALU.add)
                    if n < 2 * len(tiles):
                        link(ins)
            ins.then_inc(s("x_new", l), 1)
            dve.wait_ge(s("x_new", l), count("x_new", l, 1))

        def dve_route(dve, link, l):
            tiles = tiles_of(l)
            t0, n_t = tiles[0], len(tiles)

            def quads(ap):
                return ap[:, t0:, :].rearrange("p t (g j) -> p (t g) j", j=4)

            def flat(ap):
                return ap[:, t0:, :].rearrange("p t g -> p (t g)")

            def first_of(dst, src, top, tmp, idx):
                r4 = K("rank4").unsqueeze(1).to_broadcast([P, src.shape[1], 4])
                link(dve.tensor_tensor(tmp, src, bc(top, 4), ALU.is_equal))
                link(dve.tensor_tensor(tmp, tmp, r4, ALU.mult))
                link(dve.tensor_reduce(idx, tmp, AX.X, ALU.max))
                link(dve.tensor_tensor(dst, tmp, bc(idx, 4), ALU.is_equal))
            dve.wait_ge(s("logit_exp", l), count("logit_exp", l, 1))
            sc_ = sc[:, t0:, :]
            link(dve.tensor_scalar(sc_, sc_, 1.0, None, ALU.add))
            link(dve.reciprocal(sc_, sc_))
            link(dve.tensor_tensor(bi[:, t0:, :], sc_, bc_mid(Rw("router_b"), n_t), ALU.add))
            q, tmp = quads(bi), quads(over)
            idx = off[:, 0:n_t * 4]
            link(dve.tensor_reduce(flat(m1), q, AX.X, ALU.max))
            first_of(quads(oh[0]), q, flat(m1), tmp, idx)
            link(dve.scalar_tensor_tensor(out=q, in0=quads(oh[0]), scalar=-BIG, in1=q, op0=ALU.mult, op1=ALU.add))
            link(dve.tensor_reduce(flat(m2), q, AX.X, ALU.max))
            first_of(quads(oh[1]), q, flat(m2), tmp, idx)
            link(dve.tensor_tensor(flat(gsc), flat(m1), flat(m2), ALU.add))
            link(dve.tensor_reduce(gmax[:, t0:], gsc[:, t0:, :], AX.X, ALU.max))
            first_of(gsel[:, t0:, :], gsc[:, t0:, :], gmax[:, t0:], rank[:, t0:, 0:4], cnt[:, 0:n_t])
            for c in range(2):
                link(dve.tensor_tensor(quads(oh[c]), quads(oh[c]), bc(flat(gsel), 4), ALU.mult))
            dve.tensor_tensor(t16[:, t0:, :], oh[0][:, t0:, :], oh[1][:, t0:, :], ALU.add).then_inc(s("assigned", l), 1)
            for c in range(2):
                link(dve.tensor_tensor(over[:, t0:, :], oh[c][:, t0:, :], sc_, ALU.mult))
                link(dve.tensor_reduce(gates[:, c, t0:], over[:, t0:, :], AX.X, ALU.add))
            link(dve.tensor_tensor(gmax[:, t0:], gates[:, 0, t0:], gates[:, 1, t0:], ALU.add))
            link(dve.reciprocal(gmax[:, t0:], gmax[:, t0:]))
            for c in range(2):
                link(dve.tensor_tensor(gates[:, c, t0:], gates[:, c, t0:], gmax[:, t0:], ALU.mult))
            dve.wait_ge(s("rank_full", l), count("rank_full", l, 1))
            dve.tensor_copy(cnt[:], ps[:, 6, 64:64 + NE])
            link(dve.tensor_copy(rank[:, t0:, :], view(ps[:, 6, t0 * NE:TT * NE], n_t, NE)))
            link(dve.tensor_scalar(xtr[:], cnt[:], float(P), None, ALU.is_gt))
            for m in range(2, TOK // P):
                link(dve.tensor_scalar(incl[:], cnt[:], float(P * m), None, ALU.is_gt))
                link(dve.tensor_tensor(xtr[:], xtr[:], incl[:], ALU.add))
            link(dve.tensor_copy(incl[:], xtr[:]))
            a, b = incl, scan_t
            for sh in (1, 2, 4, 8):
                dve.tensor_copy(b[:, 0:sh], a[:, 0:sh])
                link(dve.tensor_tensor(b[:, sh:NE], a[:, sh:NE], a[:, 0:NE - sh], ALU.add))
                a, b = b, a
            link(dve.tensor_tensor(off[:], a[:], xtr[:], ALU.subtract))
            link(dve.tensor_scalar(off[:], off[:], float(P), float(NE * P - P), ALU.mult, ALU.add))
            link(dve.tensor_tensor(off[:], off[:], K("first_slot"), ALU.subtract))
            link(dve.tensor_scalar(over[:, t0:, :], rank[:, t0:, :], float(P), None, ALU.is_ge))
            link(dve.tensor_tensor(over[:, t0:, :], over[:, t0:, :], bc_mid(off[:], n_t), ALU.mult))
            link(dve.tensor_tensor(rank[:, t0:, :], rank[:, t0:, :], over[:, t0:, :], ALU.add))
            link(dve.tensor_tensor(rank[:, t0:, :], rank[:, t0:, :], bc_mid(K("first_slot"), n_t), ALU.add))
            for c in range(2):
                link(dve.tensor_tensor(over[:, t0:, :], oh[c][:, t0:, :], rank[:, t0:, :], ALU.mult))
                link(dve.tensor_reduce(slotf[:, c, t0:], over[:, t0:, :], AX.X, ALU.add))
                link(dve.tensor_copy(slot_idx[:, c * TT + t0:(c + 1) * TT], slotf[:, c, t0:]))
            link(dve.tensor_tensor(blk[:], a[:].unsqueeze(1).to_broadcast([P, 8, NE]), bc(K("block"), NE), ALU.is_le))
            link(dve.tensor_reduce(blkf[:], blk[:], AX.X, ALU.add))
            link(dve.tensor_scalar(blkf[:], blkf[:], float(NE - 1), None, ALU.min))
            dve.tensor_copy(extra[:, 0:8], blkf[:])
            dve.tensor_copy(extra[:, 8:9], a[:, NE - 1:NE]).then_inc(s("route_ready", l), 1)

        def dve_experts(dve, link, l):
            def take_x(i):
                dve.wait_ge(s("xt_full", l), count("xt_full", l, i + 1))
                dve.tensor_copy(hflat[:, 1024:1536], ps[:, 0, :])
                dve.tensor_copy(hflat[:, 1536:2048], ps[:, 1, :]).then_inc(s("xt_ready", l), 1)

            def hidden(i, half):
                dve.wait_ge(s("silu_ready", l), count("silu_ready", l, i * 2 + half + 1))
                if not first(i):
                    dve.wait_ge(s("ht_full", l), count("ht_full", l, i * 2))
                dve.tensor_tensor(hid[:, half * 512:(half + 1) * 512], ps[:, 3 + 2 * half, :], silu_h[half], ALU.mult)\
                    .then_inc(s("hid_ready", l), 1)

            def block(i):
                hidden(i, 0)
                hidden(i, 1)
                take_x(i + 1)
            dve.wait_ge(s("rows_full", l), count("rows_full", l, 2 * len(tiles_of(l))))
            take_x(0)
            block(0)
            with dve.Fori(1, NE) as i:
                block(i)
            n_extra = dve.value_load(extra[0:1, 8:9], min_val=0, max_val=XTRA)
            for j in range(extra_blocks(l)):
                with dve.If(n_extra > j):
                    block(NE + j)

        def dve_layer(dve, link, l):
            tiles = tiles_of(l)
            if l == 0:
                dve.wait_ge(cond_exp, 1)
                link(dve.tensor_scalar(cond_e[:], cond_e[:], 1.0, None, ALU.add))
                link(dve.reciprocal(cond_e[:], cond_e[:]))
                dve.tensor_tensor(cond[:], cond[:], cond_e[:], ALU.mult).then_inc(cond_ready, 1)
            dve.wait_ge(s("small_in", l), count("small_in", l, 80))
            dve.tensor_scalar(neg_sink[:], Rw("sink"), -1.0, None, ALU.mult).then_inc(s("neg_ready", l), 1)
            for c in range(12):
                dve.wait_ge(stream_full, filled(l, "mod", c))
                bank = bank_of(l, "mod", c)
                part = modr[0:2, c * 512:(c + 1) * 512]
                dve.tensor_tensor(part, ps[0:2, bank, :], part, ALU.add).then_inc(free["dve"], 1)
            dve.wait_ge(s("modT_full", l), count("modT_full", l, 1))
            link(dve.tensor_copy(modc[:], ps[:, 6, 0:64].rearrange("p (v k c) -> p v k c", v=4, k=KO)))
            for m in range(2):
                link(dve.scalar_tensor_tensor(out=scale_a[:, m], in0=modc[:, 2 * m + 1], scalar=1.0,
                                              in1=bc(Cl("norm1" if m == 0 else "norm2"), 2), op0=ALU.add, op1=ALU.mult))
            dve_norm(dve, l, 1, range(TT))
            for i in range(12):
                dve_conv_acc(dve, link, l, i)
            dve_ssd(dve, link, l)
            dve_gla(dve, link, l)
            dve_att(dve, link, l)
            dve_merge(dve, link, l)
            dve_norm(dve, l, 2, tiles)
            dve_route(dve, link, l)
            dve_experts(dve, link, l)
            dve.wait_ge(s("y_got", l), count("y_got", l, 16 * (2 * len(tiles) + 3)))
            for t in tiles:
                c = 0 if t < 2 else 1
                y0, y1 = yr[:, t, 0, :], yr[:, t, 1, :]
                link(dve.tensor_scalar(y0, y0, gates[:, 0, t:t + 1], None, ALU.mult))
                link(dve.scalar_tensor_tensor(out=y0, in0=y1, scalar=gates[:, 1, t:t + 1], in1=y0, op0=ALU.mult, op1=ALU.add))
                link(dve.tensor_tensor(y0, y0, gate_bc[:, c, :], ALU.mult))
                link(dve.tensor_tensor(xb[:, t, :], xb[:, t, :], y0, ALU.add))
            dve.tensor_copy(rstd[:, 0:1], xb[:, tiles[0], 0:1]).then_inc(s("layer_done", l), 1)

        block = ctx.enter_context(nc.Block())

        @block.sync
        def _(sp):
            for l in range(NL):
                sp_stream(sp, l)
                sp_experts(sp, l)
            sp.wait_ge(s("layer_done", NL - 1), count("layer_done", NL - 1, 1))
            sp.dma_start(out[0].rearrange("(t p) d -> p t d", p=P), xb[:, 2:, :]).then_inc(s("out_saved", 0), 16)
            sp.wait_ge(s("out_saved", 0), count("out_saved", 0, 16))

        @block.gpsimd
        def _(pool):
            link = Chain(pool, "pool")
            for l in range(NL):
                pool_layer(pool, link, l)

        @block.tensor
        def _(pe):
            for l in range(NL):
                if l:
                    pe.wait_ge(s("layer_done", l - 1), count("layer_done", l - 1, 1))
                pe_layer(pe, l)

        @block.scalar
        def _(act):
            nonlocal alink
            alink = Chain(act, "act")
            for l in range(NL):
                act_layer(act, l)

        @block.vector
        def _(dve):
            link = Chain(dve, "dve")
            for l in range(NL):
                dve_layer(dve, link, l)


def pack(inputs):
    a = {k: np.ascontiguousarray(v) for k, v in inputs.items()}
    got = {k: a[k] for k in ("x", "ctx", "w_mod", "b_mod", "w_in", "gla_w2", "w_br_a", "w_br_b", "w_br_c", "w_out",
                             "router_w", "w1", "w3", "w2")}
    got["consts"] = const_pack()
    c = np.stack([a["c_ctx"], a["c"][0]])
    got["cond"] = c.reshape(2, KO, P).transpose(2, 1, 0)
    rows = [a["q_norm_g"], a["k_norm_g"], a["gla_norm_g"], a["ssd_norm_g"], a["ssd_dt_bias"].reshape(NL, 32),
            a["ssd_a_log"].reshape(NL, 32), a["ssd_d"], a["att_sink"], a["gla_b2"].reshape(NL, 512),
            np.tile(a["router_b"], (NL, 1))]
    got["rows"] = np.concatenate(rows, 1)
    conv_w = a["ssd_conv_w"].reshape(NL, 5, 12, P).transpose(0, 3, 2, 1).reshape(NL, P, 60)
    cols = [a["norm1_g"].reshape(NL, 8, P).transpose(0, 2, 1), a["norm2_g"].reshape(NL, 8, P).transpose(0, 2, 1), conv_w,
            a["ssd_conv_b"].reshape(NL, 12, P).transpose(0, 2, 1), a["gate_b"].reshape(NL, 24, P).transpose(0, 2, 1)]
    got["cols"] = np.concatenate(cols, 2)
    return {k: np.ascontiguousarray(v) for k, v in got.items()}


def kernel(**inputs):
    import concourse.bacc as _bacc
    from concourse.bass_utils import run_bass_kernel_spmd as _run

    nc = _bacc.Bacc("TRN2", target_bir_lowering=False, num_devices=1)
    arrays, I = {}, {}
    for name, a in pack(inputs).items():
        arrays[f"in_{name}"] = a
        I[name] = nc.dram_tensor(f"in_{name}", a.shape, mybir.dt.from_np(a.dtype), kind="ExternalInput").ap()
    out = nc.dram_tensor("out_x", (1, LAT, D), F32, kind="ExternalOutput").ap()
    build(nc, I, out)
    r = _run(nc, [arrays], core_ids=[0])
    return r.results[0]["out_x"]
```

```python
import numpy as np
import concourse.bass as bass
from concourse import mybir
from contextlib import ExitStack

F32 = mybir.dt.float32
I32 = mybir.dt.int32
U32 = mybir.dt.uint32
ALU = mybir.AluOpType
ACT = mybir.ActivationFunctionType
AX = mybir.AxisListType

P = 128
D = 1024
KO = D // P
CTX, LAT = 256, 256
TOK = CTX + LAT
TT = TOK // P
NL = 2
NMOD = 6
EPS = 1e-6
NE, NG, EPG = 16, 4, 4
FF = 1024
CLAMP = 40.0
BIG = 1e30
XTRA = 7
SLOTS = (NE + XTRA) * P

C_GQ, C_GK, C_GV, C_GR, C_GF, C_GB = 0, 256, 512, 1024, 1536, 1552
C_AQ, C_AK, C_Z, C_XBC, C_DT, C_MG = 1568, 2080, 2336, 3360, 4896, 4928
N_IN = 8000
QH, HD = 8, 64
SH, SP = 16, 64

CONST = {}


def const_pack():
    s, t = np.arange(P)[:, None], np.arange(P)[None, :]
    parts = {
        "ident": s == t, "upper": s <= t, "lower": s >= t, "strict": s < t, "ones": np.ones((P, P)),
    }
    window = np.zeros((P, 2, 256), np.float32)
    for b in range(2):
        far = np.abs(np.arange(256)[None, :] - (b * P + np.arange(P)[:, None])) > 128
        window[:, b] = np.where(far, -BIG, 0.0)
    parts["window"] = window.reshape(P, -1)
    pos = np.arange(LAT)
    inv = (10000.0 ** (-np.arange(0, 32, 2, dtype=np.float32) / 32)).astype(np.float32)
    row = (pos // 64).astype(np.float32)[:, None] * inv
    col = (pos % 64).astype(np.float32)[:, None] * inv
    cos = np.concatenate([np.cos(row), np.cos(row), np.cos(col), np.cos(col)], 1)
    sin = np.concatenate([-np.sin(row), np.sin(row), -np.sin(col), np.sin(col)], 1)
    parts["cos"] = cos.reshape(2, P, 64).transpose(1, 0, 2).reshape(P, -1)
    parts["sin"] = sin.reshape(2, P, 64).transpose(1, 0, 2).reshape(P, -1)
    parts["token"] = np.arange(P)[:, None] + P * np.arange(TT)[None, :]
    parts["first_slot"] = np.tile(np.arange(NE) * P, (P, 1))
    parts["block"] = np.tile(np.arange(8), (P, 1))
    parts["rank4"] = np.tile(4 - np.arange(4), (P, 1))
    at = 0
    cols = []
    for k, v in parts.items():
        v = np.asarray(v, np.float32)
        CONST[k] = (at, v.shape[1])
        at += v.shape[1]
        cols.append(v)
    return np.concatenate(cols, 1)


NCONST = const_pack().shape[1]

ROWS = {}
_at = 0
for _k, _n in (("q_norm", 64), ("k_norm", 64), ("gla_norm", 128), ("ssd_norm", 1024), ("dt_bias", 32),
               ("a_log", 32), ("ssd_d", 16), ("sink", 8), ("gla_b2", 512), ("router_b", 16)):
    ROWS[_k] = (_at, _n)
    _at += _n
NROWS = _at
COLS = {"norm1": (0, 8), "norm2": (8, 8), "conv_w": (16, 60), "conv_b": (76, 12), "gate_b": (88, 24)}
NCOLS = 112
RING = 4
SLOT_W = 512
EARLY = 8
NSTREAM = 2


def early_mods(n):
    return range(2 * n, 2 * n + 2) if n < EARLY // 2 else range(0)


def plan_layer(l):
    act, dve = "act", "dve"
    tiles = list(range(TT)) if l < NL - 1 else [2, 3]
    out = [(("mod", c, 0), [("mod", c, dve)]) for c in range(12)] if l == 0 else []
    for b in range(3):
        groups = [("xbc", b * 4 + i, act) for i in range(4)]
        out.append((("xbc", b), groups))
    out.append((("dt", 0), [("dt", t, dve) for t in range(TT)]))
    out.append((("qk", 0), [("qk", i, act) for i in range(4)]))
    out.append((("gates", 0), [("gates", 0, act)]))
    out.append((("v", 0), [("v", t, act) for t in range(TT)]))
    out.append((("attq", 0), [("attq", t, act) for t in tiles]))
    out.append((("attkv", 0), [("attkv", t, act) for t in range(TT)]))
    for b in range(2):
        out.append((("z", b), [("z", (b, t), act) for t in tiles]))
    out.append((("r", 0), [("r", t, act) for t in tiles]))
    for j in range(3):
        for half in range(2):
            pairs = []
            for i in range(4):
                pairs += [("gate", (j, half * 4 + i), act), ("prod", (j, half * 4 + i), dve)]
            out.append((("pair", j, half), pairs))
            if l < NL - 1:
                out += [(("mod", c, l + 1), [("mod", c, dve)]) for c in early_mods(2 * j + half)]
    out.append((("outs", 0), [("out", (half, t), dve) for t in tiles for half in range(2)]))
    if l < NL - 1:
        out += [(("mod", c, l + 1), [("mod", c, dve)]) for c in range(EARLY, 12)]
    return tiles, out


def plan():
    loads, groups, find = [], [], {}
    ordinal = {"act": 0, "dve": 0}
    for l in range(NL):
        for block, served in plan_layer(l)[1]:
            kinds = [block]
            if block[0] == "pair":
                _, j, half = block
                kinds = [("mg", j, half), ("wbr", j, half)]
            elif block[0] == "outs":
                kinds = [("out", 0), ("out", 1)]
            owner = block[2] if block[0] == "mod" else l
            first = len(loads)
            for k in kinds:
                loads.append({"layer": l, "owner": owner, "block": k, "slot": len(loads) % RING})
            for kind, index, engine in served:
                n = len(groups)
                ordinal[engine] += 1
                need = first + (1 if kind == "prod" or (kind == "out" and index[0]) else 0)
                groups.append({"layer": owner, "kind": kind, "index": index, "engine": engine,
                               "ordinal": ordinal[engine], "bank": n % NSTREAM, "load": need, "number": n})
                find[(owner, kind, index)] = n
                loads[need]["last"] = n
    return loads, groups, find


EXPERT_SEMS = ("up_full", "down_full", "gathered", "xt_full", "xt_ready", "stored", "hid_ready",
               "ht_full", "ht_ready", "ob_done", "silu_ready")
STEPS = {
    "pool_step": "branches_final",
    "pe_step": "modT_full cum_full lg_full logit_full rank_full",
    "act_step": "sp2 ecs_ready gsp ar_ready bme_ready gsq branch_rs sink_exp logit_exp all_stored",
    "dve_step": "modc_ready neg_ready sp1 da_ready cum_ready wd_pre w_ready gabs ass_ready g_ready btm_ready sp_ready "
                "gss_ready sink_pre merged assigned route_ready",
}
NORMS = {"ss": TT, "rs": TT, "xn": TT, "tr": TT, "hT": TT}
SHARED = {n: (sem, i) for sem, names in STEPS.items() for i, n in enumerate(names.split())}
SHARED.update({f"{n}{which}": (n, first * (which - 1)) for n, first in NORMS.items() for which in (1, 2)})
FIRST_LAYER = {"x_in": 0, "zeroed": 0, "y_zero": 0, "eps_set": 0, "tok_id": 0, "xd_saved": 0, "out_saved": 0,
               "small_in": 16 * 3, "cols_in": 16, "bias_in": 64, "mod_saved": 64, "tok_zero": 16, "x_saved": 16, "row_saved": 16, "tok_got": 16,
               "x_again": 16 * (TT + 2), "tok_put": 16 * 2 * TT, "y_first": 16 * TT, "y_rest": 16 * TT, "rest_in": 48,
               "merge_acc": 2 * KO, "x_tile": TT, "x_final": TT, "conv_acc": 12, "conv_done": 12, "ct_full": 10, "ct_done": 10,
               "pool_x": 3 * TT, "wx_ready": 6, "upd_full": 6, "s_ready": 6, "inter_full": 6, "inter_done": 6, "yt_full": 4 * TT}
FIRST_LAYER.update({sem: len(names.split()) for sem, names in STEPS.items()})
FIRST_LAYER.update({n: 2 * first for n, first in NORMS.items()})
for _names, _n in (
        ("cb_full cbm_ready y_evac b_full b_done kdt_full "
         "kdt_ready kv_full kv_done eb_ready qkd_ready sc_full gy_full gy_done qk_full qk_turned att_prep o_raw o_done", TT),
        ("p_ready yz_ready yt_act yt_dve rows_full row_ready", 2 * TT),
        ("bc_full diff_done dm_ready e_ready m_ready ymm_done s_full nmax_ready p_exp pt_full pt_ready o_full", 8 * TT)):
    FIRST_LAYER.update(dict.fromkeys(_names.split(), _n))


def build(nc, I, out):
    loads, groups, find = plan()
    with ExitStack() as ctx:
        def sb(name, shape, dt=F32):
            return ctx.enter_context(nc.sbuf_tensor(name, shape, dt))

        def sem(name):
            return ctx.enter_context(nc.semaphore(name))

        consts = sb("consts", [P, NCONST])
        rows = sb("rows", [P, NROWS])
        cols = sb("cols", [P, NCOLS])
        router_w = sb("router_w", [P, KO, NE])
        gate_w2 = sb("gate_w2", [16, 512])
        eps_t = sb("eps_t", [P, 1])
        cond = sb("cond", [P, KO, 2])
        modc = sb("modc", [P, 4, KO, 2])
        scale_a = sb("scale_a", [P, 2, KO, 2])
        neg_sink = sb("neg_sink", [P, 8])
        neg_a = sb("neg_a", [P, 32])
        sumsq = sb("sumsq", [P, 16])
        rstd = sb("rstd", [P, 16])
        hT = sb("hT", [P, KO, TOK])
        xb = sb("xb", [P, TT, D])
        ring = sb("ring", [P, RING, KO, SLOT_W])
        small = sb("small", [P, 1408])
        slot_idx = sb("slot_idx", [P, 2 * TT], U32)
        tok_idx = sb("tok_idx", [P, NE + XTRA + 1], U32)
        tok_id = sb("tok_id", [P, TT], U32)
        zero_idx = sb("zero_idx", [P, NE + XTRA + 1], U32)
        extra = sb("extra", [P, 16], I32)
        arena = sb("arena", [P, 22528])
        ps = ctx.enter_context(nc.psum_tensor("ps", [P, 8, 512], F32))

        x_dram = nc.dram_tensor("x_scratch", (TOK, D), F32).ap()
        mod_dram = nc.dram_tensor("mod_scratch", (NL, 2, NMOD * D), F32).ap()
        h_dram = nc.dram_tensor("h_scratch", (TOK, D), F32).ap()
        tok_dram = nc.dram_tensor("tok_scratch", ((NE + XTRA + 1) * P, 1), U32).ap()
        y_dram = nc.dram_tensor("y_scratch", (SLOTS, D), F32).ap()

        def K(name):
            at, n = CONST[name]
            return consts[:, at:at + n]

        def Rw(name):
            at, n = ROWS[name]
            return rows[:, at:at + n]

        def Cl(name):
            at, n = COLS[name]
            return cols[:, at:at + n]

        def region(at, *shape):
            n = int(np.prod(shape))
            v = arena[:, at:at + n]
            names = "abcd"[:len(shape)]
            if len(shape) == 1:
                return v
            spec = "p (" + " ".join(names) + ") -> p " + " ".join(names)
            return v.rearrange(spec, **dict(zip(names, shape)))

        def view(ap, *shape):
            names = "abcd"[:len(shape)]
            spec = "p (" + " ".join(names) + ") -> p " + " ".join(names)
            return ap.rearrange(spec, **dict(zip(names, shape)))

        ident, upper, lower, ones = K("ident"), K("upper"), K("lower"), K("ones")
        tri = [upper, lower]
        qkT = region(0, 4, TOK)
        gv = region(2048, TT, 512)
        gT = region(4096, 2, TOK)
        att = region(5120, TT, 768)
        ys = region(8192, TT, 1024)
        yg = region(12288, TT, 512)
        mod_rows = [region(10240, 12, P)] + [view(rows[:, 0:12 * P], 12, P)] * (NL - 1)
        bcT = region(14336, 4, TOK)
        b_tm = region(16384, TT, 256)
        TMP = 17408
        xn = region(TMP, TT, D)
        junk = region(TMP + 4096, D)
        raw = region(TMP, 3, TOK)
        xsT = region(TMP + 1536, 2, TOK)
        xs = xb
        xw = [[region(TMP + i * 2048 + d * 1024, 1024) for d in range(2)] for i in range(2)]
        state = region(TMP + 2048, 2, 1024)
        cbm = region(TMP + 4096, 2, 2, P)
        dd = [region(12288, 512), region(12800, 512), region(TMP + 4608, 512)]
        mm = [region(13312 + i * 512, 512) for i in range(2)]
        o = [0]

        def sm(*shape):
            n = int(np.prod(shape))
            v = small[:, o[0]:o[0] + n]
            o[0] += n
            return v if len(shape) == 1 else view(v, *shape)

        dt_raw = sm(TT, 32)
        dt = sm(TT, 32)
        da = sm(TT, 32)
        cums = sm(TT, 64)
        ecs = sm(TT, 64)
        wd = sm(TT, 32)
        zs = [region(4096 + i * 512, 512) for i in range(2)]
        gg = view(xb[:, 0:2, :].rearrange("p a b -> p (a b)"), TT, 512)
        kv = view(xb[:, 2:4, :].rearrange("p a b -> p (a b)"), TT, 2, 2, P)
        qd = region(14336, TT * 2, 2, P)
        kd = region(16384, TT * 2, 2, P)
        sp = region(18432, TT * 2, 2, P)
        eb = region(20480, 2, 2, 2, P)
        pm = [region(21504, 4, P), region(22016, 4, P)]
        kdT = region(21504, 4, P)
        gs = region(20480, 4, P)
        bmt = sm(TT, 2, 2, 2)
        bme = sm(TT, 2, 2, 2)
        btm = sm(TT, 2, 2)
        gss = sm(TT, 4)
        qT = region(14336, 4, TOK)
        kT2 = region(16384, 2, TOK)
        pb = [region(17408 + i * 512, 512) for i in range(2)]
        pT = [region(18432 + i * 512, 4, P) for i in range(2)]
        rt, ru = region(19456, 640), region(20096, 640)
        kdup = region(20736, TT, 2, 2, 64)
        ass = sm(TT, 10)
        nmax = sm(TT * 8)
        rsum = sm(TT * 8)
        yT = region(14336, 16, TOK)
        merged = region(0, KO, TOK)
        gate_e = [region(4096 + i * 512, 512) for i in range(2)]
        gate_bc = region(8192, 2, D)
        o[0] = 0
        sc = sm(TT, NE)
        bi = sm(TT, NE)
        oh = [sm(TT, NE), sm(TT, NE)]
        t16 = sm(TT, NE)
        m1, m2, gsc, gsel = sm(TT, 4), sm(TT, 4), sm(TT, 4), sm(TT, 4)
        gmax = sm(TT)
        gates = sm(2, TT)
        rank = sm(TT, NE)
        over = sm(TT, NE)
        slotf = sm(2, TT)
        cnt, xtr, incl, scan_t = sm(NE), sm(NE), sm(NE), sm(NE)
        off = sm(NE)
        blk = sm(8, NE)
        blkf = sm(8)
        ex_slot = [region(i * 4096, KO, 512) for i in range(5)] + [view(xb[:].rearrange("p a b -> p (a b)"), KO, 512)]
        hflat = hT[:].rearrange("p a b -> p (a b)")
        h_rows = region(TMP, TT, D)
        xg = hflat[:, 0:1024]
        xT = view(hflat[:, 1024:2048], KO, P)
        hid = hflat[:, 2048:3072]
        hidT = view(hflat[:, 3072:4096], KO, P)
        ob = region(20480, 1024)
        silu_h = [region(21504 + i * 512, 512) for i in range(2)]
        yr = region(0, TT, 2, D)

        landed = [sem(f"landed{i}") for i in range(RING)]
        stream_full = sem("stream_full")
        free = {"act": sem("free_act"), "dve": sem("free_dve")}
        const_in = sem("const_in")
        cond_in, cond_ready = sem("cond_in"), sem("cond_ready")
        chain = {"dve": sem("chain_dve"), "act": sem("chain_act"), "pool": sem("chain_pool")}
        made = {}

        def own(name):
            return name in EXPERT_SEMS or name.startswith("expert_in")

        def s(name, l):
            name, _ = SHARED.get(name, (name, 0))
            key = f"{name}_{l}" if own(name) else name
            if key not in made:
                made[key] = sem(key)
            return made[key]

        def first(i):
            return isinstance(i, int) and i == 0

        def count(name, l, value):
            sem_name, before = SHARED.get(name, (name, 0))
            earlier = 0 if own(name) or l == 0 else FIRST_LAYER[sem_name]
            return value + before + earlier

        class Chain:

            def __init__(self, eng, name):
                self.eng, self.sem, self.n = eng, chain[name], 0

            def __call__(self, ins):
                self.n += 1
                ins.then_inc(self.sem, 1)
                self.eng.wait_ge(self.sem, self.n)

        alink = None

        def tiles_of(l):
            return plan_layer(l)[0]

        def span_of(l):
            return (0, TOK) if l < NL - 1 else (CTX, TOK)

        def filled(l, kind, index):
            return groups[find[l, kind, index]]["number"] + 1

        def bank_of(l, kind, index):
            return groups[find[l, kind, index]]["bank"]

        def freer(l, kind, index):
            return free[groups[find[l, kind, index]]["engine"]]

        def freed(l, kind, index):
            return groups[find[l, kind, index]]["ordinal"]

        def for_outputs(kind, index):
            return (kind == "qk" and index < 2) or (kind == "xbc" and index >= 10)

        def z_groups(l, step):
            tiles = tiles_of(l)
            every = [(b * len(tiles) + i, (b, t)) for b in range(2) for i, t in enumerate(tiles)]
            return every[step * len(every) // TT:(step + 1) * len(every) // TT]

        def n_inters(l):
            return sum(b in tiles_of(l) for d in range(2) for b in ORDER[d][1:])

        SPREAD = (3, 4, 7)

        def fills(l, step):
            groups_ = [("v", t) for t in range(TT)] + [("attq", t) for t in tiles_of(l)]
            n = 8 * len(tiles_of(l))
            return groups_[step * len(groups_) // n:(step + 1) * len(groups_) // n]

        QUARTERS = [slice(32 * j, 32 * j + 2) for j in range(4)]
        MOD_BANKS = (6, 7, 0, 1)
        ORDER = [[0, 1, 2, 3], [1, 0, 3, 2]]

        def block_source(l, block):
            kind = block[0]
            w_in = I["w_in"][l].rearrange("(k p) n -> p k n", p=P)

            def cols_of(w, a, n):
                return w[:, :, a:a + n], n
            if kind == "mod":
                return cols_of(I["w_mod"][l].rearrange("(k p) n -> p k n", p=P), block[1] * 512, 512)
            if kind == "out":
                return cols_of(I["w_out"][l].rearrange("(k p) n -> p k n", p=P), block[1] * 512, 512)
            if kind == "wbr":
                name = ("w_br_a", "w_br_b", "w_br_c")[block[1]]
                return cols_of(I[name][l].rearrange("(k p) n -> p k n", p=P), block[2] * 512, 512)
            at, n = {"xbc": (C_XBC + 512 * block[1], 512), "dt": (C_DT, 32), "qk": (C_GQ, 512),
                     "gates": (C_GF, 32), "v": (C_GV, 512), "attq": (C_AQ, 512), "attkv": (C_AK, 256),
                     "z": (C_Z + 512 * block[1], 512), "r": (C_GR, 512),
                     "mg": (C_MG + D * block[1] + 512 * (block[2] if len(block) > 2 else 0), 512),
                     }[kind]
            return cols_of(w_in, at, n)

        def sp_stream(sp, l, a, b):
            for n in [n for n, load in enumerate(loads) if load["layer"] == l][a:b]:
                load = loads[n]
                if n >= RING:
                    sp.wait_ge(stream_full, loads[n - RING]["last"] + 1)
                src, w = block_source(load["owner"], load["block"])
                dst = ring[:, load["slot"], 0:src.shape[1], 0:w]
                sp.dma_start(dst, src).then_inc(landed[load["slot"]], 16)

        EXPERT = [("w1", 0), ("w3", 0), ("w1", 1), ("w3", 1), ("w2", 0), ("w2", 1)]

        def sp_experts(sp, l):
            def load(slot, e):
                name, half = EXPERT[slot]
                src = I[name][l][bass.ds(e, 1), :, half * 512:(half + 1) * 512]
                sp.dma_start(ex_slot[slot], src.rearrange("e (k p) n -> p (e k) n", p=P))\
                  .then_inc(s(f"expert_in{slot}", l), 16)

            UP, DOWN = range(4), range(4, 6)

            def consumed(slot, i):
                if slot in UP:
                    sp.wait_ge(s("up_full", l), count("up_full", l, i * 2 + (1 if slot < 2 else 2)))
                else:
                    sp.wait_ge(s("down_full", l), count("down_full", l, i * 2 + (slot - 3)))
            sp.wait_ge(s("x_tile", l), count("x_tile", l, len(tiles_of(l))))
            load(0, 0)
            load(1, 0)
            sp.wait_ge(s("gathered", l), count("gathered", l, 16))
            load(2, 0)
            load(3, 0)
            sp.wait_ge(s("x_saved", l), count("x_saved", l, 16))
            sp.wait_ge(s("xn2", l), count("xn2", l, len(tiles_of(l))))
            load(5, 0)
            sp.wait_ge(s("row_saved", l), count("row_saved", l, 16))
            load(4, 0)
            for slot in UP:
                consumed(slot, 0)
                load(slot, 1)
            if l < NL - 1:
                sp_stream(sp, l + 1, 0, RING)
            with sp.Fori(2, NE) as i:
                for slot in UP:
                    consumed(slot, i - 1)
                    load(slot, i)
                for slot in DOWN:
                    consumed(slot, i - 2)
                    load(slot, i - 1)
            for slot in DOWN:
                consumed(slot, NE - 2)
                load(slot, NE - 1)
            sp.wait_ge(s("route_ready", l), count("route_ready", l, 1))
            n_extra = sp.value_load(extra[0:1, 8:9], min_val=0, max_val=XTRA)
            for j in range(extra_blocks(l)):
                with sp.If(n_extra > j):
                    e = sp.value_load(extra[0:1, j:j + 1], min_val=0, max_val=NE - 1)
                    for slot in (*UP, *DOWN):
                        consumed(slot, NE + j - 1)
                        load(slot, e)

        def sp_rest(sp, l):
            tiles = tiles_of(l)
            t0 = tiles[0]
            sp.wait_ge(s("all_stored", l), count("all_stored", l, 1))
            sp.dma_start(xb[:, t0:, :], x_dram[t0 * P:, :].rearrange("(t p) d -> p t d", p=P)).then_inc(s("rest_in", l), 16)
            for c in range(2):
                sp.dma_start(gate_bc[:, c, :], mod_dram[l, c:c + 1, 5 * D:6 * D].to_broadcast([P, D]))\
                    .then_inc(s("rest_in", l), 16)

        def extra_blocks(l):
            return (len(tiles_of(l)) * P * 2 - 1) // P

        def small_loads(pool, l):
            small_in = s("small_in", l)
            pool.dma_start(rows[:], I["rows"][l:l + 1, :].to_broadcast([P, NROWS])).then_inc(small_in, 16)
            pool.dma_start(router_w[:], I["router_w"].rearrange("(k p) e -> p k e", p=P)).then_inc(small_in, 16)
            pool.dma_start(view(gate_w2[:], 2, 256), I["gla_w2"][l].rearrange("d r n -> r d n")).then_inc(small_in, 16)

        def cols_load(pool, l):
            pool.dma_start(cols[:], I["cols"][l]).then_inc(s("cols_in", l), 16)

        def mod_save(pool, l):
            pool.wait_ge(freer(l, "mod", 11), freed(l, "mod", 11))
            d4 = mod_dram[l].rearrange("c (g j x) -> c g j x", j=4, x=P)
            for j, q in enumerate(QUARTERS):
                pool.dma_start(d4[:, :, j, :], mod_rows[l][q]).then_inc(s("mod_saved", l), 16)
            pool.wait_ge(s("mod_saved", l), count("mod_saved", l, 64))

        def bias_load(pool, l):
            b4 = I["b_mod"][l:l + 1, :].to_broadcast([2, NMOD * D]).rearrange("c (g j x) -> c g j x", j=4, x=P)
            for j, q in enumerate(QUARTERS):
                pool.dma_start(mod_rows[l][q], b4[:, :, j, :]).then_inc(s("bias_in", l), 16)

        def pool_layer(pool, link, l):
            tiles = tiles_of(l)
            if l == 0:
                bias_load(pool, 0)
                pool.dma_start(consts[:], I["consts"]).then_inc(const_in, 16)
                for t in range(TT):
                    src = I["ctx"][0] if t < 2 else I["x"][0]
                    pool.dma_start(xb[:, t, :], src[(t % 2) * P:(t % 2 + 1) * P, :]).then_inc(s("x_in", 0), 16)
                pool.memset(zero_idx[:], 0).then_inc(s("zeroed", 0), 1)
                pool.memset(eps_t[:], EPS).then_inc(s("eps_set", 0), 1)
            else:
                pool.wait_ge(s("x_final", l - 1), count("x_final", l - 1, len(tiles_of(l - 1))))
                for t in range(TT):
                    pool.dma_start(x_dram[t * P:(t + 1) * P, :], xb[:, t, :]).then_inc(s("xd_saved", l), 16)
            if l == 0:
                small_loads(pool, l)
                cols_load(pool, l)
                mod_save(pool, l)
            if l == 0:
                pool.wait_ge(s("ss1", 0), count("ss1", 0, TT))
                pool.memset(junk, 0.0).then_inc(s("zeroed", 0), 1)
                pool.wait_ge(s("zeroed", 0), count("zeroed", 0, 2))
                for b in range(NE * P, SLOTS, P):
                    pool.dma_start(y_dram[b:b + P, :], junk).then_inc(s("y_zero", 0), 16)
            pool.dma_start(tok_dram.rearrange("(p b) o -> p (b o)", p=P), zero_idx[:]).then_inc(s("tok_zero", l), 16)
            pool.wait_ge(s("ct_done", l), count("ct_done", l, 10))
            pool.wait_ge(s("w_ready", l), count("w_ready", l, 1))
            for q, t in enumerate(tiles):
                x3 = view(xs[:, t, :], SH, SP)
                for d in range(2):
                    if q >= 2:
                        pool.wait_ge(s("ymm_done", l), count("ymm_done", l, 8 * (q - 1)))
                    pool.tensor_tensor(view(xw[q % 2][d], SH, SP), x3,
                                       dt[:, t, d * 16:d * 16 + 16].unsqueeze(2).to_broadcast([P, SH, SP]),
                                       ALU.mult).then_inc(s("pool_x", l), 1)
                pool.tensor_tensor(view(ys[:, t, :], SH, SP), x3,
                                   Rw("ssd_d").unsqueeze(2).to_broadcast([P, SH, SP]),
                                   ALU.mult).then_inc(s("pool_x", l), 1)
            pool.wait_ge(s("ymm_done", l), count("ymm_done", l, 8 * len(tiles)))
            for k in range(3):
                for d in range(2):
                    b = ORDER[d][k]
                    if k:
                        pool.wait_ge(s("upd_full", l), count("upd_full", l, 2 * (k - 1) + d + 1))
                    pool.tensor_tensor(view(xw[0][d], SH, SP), view(xs[:, b, :], SH, SP),
                                       wd[:, b, d * 16:d * 16 + 16].unsqueeze(2).to_broadcast([P, SH, SP]),
                                       ALU.mult).then_inc(s("wx_ready", l), 1)
            pool.wait_ge(s("branch_rs", l), count("branch_rs", l, 1))
            t0 = tiles[0]
            pool.wait_ge(freer(l, "r", tiles[-1]), freed(l, "r", tiles[-1]))
            for t in tiles:
                y4 = view(yg[:, t, :], 4, P)
                link(pool.tensor_tensor(y4, y4, bc(gss[:, t, :], P), ALU.mult))
                link(pool.tensor_tensor(y4, y4, bc_mid(Rw("gla_norm"), 4), ALU.mult))
                pool.tensor_tensor(yg[:, t, :], yg[:, t, :], kv[:, t].rearrange("p a b c -> p (a b c)"), ALU.mult)
                y2 = view(ys[:, t, :], 2, 512)
                link(pool.tensor_tensor(y2, y2, bc(rstd[:, 2 * t:2 * t + 2], 512), ALU.mult))
                ins = pool.tensor_tensor(ys[:, t, :], ys[:, t, :], Rw("ssd_norm"), ALU.mult)
            ins.then_inc(s("branches_final", l), 1)
            pool.wait_ge(s("yt_act", l), count("yt_act", l, 2 * len(tiles)))
            pool.wait_ge(s("yt_dve", l), count("yt_dve", l, 2 * len(tiles)))
            if l:
                pool.wait_ge(s("xd_saved", l), count("xd_saved", l, 16 * TT))
            for t in tiles:
                if l == 0:
                    src = (I["ctx"][0] if t < 2 else I["x"][0])[(t % 2) * P:(t % 2 + 1) * P, :]
                else:
                    src = x_dram[t * P:(t + 1) * P, :]
                pool.dma_start(xb[:, t, :], src).then_inc(s("x_again", l), 16)
            for c in range(2):
                pool.dma_start(gate_bc[:, c, :], mod_dram[l, c:c + 1, 2 * D:3 * D].to_broadcast([P, D]))\
                    .then_inc(s("x_again", l), 16)
            if l < NL - 1:
                bias_load(pool, l + 1)
            pool.wait_ge(s("x_tile", l), count("x_tile", l, len(tiles_of(l))))
            if l < NL - 1:
                cols_load(pool, l + 1)
            pool.dma_start(x_dram[t0 * P:, :].rearrange("(t p) d -> p t d", p=P), xb[:, t0:, :])\
                .then_inc(s("x_saved", l), 16)
            pool.wait_ge(s("row_ready", l), count("row_ready", l, 2 * len(tiles)))
            pool.dma_start(h_dram[t0 * P:, :].rearrange("(t p) d -> p t d", p=P), h_rows[:, t0:, :])\
                .then_inc(s("row_saved", l), 16)
            if l == 0:
                pool.tensor_copy(tok_id[:], K("token")).then_inc(s("tok_id", 0), 1)
                pool.wait_ge(s("tok_id", 0), count("tok_id", 0, 1))
            pool.wait_ge(s("tok_zero", l), count("tok_zero", l, 16))
            pool.wait_ge(s("route_ready", l), count("route_ready", l, 1))
            n = 0
            for c in range(2):
                for t in tiles:
                    pool.indirect_dma_start(tok_dram, bass.IndirectOffsetOnAxis(ap=slot_idx[:, c * TT + t:c * TT + t + 1], axis=0),
                                            tok_id[:, t:t + 1], None).then_inc(s("tok_put", l), 16)
                    n += 1
            pool.wait_ge(s("tok_put", l), count("tok_put", l, 16 * n))
            pool.wait_ge(s("row_saved", l), count("row_saved", l, 16))
            pool.dma_start(tok_idx[:], tok_dram.rearrange("(b p) o -> p (b o)", p=P), allow_slow_non_contiguous=True)\
                .then_inc(s("tok_got", l), 16)
            pool.wait_ge(s("tok_got", l), count("tok_got", l, 16))
            pool.wait_ge(s("rows_full", l), count("rows_full", l, 2 * len(tiles)))

            def gather(idx):
                pool.indirect_dma_start(xg, None, h_dram, bass.IndirectOffsetOnAxis(ap=idx, axis=0))\
                    .then_inc(s("gathered", l), 16)
            gather(tok_idx[:, 0:1])
            if l < NL - 1:
                mod_save(pool, l + 1)
                pool.wait_ge(s("modc_ready", l + 1), count("modc_ready", l + 1, 1))
                small_loads(pool, l + 1)
            for i in range(NE):
                pool.wait_ge(s("xt_full", l), count("xt_full", l, i + 1))
                gather(tok_idx[:, i + 1:i + 2])
            n_extra = pool.value_load(extra[0:1, 8:9], min_val=0, max_val=XTRA)
            for j in range(extra_blocks(l)):
                with pool.If(n_extra > j):
                    pool.wait_ge(s("xt_full", l), count("xt_full", l, NE + j + 1))
                    gather(tok_idx[:, NE + j + 1:NE + j + 2])
                    pool.wait_ge(s("stored", l), count("stored", l, 16 * (NE + j)))
            pool.wait_ge(s("all_stored", l), count("all_stored", l, 1))
            for n, t in enumerate(tiles):
                for c in range(2):
                    pool.indirect_dma_start(yr[:, t, c, :], None, y_dram,
                                            bass.IndirectOffsetOnAxis(ap=slot_idx[:, c * TT + t:c * TT + t + 1], axis=0))\
                        .then_inc(s("y_first" if n < len(tiles) // 2 else "y_rest", l), 16)

        def pe_group(pe, l, kind, index):
            n = find[l, kind, index]
            g = groups[n]
            load = g["load"]
            pe.wait_ge(landed[loads[load]["slot"]], 16 * (load // RING + 1))
            if n >= NSTREAM:
                before = groups[n - NSTREAM]
                pe.wait_ge(free[before["engine"]], before["ordinal"])
            w = ring[:, loads[load]["slot"]]
            a, b = span_of(l)
            ks = KO
            if kind == "mod":
                for k in range(KO):
                    for j, q in enumerate(QUARTERS):
                        ins = pe.matmul(ps[q, g["bank"], 0:P], cond[:, k, :], w[:, k, j * P:(j + 1) * P],
                                        start=(k == 0), stop=(k == KO - 1))
                ins.then_inc(stream_full, 1)
                return
            elif kind in ("xbc", "qk"):
                i = index % 4
                if not for_outputs(kind, index):
                    a, b = 0, TOK
                dst = ps[:, g["bank"], 0:b - a]
                left, right = lambda k: w[:, k, i * P:(i + 1) * P], lambda k: hT[:, k, a:b]
            elif kind == "gates":
                for k in range(KO):
                    for d in range(2):
                        for half in range(2):
                            lo = 32 * (2 * d + half)
                            ins = pe.matmul(ps[lo:lo + 16, g["bank"], 0:CTX], w[:, k, d * 16:(d + 1) * 16],
                                            hT[:, k, half * CTX:(half + 1) * CTX], start=(k == 0), stop=(k == KO - 1))
                ins.then_inc(stream_full, 1)
                return
            elif kind in ("dt", "v", "attq", "attkv", "z", "r"):
                t = index[1] if kind == "z" else index
                n_cols = {"dt": 32, "attkv": 256}.get(kind, 512)
                dst = ps[:, g["bank"], 0:n_cols]
                left, right = lambda k: hT[:, k, t * P:(t + 1) * P], lambda k: w[:, k, 0:n_cols]
            elif kind == "gate":
                i = index[1] % 4
                dst = ps[:, g["bank"], 0:b - a]
                left, right = lambda k: w[:, k, i * P:(i + 1) * P], lambda k: hT[:, k, a:b]
            elif kind == "prod":
                j, i = index[0], index[1] % 4
                row = (0, 4, 8)[j]
                ks = (4, 4, 8)[j]
                dst = ps[:, g["bank"], 0:b - a]
                left, right = lambda k: w[:, k, i * P:(i + 1) * P], lambda k: yT[:, row + k, a:b]
            else:
                t = index[1]
                dst = ps[:, g["bank"], :]
                left, right = lambda k: merged[:, k, t * P:(t + 1) * P], lambda k: w[:, k, :]
            for k in range(ks):
                ins = pe.matmul(dst, left(k), right(k), start=(k == 0), stop=(k == ks - 1))
            ins.then_inc(stream_full, 1)

        def pe_turn_norm(pe, l, which, n, t):
            pe.wait_ge(s(f"xn{which}", l), count(f"xn{which}", l, n + 1))
            if n >= 2:
                pe.wait_ge(s(f"hT{which}", l), count(f"hT{which}", l, n - 1))
            for k in range(KO):
                ins = pe.transpose(ps[:, 2 + 2 * (n % 2) + k // 4, (k % 4) * P:(k % 4 + 1) * P],
                                   xn[:, t, k * P:(k + 1) * P], ident)
            ins.then_inc(s(f"tr{which}", l), 1)

        def pe_logits(pe, l, n, t):
            pe.wait_ge(s("hT2", l), count("hT2", l, n + 1))
            for k in range(KO):
                ins = pe.matmul(ps[:, 6, t * NE:(t + 1) * NE], hT[:, k, t * P:(t + 1) * P], router_w[:, k, :],
                                start=(k == 0), stop=(k == KO - 1))
            if t == TT - 1:
                ins.then_inc(s("logit_full", l), 1)

        def pe_decay_sums(pe, l):
            pe.wait_ge(s("da_ready", l), count("da_ready", l, 1))
            pe.wait_ge(s("ct_done", l), count("ct_done", l, 9))
            for t in range(TT):
                pe.matmul(ps[:, 4, t * 64:t * 64 + 16], upper, da[:, t, 0:16], start=True, stop=True)
                pe.matmul(ps[:, 4, t * 64 + 16:t * 64 + 32], lower, da[:, t, 16:32], start=True, stop=True)
                ins = pe.matmul(ps[:, 4, t * 64 + 32:t * 64 + 64], ones, da[:, t, :], start=True, stop=True)
            ins.then_inc(s("cum_full", l), 1)

        def pe_scan(pe, l):
            tiles = tiles_of(l)
            pe.wait_ge(s("ct_done", l), count("ct_done", l, 10))

            def spread(q, t, k):
                kq = q * 8 + k
                if kq >= 3:
                    pe.wait_ge(s("diff_done", l), count("diff_done", l, kq - 2))
                d, quad = k // 4, k % 4
                for i in range(4):
                    h = d * 16 + quad * 4 + i
                    ins = pe.matmul(ps[:, SPREAD[kq % 3], i * P:(i + 1) * P],
                                    da[:, t, h:h + 1].to_broadcast([P, P]), tri[d], start=True, stop=True)
                ins.then_inc(s("bc_full", l), 1)

            def within(q, t, k):
                kq = q * 8 + k
                d, quad = k // 4, k % 4
                pe.wait_ge(s("m_ready", l), count("m_ready", l, kq + 1))
                if k == 0:
                    pe.wait_ge(s("pool_x", l), count("pool_x", l, 3 * q + 3))
                    if q:
                        pe.wait_ge(s("y_evac", l), count("y_evac", l, q))
                for i in range(4):
                    h = quad * 4 + i
                    ins = pe.matmul(ps[:, 5 + h // 8, (h % 8) * SP:(h % 8 + 1) * SP],
                                    mm[kq % 2][:, i * P:(i + 1) * P], xw[q % 2][d][:, h * SP:(h + 1) * SP],
                                    start=(d == 0 and h % 8 == 0), stop=(d == 1), skip_group_check=True)
                ins.then_inc(s("ymm_done", l), 1)
            pe.wait_ge(s("cum_ready", l), count("cum_ready", l, 1))
            steps = []
            for q, t in enumerate(tiles):
                if q:
                    pe.wait_ge(s("cbm_ready", l), count("cbm_ready", l, q))
                for g in range(2):
                    ins = pe.matmul(ps[:, 2, g * P:(g + 1) * P], bcT[:, g, t * P:(t + 1) * P],
                                    bcT[:, 2 + g, t * P:(t + 1) * P], start=True, stop=True)
                ins.then_inc(s("cb_full", l), 1)
                for k in range(8):
                    spread(q, t, k)
                    for kind, index in fills(l, q * 8 + k):
                        pe_group(pe, l, kind, index)
                    steps.append((q, t, k))
                    if len(steps) > 2:
                        within(*steps[-3])
            within(*steps[-2])
            within(*steps[-1])
            pe.wait_ge(s("y_evac", l), count("y_evac", l, len(tiles)))
            pe.wait_ge(s("cbm_ready", l), count("cbm_ready", l, len(tiles)))
            n_inter = 0
            for k in range(4):
                for d in range(2):
                    b = ORDER[d][k]
                    u = 2 * k + d
                    if k and b in tiles:
                        pe.wait_ge(s("s_ready", l), count("s_ready", l, u - 1))
                        if n_inter:
                            pe.wait_ge(s("inter_done", l), count("inter_done", l, n_inter))
                        for g in range(2):
                            ins = pe.matmul(ps[:, 2 + g, :], bcT[:, 2 + g, b * P:(b + 1) * P],
                                            state[:, d, g * 512:(g + 1) * 512], start=True, stop=True)
                        ins.then_inc(s("inter_full", l), 1)
                        n_inter += 1
                    if k < 3:
                        if u:
                            pe.wait_ge(s("s_ready", l), count("s_ready", l, u))
                        pe.wait_ge(s("wx_ready", l), count("wx_ready", l, u + 1))
                        for g in range(2):
                            ins = pe.matmul(ps[:, 5 + g, :], b_tm[:, b, g * P:(g + 1) * P],
                                            xw[0][d][:, g * 512:(g + 1) * 512], start=True, stop=True)
                        ins.then_inc(s("upd_full", l), 1)
                        if u < TT:
                            pe_group(pe, l, "attkv", u)

        def pe_gla(pe, l):
            tiles = tiles_of(l)
            pe.wait_ge(s("inter_done", l), count("inter_done", l, n_inters(l)))
            pe.wait_ge(s("s_ready", l), count("s_ready", l, 6))
            for t in range(TT):
                for d in range(2):
                    ins = pe.matmul(ps[:, 2 + t, d * 256:(d + 1) * 256], gT[0:16, d, t * P:(t + 1) * P],
                                    gate_w2[:, d * 256:(d + 1) * 256], start=True, stop=True)
            ins.then_inc(s("lg_full", l), 1)
            for _, index in z_groups(l, 0):
                pe_group(pe, l, "z", index)
            pe.wait_ge(s("g_ready", l), count("g_ready", l, 1))

            def running(t):
                if t >= 2:
                    pe.wait_ge(s("b_done", l), count("b_done", l, t - 1))
                for d in range(2):
                    for f in range(2):
                        j = d * 2 + f
                        ins = pe.matmul(ps[:, 6 + t % 2, j * P:(j + 1) * P],
                                        gg[:, t, d * 256 + f * P:d * 256 + (f + 1) * P], tri[d], start=True, stop=True)
                ins.then_inc(s("b_full", l), 1)
            running(0)
            for t in range(TT):
                if t < TT - 1:
                    running(t + 1)
                    for _, index in z_groups(l, t + 1):
                        pe_group(pe, l, "z", index)
                else:
                    pe_group(pe, l, "r", tiles[0])
                pe.wait_ge(s("qkd_ready", l), count("qkd_ready", l, t + 1))
                if t:
                    pe.wait_ge(s("kdt_ready", l), count("kdt_ready", l, t))
                for d in range(2):
                    for f in range(2):
                        ins = pe.transpose(ps[:, 2, (d * 2 + f) * P:(d * 2 + f + 1) * P], kd[:, t * 2 + d, f, :], ident)
                ins.then_inc(s("kdt_full", l), 1)
                pe.wait_ge(s("kdt_ready", l), count("kdt_ready", l, t + 1))
                if t:
                    pe.wait_ge(s("kv_done", l), count("kv_done", l, t))
                for d in range(2):
                    for f in range(2):
                        ins = pe.matmul(ps[:, 3 + d, f * 256:(f + 1) * 256], kdT[:, d * 2 + f, :],
                                        gv[:, t, f * 256:(f + 1) * 256], start=True, stop=True)
                ins.then_inc(s("kv_full", l), 1)
            pe.wait_ge(s("kv_done", l), count("kv_done", l, TT))
            pe_group(pe, l, "r", tiles[1])

            def scores(q, t):
                if q >= 2:
                    pe.wait_ge(s("p_ready", l), count("p_ready", l, 2 * (q - 1)))
                for d in range(2):
                    for h in range(4):
                        lo, f = 64 * (h % 2), h // 2
                        ins = pe.matmul(ps[:, (2, 6)[q % 2] + h % 2, (d * 2 + f) * P:(d * 2 + f + 1) * P],
                                        kd[lo:lo + 64, t * 2 + d, f, :],
                                        qd[lo:lo + 64, t * 2 + d, f, :], start=True, stop=True)
                ins.then_inc(s("sc_full", l), 1)
            scores(0, tiles[0])
            scores(1, tiles[1])
            pe.wait_ge(s("sp_ready", l), count("sp_ready", l, 1))
            for q, t in enumerate(tiles):
                pe.wait_ge(s("p_ready", l), count("p_ready", l, 2 * q + 2))
                if q:
                    pe.wait_ge(s("gy_done", l), count("gy_done", l, q))
                for h in range(4):
                    lo, f = 64 * (h % 2), h // 2
                    dst = ps[:, 4 + h % 2, f * P:(f + 1) * P]
                    terms = [(pm[d][:, h, :], gv[:, t, h * P:(h + 1) * P]) for d in range(2)]
                    terms += [(qd[lo:lo + 64, t * 2 + d, f, :], sp[lo:lo + 64, t * 2 + d, f, :])
                              for d in range(2) if t != ORDER[d][0]]
                    for n, (a, b) in enumerate(terms):
                        ins = pe.matmul(dst, a, b, start=(n == 0), stop=(n == len(terms) - 1))
                ins.then_inc(s("gy_full", l), 1)
                if q + 2 < len(tiles):
                    pe_group(pe, l, "r", tiles[q + 2])
                    scores(q + 2, tiles[q + 2])

        def pe_att(pe, l):
            tiles = tiles_of(l)
            for t in range(TT):
                pe.wait_ge(s("att_prep", l), count("att_prep", l, t + 1))
                if t:
                    pe.wait_ge(s("qk_turned", l), count("qk_turned", l, t))
                if t in tiles:
                    for f in range(4):
                        pe.transpose(ps[:, 2, f * P:(f + 1) * P], att[:, t, f * P:(f + 1) * P], ident)
                for g in range(2):
                    ins = pe.transpose(ps[:, 3, g * P:(g + 1) * P],
                                       kdup[:, t, g, :, :].rearrange("p a b -> p (a b)"), ident)
                ins.then_inc(s("qk_full", l), 1)
            pe.wait_ge(s("qk_turned", l), count("qk_turned", l, TT))
            pe.wait_ge(s("gy_done", l), count("gy_done", l, len(tiles)))

            def scores(q, t, h):
                n = q * 8 + h
                if n >= 2:
                    pe.wait_ge(s("p_exp", l), count("p_exp", l, n - 1))
                lo = 64 * (h % 2)
                w = CTX if t < 2 else TOK
                a = qT[lo:lo + 64, h // 2, t * P:(t + 1) * P]
                ins = pe.matmul(ps[:, 4 + n % 2, 0:w], a, kT2[lo:lo + 64, h // 4, 0:w], start=True, stop=(t < 2),
                                skip_group_check=True)
                if t >= 2:
                    ins = pe.matmul(ps[:, 4 + n % 2, CTX:TOK], ident, view(K("window"), 2, 256)[:, t - 2, :],
                                    start=False, stop=True, skip_group_check=True)
                ins.then_inc(s("s_full", l), 1)

            def turn(q, t, h):
                n = q * 8 + h
                pe.wait_ge(s("p_exp", l), count("p_exp", l, n + 1))
                if n >= 2:
                    pe.wait_ge(s("pt_ready", l), count("pt_ready", l, n - 1))
                for j in range(2 if t < 2 else 4):
                    ins = pe.transpose(ps[:, 6 + n % 2, j * P:(j + 1) * P], pb[n % 2][:, j * P:(j + 1) * P], ident)
                ins.then_inc(s("pt_full", l), 1)

            def values(q, t, h):
                n = q * 8 + h
                pe.wait_ge(s("pt_ready", l), count("pt_ready", l, n + 1))
                if h == 0 and q >= 2:
                    pe.wait_ge(s("o_raw", l), count("o_raw", l, q - 1))
                nk = 2 if t < 2 else 4
                for j in range(nk):
                    g = h // 4
                    ins = pe.matmul(ps[:, 2 + q % 2, h * 64:(h + 1) * 64], pT[n % 2][:, j, :],
                                    att[:, j, 640 + g * 64:640 + (g + 1) * 64], start=(j == 0), stop=(j == nk - 1))
                ins.then_inc(s("o_full", l), 1)
            seq = [(q, t, h) for q, t in enumerate(tiles) for h in range(8)]
            for i in range(len(seq) + 2):
                if i < len(seq):
                    scores(*seq[i])
                if 1 <= i <= len(seq):
                    turn(*seq[i - 1])
                if i >= 2:
                    values(*seq[i - 2])

        def y_source(t, c):
            if c < 2:
                return ys[:, t, c * 512:(c + 1) * 512], 8 + 4 * c
            if c == 2:
                return yg[:, t, :], 0
            return att[:, t, 0:512], 4

        def pe_turn_y(pe, l):
            tiles = tiles_of(l)
            pe.wait_ge(s("branches_final", l), count("branches_final", l, 1))
            pe.wait_ge(s("o_done", l), count("o_done", l, len(tiles)))
            for n in range(4 * len(tiles)):
                src, _ = y_source(tiles[n // 4], n % 4)
                if n >= 4:
                    pe.wait_ge(s("yt_dve" if n % 2 else "yt_act", l), count("yt_dve" if n % 2 else "yt_act", l, (n - 4) // 2 + 1))
                for i in range(4):
                    ins = pe.transpose(ps[:, 2 + n % 4, i * P:(i + 1) * P], src[:, i * P:(i + 1) * P], ident)
                ins.then_inc(s("yt_full", l), 1)
            pe.wait_ge(s("yt_act", l), count("yt_act", l, 2 * len(tiles)))
            pe.wait_ge(s("yt_dve", l), count("yt_dve", l, 2 * len(tiles)))

        def pe_ranks(pe, l):
            tiles = tiles_of(l)
            pe.wait_ge(s("assigned", l), count("assigned", l, 1))
            for n, t in enumerate(tiles):
                for m in range(n):
                    pe.matmul(ps[:, 6, t * NE:(t + 1) * NE], ones, t16[:, tiles[m], :], start=(m == 0), stop=False)
                pe.matmul(ps[:, 6, t * NE:(t + 1) * NE], K("strict"), t16[:, t, :], start=(n == 0), stop=True)
            for n, t in enumerate(tiles):
                ins = pe.matmul(ps[:, 6, 64:64 + NE], ones, t16[:, t, :], start=(n == 0), stop=(n == len(tiles) - 1))
            ins.then_inc(s("rank_full", l), 1)

        def pe_route(pe, l):
            tiles = tiles_of(l)
            for n in range(2 * len(tiles)):
                if n == 2 * len(tiles) - 2:
                    pe_ranks(pe, l)
                t, half = tiles[n // 2], n % 2
                if n >= 2:
                    pe.wait_ge(s("row_ready", l), count("row_ready", l, n - 1))
                for i in range(4):
                    ins = pe.transpose(ps[:, 2 + n % 2, i * P:(i + 1) * P],
                                       hT[:, half * 4 + i, t * P:(t + 1) * P], ident)
                ins.then_inc(s("rows_full", l), 1)
            if l < NL - 1:
                for c in range(EARLY, 12):
                    pe_group(pe, l + 1, "mod", c)
                pe_turn_mod(pe, l + 1)

        def pe_experts(pe, l):
            def turn_x(i):
                pe.wait_ge(s("gathered", l), count("gathered", l, (i + 1) * 16))
                for k in range(KO):
                    ins = pe.transpose(ps[:, k // 4, (k % 4) * P:(k % 4 + 1) * P], xg[:, k * P:(k + 1) * P], ident)
                ins.then_inc(s("xt_full", l), 1)

            def up(i, half):
                if half == 0:
                    pe.wait_ge(s("xt_ready", l), count("xt_ready", l, i + 1))
                if not first(i):
                    pe.wait_ge(s("hid_ready", l), count("hid_ready", l, i * 2 - 1 + half))
                for m in range(2):
                    slot = half * 2 + m
                    pe.wait_ge(s(f"expert_in{slot}", l), count(f"expert_in{slot}", l, (i + 1) * 16))
                    for k in range(KO):
                        ins = pe.matmul(ps[:, 2 + slot, :], xT[:, k, :], ex_slot[slot][:, k, :],
                                        start=(k == 0), stop=(k == KO - 1))
                ins.then_inc(s("up_full", l), 1)

            def turn_hid(i):
                pe.wait_ge(s("xt_ready", l), count("xt_ready", l, i + 2))
                for half in range(2):
                    pe.wait_ge(s("hid_ready", l), count("hid_ready", l, i * 2 + half + 1))
                    for j in range(4):
                        ins = pe.transpose(ps[:, half, j * P:(j + 1) * P],
                                           hid[:, half * 512 + j * P:half * 512 + (j + 1) * P], ident)
                    ins.then_inc(s("ht_full", l), 1)

            def down(i):
                pe.wait_ge(s("ht_ready", l), count("ht_ready", l, i * 2 + 2))
                for half in range(2):
                    pe.wait_ge(s(f"expert_in{4 + half}", l), count(f"expert_in{4 + half}", l, (i + 1) * 16))
                    for k in range(KO):
                        ins = pe.matmul(ps[:, 6 + half, :], hidT[:, k, :], ex_slot[4 + half][:, k, :],
                                        start=(k == 0), stop=(k == KO - 1))
                    ins.then_inc(s("down_full", l), 1)

            def block(i):
                up(i, 0)
                up(i, 1)
                if not first(i):
                    pe.wait_ge(s("ht_ready", l), count("ht_ready", l, i * 2))
                turn_x(i + 1)
                if not first(i):
                    down(i - 1)
                turn_hid(i)
            pe.wait_ge(s("row_ready", l), count("row_ready", l, 2 * len(tiles_of(l))))
            pe.wait_ge(s("route_ready", l), count("route_ready", l, 1))
            turn_x(0)
            block(0)
            with pe.Fori(1, NE) as i:
                block(i)
            n_extra = pe.value_load(extra[0:1, 8:9], min_val=0, max_val=XTRA)
            for j in range(extra_blocks(l)):
                with pe.If(n_extra > j):
                    block(NE + j)
            down(n_extra + (NE - 1))

        def pe_turn_mod(pe, l):
            pe.wait_ge(freer(l, "mod", 11), freed(l, "mod", 11))
            for v, m in enumerate((0, 1, 3, 4)):
                for k in range(KO):
                    j, at = k % 4, (v * 2 + k // 4) * 2
                    q = QUARTERS[j]
                    ins = pe.transpose(ps[:, MOD_BANKS[j], at:at + 2], mod_rows[l][q, m * 2 + k // 4, :], ident[q, q])
            ins.then_inc(s("modT_full", l), 1)
            pe.wait_ge(s("modc_ready", l), count("modc_ready", l, 1))

        def pe_layer(pe, l):
            tiles = tiles_of(l)
            if l == 0:
                pe.wait_ge(cond_ready, 1)
                for c in range(12):
                    pe_group(pe, l, "mod", c)
                pe.wait_ge(const_in, 16)
                pe_turn_mod(pe, l)
            for t in range(TT):
                pe_turn_norm(pe, l, 1, t, t)
            pe.wait_ge(s("hT1", l), count("hT1", l, TT))

            def turn_conv(i):
                pe.wait_ge(s("conv_done", l), count("conv_done", l, i + 1))
                if i >= 2:
                    pe.wait_ge(s("ct_done", l), count("ct_done", l, i - 1))
                src = xsT[:, i % 2, :] if i < 8 else bcT[:, i - 8, :]
                for t in range(TT):
                    ins = pe.transpose(ps[:, 2 + i % 2, t * P:(t + 1) * P], src[:, t * P:(t + 1) * P], ident)
                ins.then_inc(s("ct_full", l), 1)
            for i in range(12):
                pe_group(pe, l, "xbc", i)
                if i >= 2:
                    turn_conv(i - 2)
            for t in range(TT):
                pe_group(pe, l, "dt", t)
            for i in range(4):
                pe_group(pe, l, "qk", i)
            pe_decay_sums(pe, l)
            pe_group(pe, l, "gates", 0)
            pe_scan(pe, l)
            pe.wait_ge(freer(l, "attkv", TT - 1), freed(l, "attkv", TT - 1))
            pe_gla(pe, l)
            pe_att(pe, l)
            pe_turn_y(pe, l)
            for j in range(3):
                for i in range(KO):
                    pe_group(pe, l, "gate", (j, i))
                    pe_group(pe, l, "prod", (j, i))
                    if l < NL - 1 and i % 4 == 3:
                        for c in early_mods(2 * j + i // 4):
                            pe_group(pe, l + 1, "mod", c)
            pe.wait_ge(freer(l, "prod", (2, KO - 1)), freed(l, "prod", (2, KO - 1)))
            pe.wait_ge(s("merged", l), count("merged", l, 1))
            for n, t in enumerate(tiles):
                pe_group(pe, l, "out", (0, t))
                pe_group(pe, l, "out", (1, t))
                if n >= 1:
                    pe_turn_norm(pe, l, 2, n - 1, tiles[n - 1])
                if n >= 2:
                    pe_logits(pe, l, n - 2, tiles[n - 2])
            n_t = len(tiles)
            pe_turn_norm(pe, l, 2, n_t - 1, tiles[-1])
            pe_logits(pe, l, n_t - 2, tiles[-2])
            pe_logits(pe, l, n_t - 1, tiles[-1])
            pe_route(pe, l)
            pe_experts(pe, l)

        def act_norm(act, l, which, n, t):
            if n:
                act.wait_ge(s(f"ss{which}", l), count(f"ss{which}", l, n))
            act.activation(junk, xb[:, t, :], ACT.Square, accum_out=sumsq[:, t:t + 1]).then_inc(s(f"ss{which}", l), 1)
            act.wait_ge(s(f"ss{which}", l), count(f"ss{which}", l, n + 1))
            rms(act, sumsq[:, t:t + 1], rstd[:, t:t + 1], D).then_inc(s(f"rs{which}", l), 1)

        def rms(act, src, dst, n):
            alink(act.activation(dst, src, ACT.Ln, scale=1.0 / n, bias=eps_t[:, 0:1]))
            return act.activation(dst, dst, ACT.Exp, scale=-0.5)

        def softplus_of_minus_abs(act, ap, src):
            alink(act.activation(ap, src, ACT.Abs))
            alink(act.activation(ap, ap, ACT.Exp, scale=-1.0))
            return act.activation(ap, ap, ACT.Ln, bias=1.0)

        def act_group(act, l, kind, index, dst, scale=1.0):
            act.wait_ge(stream_full, filled(l, kind, index))
            bank = bank_of(l, kind, index)
            w = dst.shape[-1]
            act.activation(dst, ps[:, bank, 0:w], ACT.Copy, scale=scale).then_inc(free["act"], 1)

        def act_z(act, l, step):
            for n, index in z_groups(l, step) if step < TT else []:
                act.wait_ge(stream_full, filled(l, "z", index))
                if n >= 2:
                    act.wait_ge(s("yz_ready", l), count("yz_ready", l, n - 1))
                act.activation(zs[n % 2], ps[:, bank_of(l, "z", index), :], ACT.Silu).then_inc(free["act"], 1)

        def act_r(act, l, t):
            act.wait_ge(stream_full, filled(l, "r", t))
            act.activation(kv[:, t].rearrange("p a b c -> p (a b c)"), ps[:, bank_of(l, "r", t), :], ACT.Silu)\
                .then_inc(free["act"], 1)

        def act_layer(act, l):
            tiles = tiles_of(l)
            n_t = len(tiles)
            t0 = tiles[0]
            if l == 0:
                act.wait_ge(cond_in, 16)
                act.activation(cond[:], cond[:], ACT.Silu).then_inc(cond_ready, 1)
                act.wait_ge(s("x_in", 0), count("x_in", 0, 16 * TT))
                act.wait_ge(s("eps_set", 0), count("eps_set", 0, 1))
            else:
                act.wait_ge(s("x_final", l - 1), count("x_final", l - 1, 1))
            for t in range(TT):
                if l and t:
                    act.wait_ge(s("x_final", l - 1), count("x_final", l - 1, t + 1))
                act_norm(act, l, 1, t, t)
            act.wait_ge(s("small_in", l), count("small_in", l, 48))
            alink(act.activation(neg_a[:], Rw("a_log"), ACT.Exp))
            if l:
                act.wait_ge(s("xd_saved", l), count("xd_saved", l, 16 * TT))
            act.wait_ge(s("hT1", l), count("hT1", l, TT))
            for i in range(12):
                if i >= 3:
                    act.wait_ge(s("conv_acc", l), count("conv_acc", l, i - 2))
                a, b = span_of(l) if for_outputs("xbc", i) else (0, TOK)
                act_group(act, l, "xbc", i, raw[:, i % 3, a:b])
                if i >= 1:
                    act_conv_silu(act, l, i - 1)
                if i >= 2:
                    act_conv_rows(act, l, i - 2)
            act_conv_silu(act, l, 11)
            act.wait_ge(s("sp1", l), count("sp1", l, 1))
            softplus_of_minus_abs(act, dt[:], dt_raw[:]).then_inc(s("sp2", l), 1)
            for i in range(4):
                a, b = span_of(l) if for_outputs("qk", i) else (0, TOK)
                act_group(act, l, "qk", i, qkT[:, i, a:b], scale=0.125 if i < 2 else 1.0)
            act.wait_ge(s("cum_ready", l), count("cum_ready", l, 1))
            alink(act.activation(ecs[:], cums[:], ACT.Exp))
            act.wait_ge(s("wd_pre", l), count("wd_pre", l, 1))
            act.activation(wd[:], wd[:], ACT.Exp).then_inc(s("ecs_ready", l), 1)
            act.wait_ge(stream_full, filled(l, "gates", 0))
            for d in range(2):
                for half in range(2):
                    lo = 32 * (2 * d + half)
                    ins = act.activation(gT[0:16, d, half * CTX:(half + 1) * CTX],
                                         ps[lo:lo + 16, bank_of(l, "gates", 0), 0:CTX], ACT.Copy)
            ins.then_inc(free["act"], 1)
            for kq in range(8 * n_t):
                act.wait_ge(s("dm_ready", l), count("dm_ready", l, kq + 1))
                act.activation(dd[kq % 3], dd[kq % 3], ACT.Exp).then_inc(s("e_ready", l), 1)
                for kind, t in fills(l, kq):
                    place = {"v": gv, "attq": att[:, :, 0:512]}[kind]
                    act_group(act, l, kind, t, place[:, t, :])
            for t in range(TT):
                act_group(act, l, "attkv", t, att[:, t, 512:768])
            act.wait_ge(s("gabs", l), count("gabs", l, 1))
            softplus_of_minus_abs(act, kv.rearrange("p t a b c -> p (t a b c)"), gg.rearrange("p a b -> p (a b)")).then_inc(s("gsp", l), 1)
            act.wait_ge(s("ass_ready", l), count("ass_ready", l, 1))
            rms(act, ass[:, :, 8:10], ass[:, :, 8:10], HD)
            rms(act, ass[:, t0:, 0:8], ass[:, t0:, 0:8], HD).then_inc(s("ar_ready", l), 1)
            act_z(act, l, 0)
            for t in range(TT):
                act.wait_ge(s("b_done", l), count("b_done", l, t + 1))
                act.activation(eb[:, 0], eb[:, 0], ACT.Exp)
                act.activation(eb[:, 1], eb[:, 1], ACT.Exp, scale=-1.0).then_inc(s("eb_ready", l), 1)
                act_z(act, l, t + 1)
                act.wait_ge(s("kdt_full", l), count("kdt_full", l, t + 1))
                if t:
                    act.wait_ge(s("kv_full", l), count("kv_full", l, t))
                act.activation(kdT.rearrange("p a b -> p (a b)"), ps[:, 2, :], ACT.Copy).then_inc(s("kdt_ready", l), 1)
            act.wait_ge(s("btm_ready", l), count("btm_ready", l, 1))
            act.activation(btm[:], btm[:], ACT.Exp)
            act.activation(bme[:], bmt[:], ACT.Exp).then_inc(s("bme_ready", l), 1)
            act.wait_ge(s("sp_ready", l), count("sp_ready", l, 1))
            act_r(act, l, tiles[0])
            act_r(act, l, tiles[1])
            for q, t in enumerate(tiles):
                act.wait_ge(s("gy_full", l), count("gy_full", l, q + 1))
                act.activation(yg[:, t, :].rearrange("p (f r e) -> p r f e", f=2, r=2),
                               ps[:, 4:6, 0:256].rearrange("p r (f e) -> p r f e", f=2), ACT.Copy).then_inc(s("gy_done", l), 1)
                if q + 2 < n_t:
                    act_r(act, l, tiles[q + 2])
            act.wait_ge(s("gy_done", l), count("gy_done", l, n_t))
            act.activation(qd.rearrange("p a b c -> p (a b c)")[:, t0 * 512:], yg[:, t0:, :].rearrange("p a b -> p (a b)"), ACT.Square)\
                .then_inc(s("gsq", l), 1)
            act.wait_ge(s("yz_ready", l), count("yz_ready", l, 2 * n_t))
            for t in tiles:
                for g in range(2):
                    alink(act.activation(zs[0], ys[:, t, g * 512:(g + 1) * 512], ACT.Square,
                                         accum_out=sumsq[:, t * 2 + g:t * 2 + g + 1]))
            act.wait_ge(s("gss_ready", l), count("gss_ready", l, 1))
            rms(act, gss[:, t0:, :], gss[:, t0:, :], P)
            rms(act, sumsq[:, 2 * t0:2 * TT], rstd[:, 2 * t0:2 * TT], 512).then_inc(s("branch_rs", l), 1)
            for t in range(TT):
                act.wait_ge(s("qk_full", l), count("qk_full", l, t + 1))
                if t in tiles:
                    act.activation(qT[:, :, t * P:(t + 1) * P], view(ps[:, 2, :], 4, P), ACT.Copy)
                act.activation(kT2[:, :, t * P:(t + 1) * P], view(ps[:, 3, 0:256], 2, P), ACT.Copy)\
                    .then_inc(s("qk_turned", l), 1)
            seq = [(q, t, h) for q, t in enumerate(tiles) for h in range(8)]

            def p_exp(n, t):
                w = CTX if t < 2 else TOK
                act.wait_ge(s("nmax_ready", l), count("nmax_ready", l, n + 1))
                if n >= 2:
                    act.wait_ge(s("pt_full", l), count("pt_full", l, n - 1))
                act.activation(pb[n % 2][:, 0:w], ps[:, 4 + n % 2, 0:w], ACT.Exp, scale=0.125,
                               bias=nmax[:, n:n + 1], accum_out=rsum[:, n:n + 1]).then_inc(s("p_exp", l), 1)

            def p_rows(n, t):
                w = CTX if t < 2 else TOK
                act.wait_ge(s("pt_full", l), count("pt_full", l, n + 1))
                if n >= 2:
                    act.wait_ge(s("o_full", l), count("o_full", l, n - 1))
                act.activation(pT[n % 2].rearrange("p a b -> p (a b)")[:, 0:w], ps[:, 6 + n % 2, 0:w], ACT.Copy)\
                    .then_inc(s("pt_ready", l), 1)
            for i in range(len(seq) + 1):
                if i < len(seq):
                    p_exp(i, seq[i][1])
                if i:
                    p_rows(i - 1, seq[i - 1][1])
            act.wait_ge(s("sink_pre", l), count("sink_pre", l, 1))
            act.activation(nmax[:, 0:8 * n_t], nmax[:, 0:8 * n_t], ACT.Exp).then_inc(s("sink_exp", l), 1)
            act.wait_ge(s("o_done", l), count("o_done", l, n_t))
            for n in range(0, 4 * n_t, 2):
                _, f = y_source(tiles[n // 4], n % 4)
                t = tiles[n // 4]
                act.wait_ge(s("yt_full", l), count("yt_full", l, n + 1))
                act.activation(yT[:, f:f + 4, t * P:(t + 1) * P], view(ps[:, 2 + n % 4, :], 4, P), ACT.Copy)\
                    .then_inc(s("yt_act", l), 1)
            a, b = span_of(l)
            w = b - a
            act.wait_ge(s("neg_ready", l), count("neg_ready", l, 1))
            for j in range(3):
                for i in range(KO):
                    n = j * KO + i
                    if n >= 2:
                        act.wait_ge(freer(l, "prod", ((n - 2) // KO, (n - 2) % KO)), freed(l, "prod", ((n - 2) // KO, (n - 2) % KO)))
                    if n - 2 >= KO:
                        act.wait_ge(s("merge_acc", l), count("merge_acc", l, n - 1 - KO))
                    act.wait_ge(stream_full, filled(l, "gate", (j, i)))
                    bank = bank_of(l, "gate", (j, i))
                    act.activation(gate_e[n % 2][:, 0:w], ps[:, bank, 0:w], ACT.Sigmoid,
                                   bias=Cl("gate_b")[:, n:n + 1]).then_inc(free["act"], 1)
            for n, t in enumerate(tiles):
                act.wait_ge(s("x_tile", l), count("x_tile", l, n + 1))
                act_norm(act, l, 2, n, t)
            act.wait_ge(s("logit_full", l), count("logit_full", l, 1))
            act.activation(sc[:, t0:, :], view(ps[:, 6, t0 * NE:TT * NE], n_t, NE), ACT.Exp, scale=-1.0)\
                .then_inc(s("logit_exp", l), 1)
            act.wait_ge(s("hT2", l), count("hT2", l, n_t))
            for n in range(2 * n_t):
                t, half = tiles[n // 2], n % 2
                act.wait_ge(s("rows_full", l), count("rows_full", l, n + 1))
                act.activation(h_rows[:, t, half * 512:(half + 1) * 512], ps[:, 2 + n % 2, :], ACT.Copy)\
                    .then_inc(s("row_ready", l), 1)
            act.wait_ge(s("row_saved", l), count("row_saved", l, 16))

            def results(i):
                for half in range(2):
                    act.wait_ge(s("down_full", l), count("down_full", l, i * 2 + half + 1))
                    act.activation(ob[:, half * 512:(half + 1) * 512], ps[:, 6 + half, :], ACT.Copy)\
                        .then_inc(s("ob_done", l), 1)
                act.wait_ge(s("ob_done", l), count("ob_done", l, i * 2 + 2))
                dst = y_dram[bass.ds(i * P, P), :] if not isinstance(i, int) else y_dram[i * P:(i + 1) * P, :]
                act.dma_start(dst, ob).then_inc(s("stored", l), 16)

            def expert(i):
                for half in range(2):
                    act.wait_ge(s("up_full", l), count("up_full", l, i * 2 + half + 1))
                    act.activation(silu_h[half], ps[:, 2 + 2 * half, :], ACT.Silu).then_inc(s("silu_ready", l), 1)
                if not first(i):
                    results(i - 1)
                for half in range(2):
                    act.wait_ge(s("ht_full", l), count("ht_full", l, i * 2 + half + 1))
                    act.activation(hidT[:, half * 4:half * 4 + 4, :].rearrange("p a b -> p (a b)"),
                                   ps[:, half, :], ACT.Copy).then_inc(s("ht_ready", l), 1)
                if not first(i):
                    act.wait_ge(s("stored", l), count("stored", l, i * 16))
            expert(0)
            with act.Fori(1, NE) as i:
                expert(i)
            act.wait_ge(s("route_ready", l), count("route_ready", l, 1))
            n_extra = act.value_load(extra[0:1, 8:9], min_val=0, max_val=XTRA)
            for j in range(extra_blocks(l)):
                with act.If(n_extra > j):
                    expert(NE + j)
            results(n_extra + (NE - 1))
            act.wait_ge(s("stored", l), count("stored", l, (n_extra + NE) * 16))
            act.activation(sumsq[:, 0:1], rstd[:, 0:1], ACT.Copy).then_inc(s("all_stored", l), 1)

        def act_conv_silu(act, l, i):
            act.wait_ge(s("conv_acc", l), count("conv_acc", l, i + 1))
            a, b = span_of(l) if for_outputs("xbc", i) else (0, TOK)
            acc = (xsT[:, i % 2, :] if i < 8 else bcT[:, i - 8, :])[:, a:b]
            act.activation(acc, acc, ACT.Silu).then_inc(s("conv_done", l), 1)

        def act_conv_rows(act, l, i):
            act.wait_ge(s("ct_full", l), count("ct_full", l, i + 1))
            dst = xs[:, :, i * P:(i + 1) * P] if i < 8 else b_tm[:, :, (i - 8) * P:(i - 7) * P]
            act.activation(dst, view(ps[:, 2 + i % 2, :], TT, P), ACT.Copy).then_inc(s("ct_done", l), 1)

        def dve_scale_rows(dve, l, which, n, t):
            dve.wait_ge(s(f"rs{which}", l), count(f"rs{which}", l, n + 1))
            dve.tensor_scalar(xn[:, t, :], xb[:, t, :], rstd[:, t:t + 1], None, ALU.mult).then_inc(s(f"xn{which}", l), 1)

        def dve_modulate(dve, l, which, n, t):
            c = 0 if t < 2 else 1
            dve.wait_ge(s(f"tr{which}", l), count(f"tr{which}", l, n + 1))
            for k in range(KO):
                ins = dve.tensor_scalar(hT[:, k, t * P:(t + 1) * P],
                                        ps[:, 2 + 2 * (n % 2) + k // 4, (k % 4) * P:(k % 4 + 1) * P],
                                        scale_a[:, which - 1, k, c:c + 1], modc[:, 2 * (which - 1), k, c:c + 1],
                                        ALU.mult, ALU.add)
            ins.then_inc(s(f"hT{which}", l), 1)

        def bc(ap, n):
            return ap.unsqueeze(len(ap.shape)).to_broadcast([*ap.shape, n])

        def bc_mid(ap, n):
            return ap.unsqueeze(len(ap.shape) - 1).to_broadcast([*ap.shape[:-1], n, ap.shape[-1]])

        def dve_conv_acc(dve, link, l, i):
            dve.wait_ge(freer(l, "xbc", i), freed(l, "xbc", i))
            if 2 <= i < 8:
                dve.wait_ge(s("ct_full", l), count("ct_full", l, i - 1))
            first_seq = span_of(l)[0] // CTX if for_outputs("xbc", i) else 0
            acc = view(xsT[:, i % 2, :] if i < 8 else bcT[:, i - 8, :], 2, CTX)[:, first_seq:]
            src = view(raw[:, i % 3, :], 2, CTX)[:, first_seq:]
            w = view(Cl("conv_w"), 12, 5)
            link(dve.tensor_scalar(acc, src, w[:, i, 2:3], Cl("conv_b")[:, i:i + 1], ALU.mult, ALU.add))
            for tap in (0, 1, 3, 4):
                o_ = tap - 2
                a0, a1 = max(0, -o_), 256 - max(0, o_)
                ins = dve.scalar_tensor_tensor(out=acc[:, :, a0:a1], in0=src[:, :, a0 + o_:a1 + o_], scalar=w[:, i, tap:tap + 1],
                                               in1=acc[:, :, a0:a1], op0=ALU.mult, op1=ALU.add)
                if tap < 4:
                    link(ins)
            ins.then_inc(s("conv_acc", l), 1)

        def dve_ssd(dve, link, l):
            tiles = tiles_of(l)
            for t in range(TT):
                dve.wait_ge(stream_full, filled(l, "dt", t))
                bank = bank_of(l, "dt", t)
                dve.tensor_tensor(dt_raw[:, t, :], ps[:, bank, 0:32], Rw("dt_bias"), ALU.add).then_inc(free["dve"], 1)
            dve.wait_ge(freer(l, "dt", TT - 1), freed(l, "dt", TT - 1))
            dve.tensor_copy(rstd[:, 15:16], dt_raw[:, 0, 0:1]).then_inc(s("sp1", l), 1)
            dve.wait_ge(s("sp2", l), count("sp2", l, 1))
            link(dve.scalar_tensor_tensor(out=dt[:], in0=dt_raw[:], scalar=0.0, in1=dt[:], op0=ALU.max, op1=ALU.add))
            dve.scalar_tensor_tensor(out=da[:], in0=dt[:], scalar=-1.0, in1=bc_mid(neg_a[:], TT),
                                     op0=ALU.mult, op1=ALU.mult).then_inc(s("da_ready", l), 1)
            dve.wait_ge(s("cum_full", l), count("cum_full", l, 1))
            dve.tensor_copy(cums[:], view(ps[:, 4, 0:256], TT, 64)).then_inc(s("cum_ready", l), 1)
            dve.wait_ge(s("cum_ready", l), count("cum_ready", l, 1))
            dve.tensor_tensor(wd[:], cums[:, :, 32:64], cums[:, :, 0:32], ALU.subtract).then_inc(s("wd_pre", l), 1)
            dve.wait_ge(s("ecs_ready", l), count("ecs_ready", l, 1))
            dve.tensor_tensor(wd[:], wd[:], dt[:], ALU.mult).then_inc(s("w_ready", l), 1)

            def diff(q, t, k):
                kq = q * 8 + k
                h = (k // 4) * 16 + (k % 4) * 4
                d3 = view(dd[kq % 3], 4, P)
                if kq >= 3:
                    dve.wait_ge(s("m_ready", l), count("m_ready", l, kq - 2))
                dve.wait_ge(s("bc_full", l), count("bc_full", l, kq + 1))
                dve.tensor_tensor(d3, view(ps[:, SPREAD[kq % 3], :], 4, P), bc(cums[:, t, h:h + 4], P),
                                  ALU.subtract).then_inc(s("diff_done", l), 1)
                dve.wait_ge(s("diff_done", l), count("diff_done", l, kq + 1))
                dve.tensor_scalar(dd[kq % 3], dd[kq % 3], 0.0, None, ALU.min).then_inc(s("dm_ready", l), 1)

            def decay(q, t, k):
                kq = q * 8 + k
                dve.wait_ge(s("e_ready", l), count("e_ready", l, kq + 1))
                if kq >= 2:
                    dve.wait_ge(s("ymm_done", l), count("ymm_done", l, kq - 1))
                dve.tensor_tensor(view(mm[kq % 2], 4, P), view(dd[kq % 3], 4, P),
                                  bc_mid(cbm[:, k // 4, (k % 4) // 2, :], 4), ALU.mult).then_inc(s("m_ready", l), 1)
            def evacuate(q, t):
                dve.wait_ge(s("ymm_done", l), count("ymm_done", l, 8 * (q + 1)))
                dve.wait_ge(s("pool_x", l), count("pool_x", l, 3 * (q + 1)))
                for g in range(2):
                    part = ys[:, t, g * 512:(g + 1) * 512]
                    ins = dve.tensor_tensor(part, ps[:, 5 + g, :], part, ALU.add)
                ins.then_inc(s("y_evac", l), 1)
            dve.wait_ge(s("mod_saved", l), count("mod_saved", l, 64))
            if l == 0:
                dve.wait_ge(s("y_zero", 0), count("y_zero", 0, 16 * XTRA))
            for q, t in enumerate(tiles):
                dve.wait_ge(s("cb_full", l), count("cb_full", l, q + 1))
                cb = view(ps[:, 2, 0:256], 2, P)
                if q:
                    dve.wait_ge(s("m_ready", l), count("m_ready", l, 8 * q))
                dve.tensor_tensor(cbm[:, 0], cb, bc_mid(upper, 2), ALU.mult)
                dve.tensor_tensor(cbm[:, 1], cb, bc_mid(lower, 2), ALU.mult).then_inc(s("cbm_ready", l), 1)
                dve.wait_ge(s("cbm_ready", l), count("cbm_ready", l, q + 1))
                for k in range(8):
                    diff(q, t, k)
                    if k:
                        decay(q, t, k - 1)
                    elif q:
                        evacuate(q - 1, tiles[q - 1])
                decay(q, t, 7)
            evacuate(len(tiles) - 1, tiles[-1])
            dve.wait_ge(s("y_evac", l), count("y_evac", l, len(tiles)))
            n_inter = 0
            for k in range(4):
                for d in range(2):
                    b = ORDER[d][k]
                    if k and b in tiles:
                        n_inter += 1
                        dve.wait_ge(s("inter_full", l), count("inter_full", l, n_inter))
                        for g in range(2):
                            ins = dve.tensor_tensor(view(dd[g], 8, SP), view(ps[:, 2 + g, :], 8, SP),
                                                    bc(ecs[:, b, d * 16 + g * 8:d * 16 + g * 8 + 8], SP), ALU.mult)
                        ins.then_inc(s("inter_done", l), 1)
                        dve.wait_ge(s("inter_done", l), count("inter_done", l, n_inter))
                        for g in range(2):
                            part = ys[:, b, g * 512:(g + 1) * 512]
                            ins = dve.tensor_tensor(part, part, dd[g], ALU.add)
                        link(ins)
                    if k < 3:
                        dve.wait_ge(s("upd_full", l), count("upd_full", l, 2 * k + d + 1))
                        if k:
                            st = view(state[:, d, :], SH, SP)
                            link(dve.tensor_tensor(st, st, bc(ecs[:, b, 32 + d * 16:48 + d * 16], SP), ALU.mult))
                        for g in range(2):
                            part = state[:, d, g * 512:(g + 1) * 512]
                            if k:
                                ins = dve.tensor_tensor(part, ps[:, 5 + g, :], part, ALU.add)
                            else:
                                ins = dve.tensor_copy(part, ps[:, 5 + g, :])
                        ins.then_inc(s("s_ready", l), 1)
                        dve.wait_ge(s("s_ready", l), count("s_ready", l, 2 * k + d + 1))

        def heads(l, t):
            lo = 0 if t in tiles_of(l) else 8
            return lo, 10 - lo

        def dve_z(dve, l, step):
            for n, index in z_groups(l, step):
                dve.wait_ge(freer(l, "z", index), freed(l, "z", index))
                b, t = index
                part = ys[:, t, b * 512:(b + 1) * 512]
                dve.tensor_tensor(part, part, zs[n % 2], ALU.mult).then_inc(s("yz_ready", l), 1)

        def dve_gla(dve, link, l):
            tiles = tiles_of(l)
            dve.wait_ge(s("lg_full", l), count("lg_full", l, 1))
            for t in range(TT):
                ins = dve.tensor_tensor(gg[:, t, :], ps[:, 2 + t, :], Rw("gla_b2"), ALU.add)
            ins.then_inc(s("gabs", l), 1)
            dve.wait_ge(freer(l, "attkv", TT - 1), freed(l, "attkv", TT - 1))
            for t in range(TT):
                lo, n = heads(l, t)
                x3 = view(att[:, t, lo * 64:640], n, 64)
                r3 = view(rt[:, 0:n * 64], n, 64)
                link(dve.tensor_tensor(r3, x3, x3, ALU.mult))
                ins = dve.tensor_reduce(ass[:, t, lo:10], r3, AX.X, ALU.add)
                if t < TT - 1:
                    link(ins)
            ins.then_inc(s("ass_ready", l), 1)
            flat = gg.rearrange("p a b -> p (a b)")
            kvf = kv.rearrange("p t a b c -> p (t a b c)")
            dve.wait_ge(s("gsp", l), count("gsp", l, 1))
            link(dve.scalar_tensor_tensor(out=flat, in0=flat, scalar=0.0, in1=kvf, op0=ALU.min, op1=ALU.subtract))
            dve.tensor_scalar(flat, flat, 1.0 / 16.0, None, ALU.mult).then_inc(s("g_ready", l), 1)
            dve.wait_ge(s("upd_full", l), count("upd_full", l, 6))
            dve_z(dve, l, 0)
            dve.wait_ge(s("ar_ready", l), count("ar_ready", l, 1))
            for t in range(TT):
                dve.wait_ge(s("b_full", l), count("b_full", l, t + 1))
                b4 = ps[:, 6 + t % 2, :].rearrange("p (d f n) -> p d f n", d=2, f=2)
                for d in range(2):
                    mid, end = (P // 2 - 1, P - 1) if d == 0 else (P // 2, 0)
                    dve.tensor_copy(bmt[:, t, d, :, 0:1], b4[:, d, :, mid:mid + 1])
                    ins = dve.tensor_copy(bmt[:, t, d, :, 1:2], b4[:, d, :, end:end + 1])
                link(ins)
                if t:
                    dve.wait_ge(s("qkd_ready", l), count("qkd_ready", l, t))
                for d in range(2):
                    for f in range(2):
                        m = bmt[:, t, d, f, 0:1]
                        dve.tensor_scalar(eb[:, 0, d, f, :], b4[:, d, f, :], m, CLAMP, ALU.subtract, ALU.min)
                        ins = dve.tensor_scalar(eb[:, 1, d, f, :], b4[:, d, f, :], m, -CLAMP, ALU.subtract, ALU.max)
                ins.then_inc(s("b_done", l), 1)
                dve.wait_ge(s("eb_ready", l), count("eb_ready", l, t + 1))
                for d in range(2):
                    if t in tiles:
                        dve.tensor_tensor(qd[:, t * 2 + d], eb[:, 0, d], qkT[:, 0:2, t * P:(t + 1) * P], ALU.mult)
                    ins = dve.tensor_tensor(kd[:, t * 2 + d], eb[:, 1, d], qkT[:, 2:4, t * P:(t + 1) * P], ALU.mult)
                ins.then_inc(s("qkd_ready", l), 1)
                if t < TT - 1:
                    dve_z(dve, l, t + 1)
                dve.wait_ge(s("kv_full", l), count("kv_full", l, t + 1))
                for d in range(2):
                    src = ps[:, 3 + d, :].rearrange("p (f e) -> p f e", f=2)
                    dve.tensor_copy(kv[0:64, t, d, :, :], src[0:64, :, 0:P])
                    ins = dve.tensor_copy(kv[64:128, t, d, :, :], src[64:128, :, P:2 * P])
                ins.then_inc(s("kv_done", l), 1)
                lo, n = heads(l, t)
                x3 = view(att[:, t, lo * 64:640], n, 64)
                link(dve.tensor_tensor(x3, x3, bc(ass[:, t, lo:10], 64), ALU.mult))
                if lo == 0:
                    x8 = view(att[:, t, 0:512], 8, 64)
                    dve.tensor_tensor(x8, x8, bc_mid(Rw("q_norm"), 8), ALU.mult)
                k2 = view(att[:, t, 512:640], 2, 64)
                link(dve.tensor_tensor(k2, k2, bc_mid(Rw("k_norm"), 2), ALU.mult))
            dve.tensor_tensor(btm[:], bmt[:, :, :, :, 1], bmt[:, :, :, :, 0], ALU.subtract).then_inc(s("btm_ready", l), 1)
            dve.wait_ge(s("bme_ready", l), count("bme_ready", l, 1))
            dve.wait_ge(s("kv_done", l), count("kv_done", l, TT))
            for d in range(2):
                S_ = gs[:, 2 * d:2 * d + 2, :]
                for k in range(4):
                    t = ORDER[d][k]
                    if k:
                        link(dve.tensor_tensor(sp[:, t * 2 + d], S_, bc(bme[:, t, d, :, 0], P), ALU.mult))
                    if k < 3:
                        link(dve.tensor_tensor(kv[:, t, d], kv[:, t, d], bc(btm[:, t, d, :], P), ALU.mult))
                        if k:
                            link(dve.tensor_tensor(S_, S_, bc(bme[:, t, d, :, 1], P), ALU.mult))
                            link(dve.tensor_tensor(S_, S_, kv[:, t, d], ALU.add))
                        else:
                            link(dve.tensor_copy(S_, kv[:, t, d]))
            dve.tensor_copy(gs[:, 0, 0:1], gs[:, 0, 0:1]).then_inc(s("sp_ready", l), 1)
            for q, t in enumerate(tiles):
                dve.wait_ge(s("sc_full", l), count("sc_full", l, q + 1))
                if q:
                    dve.wait_ge(s("gy_full", l), count("gy_full", l, q))
                for d in range(2):
                    bank = (2, 6)[q % 2]
                    for odd in range(2):
                        ins = dve.tensor_tensor(pm[d][:, odd::2, :],
                                                view(ps[:, bank + odd, d * 256:(d + 1) * 256], 2, P),
                                                bc_mid(tri[d], 2), ALU.mult)
                    ins.then_inc(s("p_ready", l), 1)

        def dve_att(dve, link, l):
            tiles = tiles_of(l)
            dve.wait_ge(s("gy_full", l), count("gy_full", l, len(tiles)))
            dve.wait_ge(freer(l, "attkv", TT - 1), freed(l, "attkv", TT - 1))

            dve.wait_ge(s("gsq", l), count("gsq", l, 1))
            t0, n_t = tiles[0], len(tiles)
            dve.tensor_reduce(gss[:, t0:, :], view(qd.rearrange("p a b c -> p (a b c)")[:, t0 * 512:], n_t, 4, P), AX.X, ALU.add)\
                .then_inc(s("gss_ready", l), 1)
            for t in range(TT):
                lo, n = heads(l, t)
                x3 = view(att[:, t, lo * 64:640], n, 64)
                k2 = view(att[:, t, 512:640], 2, 64)
                if t >= 2:
                    cos = view(K("cos"), 2, 64)[:, t - 2, :]
                    sin = view(K("sin"), 2, 2, 2, 16)[:, t - 2]
                    r3 = view(rt[:, 0:n * 64], n, 64)
                    link(dve.tensor_tensor(r3, x3, bc_mid(cos, n), ALU.mult))
                    x5 = att[:, t, lo * 64:640].rearrange("p (h a c e) -> p h a c e", a=2, c=2, e=16)
                    u5 = ru[:, 0:n * 64].rearrange("p (h a c e) -> p h a c e", a=2, c=2, e=16)
                    for c in range(2):
                        sn = sin[:, :, c, :].unsqueeze(1).to_broadcast([P, n, 2, 16])
                        link(dve.tensor_tensor(u5[:, :, :, c, :], x5[:, :, :, 1 - c, :], sn, ALU.mult))
                    link(dve.tensor_tensor(x3, r3, view(ru[:, 0:n * 64], n, 64), ALU.add))
                dve.tensor_copy(kdup[:, t, :, 0, :], k2)
                dve.tensor_copy(kdup[:, t, :, 1, :], k2).then_inc(s("att_prep", l), 1)
            seq = [(q, t, h) for q, t in enumerate(tiles) for h in range(8)]

            def collect(q, t):
                dve.wait_ge(s("o_full", l), count("o_full", l, q * 8 + 8))
                dve.tensor_copy(att[:, t, 0:512], ps[:, 2 + q % 2, :]).then_inc(s("o_raw", l), 1)
            for n, (q, t, h) in enumerate(seq):
                w = CTX if t < 2 else TOK
                dve.wait_ge(s("s_full", l), count("s_full", l, n + 1))
                link(dve.tensor_reduce(nmax[:, n:n + 1], ps[:, 4 + n % 2, 0:w], AX.X, ALU.max))
                dve.tensor_scalar(nmax[:, n:n + 1], nmax[:, n:n + 1], -0.125, neg_sink[:, h:h + 1],
                                  ALU.mult, ALU.min).then_inc(s("nmax_ready", l), 1)
                if h == 4 and q:
                    collect(q - 1, tiles[q - 1])
            collect(len(tiles) - 1, tiles[-1])
            n_t = len(tiles)
            dve.wait_ge(s("p_exp", l), count("p_exp", l, 8 * n_t))
            v = view(nmax[:, 0:8 * n_t], n_t, 8)
            dve.tensor_tensor(v, v, bc_mid(Rw("sink"), n_t), ALU.add).then_inc(s("sink_pre", l), 1)
            dve.wait_ge(s("sink_exp", l), count("sink_exp", l, 1))
            rs = rsum[:, 0:8 * n_t]
            link(dve.tensor_tensor(rs, rs, nmax[:, 0:8 * n_t], ALU.add))
            link(dve.reciprocal(rs, rs))
            dve.wait_ge(s("o_raw", l), count("o_raw", l, n_t))
            for q, t in enumerate(tiles):
                o8 = view(att[:, t, 0:512], 8, 64)
                dve.tensor_tensor(o8, o8, bc(rs[:, q * 8:q * 8 + 8], 64), ALU.mult).then_inc(s("o_done", l), 1)

        def dve_merge(dve, link, l):
            tiles = tiles_of(l)
            for n in range(1, 4 * len(tiles), 2):
                _, f = y_source(tiles[n // 4], n % 4)
                t = tiles[n // 4]
                dve.wait_ge(s("yt_full", l), count("yt_full", l, n + 1))
                dve.tensor_copy(yT[:, f:f + 4, t * P:(t + 1) * P], view(ps[:, 2 + n % 4, :], 4, P))\
                    .then_inc(s("yt_dve", l), 1)
            a, b = span_of(l)
            w = b - a
            for j in range(3):
                for i in range(KO):
                    e = gate_e[(j * KO + i) % 2][:, 0:w]
                    dve.wait_ge(freer(l, "gate", (j, i)), freed(l, "gate", (j, i)))
                    dve.wait_ge(stream_full, filled(l, "prod", (j, i)))
                    bank = bank_of(l, "prod", (j, i))
                    dst = merged[:, i, a:b]
                    dve.tensor_tensor(dst if j == 0 else e, ps[:, bank, 0:w], e, ALU.mult).then_inc(free["dve"], 1)
                    dve.wait_ge(freer(l, "prod", (j, i)), freed(l, "prod", (j, i)))
                    if j:
                        dve.tensor_tensor(dst, dst, e, ALU.add).then_inc(s("merge_acc", l), 1)
                        dve.wait_ge(s("merge_acc", l), count("merge_acc", l, (j - 1) * KO + i + 1))
                    if l < NL - 1 and i % 4 == 3:
                        for c in early_mods(2 * j + i // 4):
                            keep_mod(dve, l + 1, c)
            dve.tensor_copy(gate_e[0][:, 0:1], merged[:, 0, a:a + 1]).then_inc(s("merged", l), 1)
            dve.wait_ge(s("merged", l), count("merged", l, 1))
            dve.wait_ge(s("x_again", l), count("x_again", l, 16 * (len(tiles) + 2)))
            for n, t in enumerate(tiles):
                c = 0 if t < 2 else 1
                for half in range(2):
                    e = gate_e[half]
                    dve.wait_ge(stream_full, filled(l, "out", (half, t)))
                    bank = bank_of(l, "out", (half, t))
                    cols_ = slice(half * 512, (half + 1) * 512)
                    dve.tensor_tensor(e, ps[:, bank, :], gate_bc[:, c, cols_], ALU.mult).then_inc(free["dve"], 1)
                    dve.wait_ge(freer(l, "out", (half, t)), freed(l, "out", (half, t)))
                    ins = dve.tensor_tensor(xb[:, t, cols_], xb[:, t, cols_], e, ALU.add)
                ins.then_inc(s("x_tile", l), 1)
                dve_scale_rows(dve, l, 2, n, t)
                if n:
                    dve_modulate(dve, l, 2, n - 1, tiles[n - 1])
            dve_modulate(dve, l, 2, len(tiles) - 1, tiles[-1])

        def keep_mod(dve, l, c):
            dve.wait_ge(stream_full, filled(l, "mod", c))
            dve.wait_ge(s("bias_in", l), count("bias_in", l, 64))
            for q in QUARTERS:
                part = mod_rows[l][q, c, :]
                ins = dve.tensor_tensor(part, ps[q, bank_of(l, "mod", c), 0:P], part, ALU.add)
            ins.then_inc(free["dve"], 1)

        def dve_mod_columns(dve, link, l):
            dve.wait_ge(s("cols_in", l), count("cols_in", l, 16))
            dve.wait_ge(s("modT_full", l), count("modT_full", l, 1))
            for j in range(4):
                ins = dve.tensor_copy(modc[:].rearrange("p v (h j) c -> p v h j c", j=4)[:, :, :, j, :],
                                      ps[:, MOD_BANKS[j], 0:16].rearrange("p (v h c) -> p v h c", v=4, h=2))
            link(ins)
            for m in range(2):
                ins = dve.scalar_tensor_tensor(out=scale_a[:, m], in0=modc[:, 2 * m + 1], scalar=1.0,
                                               in1=bc(Cl("norm1" if m == 0 else "norm2"), 2), op0=ALU.add, op1=ALU.mult)
            ins.then_inc(s("modc_ready", l), 1)
            dve.wait_ge(s("modc_ready", l), count("modc_ready", l, 1))

        def dve_route(dve, link, l):
            tiles = tiles_of(l)
            t0, n_t = tiles[0], len(tiles)

            def quads(ap):
                return ap[:, t0:, :].rearrange("p t (g j) -> p (t g) j", j=4)

            def flat(ap):
                return ap[:, t0:, :].rearrange("p t g -> p (t g)")

            def first_of(dst, src, top, tmp, idx):
                r4 = K("rank4").unsqueeze(1).to_broadcast([P, src.shape[1], 4])
                link(dve.tensor_tensor(tmp, src, bc(top, 4), ALU.is_equal))
                link(dve.tensor_tensor(tmp, tmp, r4, ALU.mult))
                link(dve.tensor_reduce(idx, tmp, AX.X, ALU.max))
                link(dve.tensor_tensor(dst, tmp, bc(idx, 4), ALU.is_equal))
            dve.wait_ge(s("logit_exp", l), count("logit_exp", l, 1))
            sc_ = sc[:, t0:, :]
            link(dve.tensor_scalar(sc_, sc_, 1.0, None, ALU.add))
            link(dve.reciprocal(sc_, sc_))
            link(dve.tensor_tensor(bi[:, t0:, :], sc_, bc_mid(Rw("router_b"), n_t), ALU.add))
            q, tmp = quads(bi), quads(over)
            idx = off[:, 0:n_t * 4]
            link(dve.tensor_reduce(flat(m1), q, AX.X, ALU.max))
            first_of(quads(oh[0]), q, flat(m1), tmp, idx)
            link(dve.scalar_tensor_tensor(out=q, in0=quads(oh[0]), scalar=-BIG, in1=q, op0=ALU.mult, op1=ALU.add))
            link(dve.tensor_reduce(flat(m2), q, AX.X, ALU.max))
            first_of(quads(oh[1]), q, flat(m2), tmp, idx)
            link(dve.tensor_tensor(flat(gsc), flat(m1), flat(m2), ALU.add))
            link(dve.tensor_reduce(gmax[:, t0:], gsc[:, t0:, :], AX.X, ALU.max))
            first_of(gsel[:, t0:, :], gsc[:, t0:, :], gmax[:, t0:], rank[:, t0:, 0:4], cnt[:, 0:n_t])
            for c in range(2):
                link(dve.tensor_tensor(quads(oh[c]), quads(oh[c]), bc(flat(gsel), 4), ALU.mult))
            dve.tensor_tensor(t16[:, t0:, :], oh[0][:, t0:, :], oh[1][:, t0:, :], ALU.add).then_inc(s("assigned", l), 1)
            for c in range(2):
                link(dve.tensor_tensor(over[:, t0:, :], oh[c][:, t0:, :], sc_, ALU.mult))
                link(dve.tensor_reduce(gates[:, c, t0:], over[:, t0:, :], AX.X, ALU.add))
            link(dve.tensor_tensor(gmax[:, t0:], gates[:, 0, t0:], gates[:, 1, t0:], ALU.add))
            link(dve.reciprocal(gmax[:, t0:], gmax[:, t0:]))
            for c in range(2):
                link(dve.tensor_tensor(gates[:, c, t0:], gates[:, c, t0:], gmax[:, t0:], ALU.mult))
            dve.wait_ge(s("rank_full", l), count("rank_full", l, 1))
            dve.tensor_copy(cnt[:], ps[:, 6, 64:64 + NE])
            link(dve.tensor_copy(rank[:, t0:, :], view(ps[:, 6, t0 * NE:TT * NE], n_t, NE)))
            link(dve.tensor_scalar(xtr[:], cnt[:], float(P), None, ALU.is_gt))
            for m in range(2, TOK // P):
                link(dve.tensor_scalar(incl[:], cnt[:], float(P * m), None, ALU.is_gt))
                link(dve.tensor_tensor(xtr[:], xtr[:], incl[:], ALU.add))
            link(dve.tensor_copy(incl[:], xtr[:]))
            a, b = incl, scan_t
            for sh in (1, 2, 4, 8):
                dve.tensor_copy(b[:, 0:sh], a[:, 0:sh])
                link(dve.tensor_tensor(b[:, sh:NE], a[:, sh:NE], a[:, 0:NE - sh], ALU.add))
                a, b = b, a
            link(dve.tensor_tensor(off[:], a[:], xtr[:], ALU.subtract))
            link(dve.tensor_scalar(off[:], off[:], float(P), float(NE * P - P), ALU.mult, ALU.add))
            link(dve.tensor_tensor(off[:], off[:], K("first_slot"), ALU.subtract))
            link(dve.tensor_scalar(over[:, t0:, :], rank[:, t0:, :], float(P), None, ALU.is_ge))
            link(dve.tensor_tensor(over[:, t0:, :], over[:, t0:, :], bc_mid(off[:], n_t), ALU.mult))
            link(dve.tensor_tensor(rank[:, t0:, :], rank[:, t0:, :], over[:, t0:, :], ALU.add))
            link(dve.tensor_tensor(rank[:, t0:, :], rank[:, t0:, :], bc_mid(K("first_slot"), n_t), ALU.add))
            for c in range(2):
                link(dve.tensor_tensor(over[:, t0:, :], oh[c][:, t0:, :], rank[:, t0:, :], ALU.mult))
                link(dve.tensor_reduce(slotf[:, c, t0:], over[:, t0:, :], AX.X, ALU.add))
                link(dve.tensor_copy(slot_idx[:, c * TT + t0:(c + 1) * TT], slotf[:, c, t0:]))
            link(dve.tensor_tensor(blk[:], a[:].unsqueeze(1).to_broadcast([P, 8, NE]), bc(K("block"), NE), ALU.is_le))
            link(dve.tensor_reduce(blkf[:], blk[:], AX.X, ALU.add))
            link(dve.tensor_scalar(blkf[:], blkf[:], float(NE - 1), None, ALU.min))
            dve.tensor_copy(extra[:, 0:8], blkf[:])
            dve.tensor_copy(extra[:, 8:9], a[:, NE - 1:NE]).then_inc(s("route_ready", l), 1)
            if l < NL - 1:
                for c in range(EARLY, 12):
                    keep_mod(dve, l + 1, c)
                dve_mod_columns(dve, link, l + 1)

        def dve_experts(dve, link, l):
            def take_x(i):
                dve.wait_ge(s("xt_full", l), count("xt_full", l, i + 1))
                dve.tensor_copy(hflat[:, 1024:1536], ps[:, 0, :])
                dve.tensor_copy(hflat[:, 1536:2048], ps[:, 1, :]).then_inc(s("xt_ready", l), 1)

            def hidden(i, half):
                dve.wait_ge(s("silu_ready", l), count("silu_ready", l, i * 2 + half + 1))
                if not first(i):
                    dve.wait_ge(s("ht_full", l), count("ht_full", l, i * 2))
                dve.tensor_tensor(hid[:, half * 512:(half + 1) * 512], ps[:, 3 + 2 * half, :], silu_h[half], ALU.mult)\
                    .then_inc(s("hid_ready", l), 1)

            def block(i):
                hidden(i, 0)
                hidden(i, 1)
                take_x(i + 1)
            dve.wait_ge(s("rows_full", l), count("rows_full", l, 2 * len(tiles_of(l))))
            take_x(0)
            block(0)
            with dve.Fori(1, NE) as i:
                block(i)
            n_extra = dve.value_load(extra[0:1, 8:9], min_val=0, max_val=XTRA)
            for j in range(extra_blocks(l)):
                with dve.If(n_extra > j):
                    block(NE + j)

        def dve_combine(dve, link, l, t):
            tiles = tiles_of(l)
            half = len(tiles) // 2
            if t == tiles[0]:
                dve.wait_ge(s("rest_in", l), count("rest_in", l, 48))
                dve.wait_ge(s("y_first", l), count("y_first", l, 32 * half))
            if t == tiles[half]:
                dve.wait_ge(s("y_rest", l), count("y_rest", l, 32 * half))
            c = 0 if t < 2 else 1
            y0, y1 = yr[:, t, 0, :], yr[:, t, 1, :]
            link(dve.tensor_scalar(y0, y0, gates[:, 0, t:t + 1], None, ALU.mult))
            link(dve.scalar_tensor_tensor(out=y0, in0=y1, scalar=gates[:, 1, t:t + 1], in1=y0, op0=ALU.mult, op1=ALU.add))
            link(dve.tensor_tensor(y0, y0, gate_bc[:, c, :], ALU.mult))
            ins = dve.tensor_tensor(xb[:, t, :], xb[:, t, :], y0, ALU.add)
            ins.then_inc(s("x_final", l), 1)

        def dve_layer(dve, link, l):
            tiles = tiles_of(l)
            if l == 0:
                dve.wait_ge(const_in, 16)
                for c in range(12):
                    keep_mod(dve, l, c)
                dve_mod_columns(dve, link, l)
            for t in range(TT):
                if l:
                    dve_combine(dve, link, l - 1, t)
                if t:
                    dve_scale_rows(dve, l, 1, t - 1, t - 1)
            dve_scale_rows(dve, l, 1, TT - 1, TT - 1)
            dve.wait_ge(s("small_in", l), count("small_in", l, 48))
            dve.tensor_scalar(neg_sink[:], Rw("sink"), -1.0, None, ALU.mult).then_inc(s("neg_ready", l), 1)
            for t in range(TT):
                dve_modulate(dve, l, 1, t, t)
            for i in range(12):
                dve_conv_acc(dve, link, l, i)
            dve_ssd(dve, link, l)
            dve_gla(dve, link, l)
            dve_att(dve, link, l)
            dve_merge(dve, link, l)
            dve_route(dve, link, l)
            dve_experts(dve, link, l)
            if l == NL - 1:
                for t in tiles:
                    dve_combine(dve, link, l, t)

        block = ctx.enter_context(nc.Block())

        @block.sync
        def _(sp):
            sp.dma_start(cond[:], I["cond"]).then_inc(cond_in, 16)
            for l in range(NL):
                sp_stream(sp, l, RING if l else 0, None)
                sp_experts(sp, l)
                sp_rest(sp, l)
            for n in range(2):
                sp.wait_ge(s("x_final", NL - 1), count("x_final", NL - 1, n + 1))
                sp.dma_start(out[0, n * P:(n + 1) * P, :], xb[:, 2 + n, :]).then_inc(s("out_saved", 0), 16)
            sp.wait_ge(s("out_saved", 0), count("out_saved", 0, 32))

        @block.gpsimd
        def _(pool):
            link = Chain(pool, "pool")
            for l in range(NL):
                pool_layer(pool, link, l)

        @block.tensor
        def _(pe):
            for l in range(NL):
                pe_layer(pe, l)

        @block.scalar
        def _(act):
            nonlocal alink
            alink = Chain(act, "act")
            for l in range(NL):
                act_layer(act, l)

        @block.vector
        def _(dve):
            link = Chain(dve, "dve")
            for l in range(NL):
                dve_layer(dve, link, l)


def pack(inputs):
    a = {k: np.ascontiguousarray(v) for k, v in inputs.items()}
    got = {k: a[k] for k in ("x", "ctx", "w_mod", "b_mod", "w_in", "gla_w2", "w_br_a", "w_br_b", "w_br_c", "w_out",
                             "router_w", "w1", "w3", "w2")}
    got["consts"] = const_pack()
    c = np.stack([a["c_ctx"], a["c"][0]])
    got["cond"] = c.reshape(2, KO, P).transpose(2, 1, 0)
    rows = [a["q_norm_g"], a["k_norm_g"], a["gla_norm_g"], a["ssd_norm_g"], a["ssd_dt_bias"].reshape(NL, 32),
            a["ssd_a_log"].reshape(NL, 32), a["ssd_d"], a["att_sink"], a["gla_b2"].reshape(NL, 512),
            np.tile(a["router_b"], (NL, 1))]
    got["rows"] = np.concatenate(rows, 1)
    conv_w = a["ssd_conv_w"].reshape(NL, 5, 12, P).transpose(0, 3, 2, 1).reshape(NL, P, 60)
    cols = [a["norm1_g"].reshape(NL, 8, P).transpose(0, 2, 1), a["norm2_g"].reshape(NL, 8, P).transpose(0, 2, 1), conv_w,
            a["ssd_conv_b"].reshape(NL, 12, P).transpose(0, 2, 1), a["gate_b"].reshape(NL, 24, P).transpose(0, 2, 1)]
    got["cols"] = np.concatenate(cols, 2)
    return {k: np.ascontiguousarray(v) for k, v in got.items()}


def kernel(**inputs):
    import concourse.bacc as _bacc
    from concourse.bass_utils import run_bass_kernel_spmd as _run

    nc = _bacc.Bacc("TRN2", target_bir_lowering=False, num_devices=1)
    arrays, I = {}, {}
    for name, a in pack(inputs).items():
        arrays[f"in_{name}"] = a
        I[name] = nc.dram_tensor(f"in_{name}", a.shape, mybir.dt.from_np(a.dtype), kind="ExternalInput").ap()
    out = nc.dram_tensor("out_x", (1, LAT, D), F32, kind="ExternalOutput").ap()
    build(nc, I, out)
    r = _run(nc, [arrays], core_ids=[0])
    return r.results[0]["out_x"]
```
